# Optimizing a Trainium2 kernel written in Bass

```python
import jax
import jax.numpy as jnp
from jax import lax
import numpy as np

D_MODEL = 1024
BATCH = 1
SEQ = 256
DEPTH = 2

GRID_W = 64
CTX_LEN = 256
EPS = 1e-6
NEG_INF = -1e30

HEAD_DIM = 64
A_Q_HEADS = 8
A_KV_HEADS = 2
A_GROUP = A_Q_HEADS // A_KV_HEADS
B_Q_HEADS = 8
B_KV_HEADS = 2
B_GROUP = B_Q_HEADS // B_KV_HEADS
WINDOW = 128
Q_BLOCK = 128
BAND_SPAN = Q_BLOCK + 2 * WINDOW
ROPE_THETA = 10000.0
ROPE_PAIRS = HEAD_DIM // 4
A_QD = A_Q_HEADS * HEAD_DIM
A_KVD = A_KV_HEADS * HEAD_DIM
B_QD = B_Q_HEADS * HEAD_DIM
B_KVD = B_KV_HEADS * HEAD_DIM
ATTN_SPLITS = (A_QD, A_QD + A_KVD, A_QD + 2 * A_KVD, A_QD + 2 * A_KVD + B_QD, A_QD + 2 * A_KVD + B_QD + B_KVD)
ATTN_IN_DIM = A_QD + 2 * A_KVD + B_QD + 2 * B_KVD
ATTN_OUT_DIM = A_QD + B_QD

GLA_HEADS = 4
GLA_DK = D_MODEL // (2 * GLA_HEADS)
GLA_DV = D_MODEL // GLA_HEADS
GLA_KD = GLA_HEADS * GLA_DK
GLA_VD = GLA_HEADS * GLA_DV
GLA_RANK = 16
GLA_GATE_NORM = 16.0
GLA_CHUNK = 64
GLA_SPLITS = (GLA_KD, 2 * GLA_KD, 2 * GLA_KD + GLA_VD, 2 * GLA_KD + 2 * GLA_VD, 2 * GLA_KD + 2 * GLA_VD + GLA_RANK)
GLA_IN_DIM = 2 * GLA_KD + 2 * GLA_VD + 2 * GLA_RANK

PEER_HEADS = 8
PEER_N_KEYS = 128
PEER_N_EXPERTS = PEER_N_KEYS * PEER_N_KEYS
PEER_QUERY_DIM = 256
PEER_HALF = PEER_QUERY_DIM // 2
PEER_TOPK = 16
PEER_TOKEN_BLOCK = 128

N_EVEN = (DEPTH + 1) // 2
N_ODD = DEPTH // 2

kernel_name = 'hybrid_latent_dit_attn_gla_peer'

def rmsnorm(x, gain):
    x32 = x.astype(jnp.float32)
    y = x32 * lax.rsqrt(jnp.mean(x32 * x32, axis=-1, keepdims=True) + EPS)
    return (y * gain.astype(jnp.float32)).astype(x.dtype)

def adaln(cond, w, b):
    mod = jax.nn.silu(cond) @ w + b
    return jnp.split(mod[..., None, :], 6, axis=-1)

def axial_rope_tables(rows):
    row = jnp.repeat(jnp.arange(rows), GRID_W)
    col = jnp.tile(jnp.arange(GRID_W), rows)
    pos = jnp.stack([row, col], axis=-1).astype(jnp.float32)
    inv = ROPE_THETA ** (-jnp.arange(ROPE_PAIRS, dtype=jnp.float32) / ROPE_PAIRS)
    ang = pos[:, :, None] * inv
    return jnp.cos(ang), jnp.sin(ang)

def apply_rope(x, cos, sin):
    shape = x.shape
    xs = x.astype(jnp.float32).reshape(shape[:-1] + (2, 2, ROPE_PAIRS))
    bshape = (1, shape[1]) + (1,) * (len(shape) - 3) + (2, ROPE_PAIRS)
    cs, sn = cos.reshape(bshape), sin.reshape(bshape)
    x1, x2 = xs[..., 0, :], xs[..., 1, :]
    out = jnp.stack([x1 * cs - x2 * sn, x1 * sn + x2 * cs], axis=-2)
    return out.reshape(shape).astype(x.dtype)

def softmax_with_sink(s, sink):
    col = jnp.broadcast_to(sink.astype(jnp.float32)[None, :, :, None, None], s.shape[:-1] + (1,))
    return jax.nn.softmax(jnp.concatenate([s, col], axis=-1), axis=-1)[..., :-1]

def split_attn_projection(p):
    bsz, length, _ = p.shape
    qa, ka, va, qb, kb, vb = jnp.split(p, ATTN_SPLITS, axis=-1)
    return (qa.reshape(bsz, length, A_KV_HEADS, A_GROUP, HEAD_DIM),
            ka.reshape(bsz, length, A_KV_HEADS, HEAD_DIM),
            va.reshape(bsz, length, A_KV_HEADS, HEAD_DIM),
            qb.reshape(bsz, length, B_KV_HEADS, B_GROUP, HEAD_DIM),
            kb.reshape(bsz, length, B_KV_HEADS, HEAD_DIM),
            vb.reshape(bsz, length, B_KV_HEADS, HEAD_DIM))

def window_attention_latent(q, k, v, kc, vc, sink):
    bsz, length = q.shape[:2]
    n_blocks = length // Q_BLOCK
    pad = ((0, 0), (WINDOW, WINDOW), (0, 0), (0, 0))
    kp, vp = jnp.pad(k, pad), jnp.pad(v, pad)
    offs = jnp.arange(BAND_SPAN) - WINDOW
    band = jnp.abs(jnp.arange(Q_BLOCK)[:, None] - offs[None, :]) <= WINDOW
    ctx_ok = jnp.ones((Q_BLOCK, kc.shape[1]), dtype=bool)

    def block(n):
        start = n * Q_BLOCK
        qb = lax.dynamic_slice_in_dim(q, start, Q_BLOCK, axis=1)
        kb = jnp.concatenate([lax.dynamic_slice_in_dim(kp, start, BAND_SPAN, axis=1), kc], axis=1)
        vb = jnp.concatenate([lax.dynamic_slice_in_dim(vp, start, BAND_SPAN, axis=1), vc], axis=1)
        pos = start + offs
        valid = jnp.concatenate([band & ((pos >= 0) & (pos < length))[None, :], ctx_ok], axis=1)
        s = jnp.einsum('bqhgd,bkhd->bhgqk', qb, kb).astype(jnp.float32)
        p = softmax_with_sink(jnp.where(valid, s, NEG_INF), sink)
        return jnp.einsum('bhgqk,bkhd->bqhgd', p.astype(vb.dtype), vb)

    out = lax.map(block, jnp.arange(n_blocks))
    return jnp.moveaxis(out, 0, 1).reshape(bsz, length, -1)

def dense_attention_latent(q, k_all, v_all):
    bsz, length = q.shape[:2]

    def block(n):
        qb = lax.dynamic_slice_in_dim(q, n * Q_BLOCK, Q_BLOCK, axis=1)
        s = jnp.einsum('bqhgd,bkhd->bhgqk', qb, k_all).astype(jnp.float32)
        p = jax.nn.softmax(s, axis=-1)
        return jnp.einsum('bhgqk,bkhd->bqhgd', p.astype(v_all.dtype), v_all)

    out = lax.map(block, jnp.arange(length // Q_BLOCK))
    return jnp.moveaxis(out, 0, 1).reshape(bsz, length, -1)

def context_attention(q, k, v, sink):
    s = jnp.einsum('bqhgd,bkhd->bhgqk', q, k).astype(jnp.float32)
    p = jax.nn.softmax(s, axis=-1) if sink is None else softmax_with_sink(s, sink)
    o = jnp.einsum('bhgqk,bkhd->bqhgd', p.astype(v.dtype), v)
    return o.reshape(o.shape[0], o.shape[1], -1)

def attention_mixer(h_lat, h_ctx, w_in, w_out, sink, q_gain, k_gain, cos, sin, need_ctx):
    scale = HEAD_DIM ** -0.5
    qa, ka, va, qb, kb, vb = split_attn_projection(h_lat @ w_in)
    qa_c, ka_c, va_c, qb_c, kb_c, vb_c = split_attn_projection(h_ctx @ w_in)
    sink = sink.reshape(A_KV_HEADS, A_GROUP)
    qa = apply_rope(qa, cos, sin) * scale
    ka = apply_rope(ka, cos, sin)
    out_a = window_attention_latent(qa, ka, va, ka_c, va_c, sink)
    qb = apply_rope(rmsnorm(qb, q_gain), cos, sin) * scale
    kb = apply_rope(rmsnorm(kb, k_gain), cos, sin)
    kb_c = rmsnorm(kb_c, k_gain)
    out_b = dense_attention_latent(qb, jnp.concatenate([kb, kb_c], axis=1), jnp.concatenate([vb, vb_c], axis=1))
    y_lat = jnp.concatenate([out_a, out_b], axis=-1) @ w_out
    y_ctx = None
    if need_ctx:
        out_a_c = context_attention(qa_c * scale, ka_c, va_c, sink)
        out_b_c = context_attention(rmsnorm(qb_c, q_gain) * scale, kb_c, vb_c, None)
        y_ctx = jnp.concatenate([out_a_c, out_b_c], axis=-1) @ w_out
    return y_lat, y_ctx

def gla_project(h, w_in, gate_w, gate_b):
    bsz, length, _ = h.shape
    q, k, v, r, g_f, g_b = jnp.split(h @ w_in, GLA_SPLITS, axis=-1)

    def heads(t, d):
        return t.reshape(bsz, length, GLA_HEADS, d)

    def log_decay(g, i):
        return heads(jax.nn.log_sigmoid((g @ gate_w[i] + gate_b[i]).astype(jnp.float32)) / GLA_GATE_NORM, GLA_DK)

    return (heads(q, GLA_DK) * GLA_DK ** -0.5, heads(k, GLA_DK), heads(v, GLA_DV), heads(r, GLA_DV),
            log_decay(g_f, 0), log_decay(g_b, 1))

def gla_chunked(q, k, v, log_g, state0, with_output):
    bsz, length, nh, _ = q.shape
    dv = v.shape[-1]
    nc = length // GLA_CHUNK

    def to_chunks(t):
        return jnp.transpose(t.astype(jnp.float32).reshape(bsz, nc, GLA_CHUNK, nh, t.shape[-1]), (1, 0, 3, 2, 4))

    qc, kc, vc, gc = (to_chunks(t) for t in (q, k, v, log_g))
    b = jnp.cumsum(gc, axis=3)
    b_end = b[:, :, :, -1:, :]
    k_end = kc * jnp.exp(b_end - b)
    decay_end = jnp.exp(b[:, :, :, -1, :])
    if not with_output:
        def step_state(S, xs):
            ke, vv, de = xs
            return de[..., None] * S + jnp.einsum('bhcd,bhce->bhde', ke, vv), None
        s_fin, _ = lax.scan(step_state, state0, (k_end, vc, decay_end))
        return None, s_fin
    q_dec = qc * jnp.exp(b)

    def step(S, xs):
        qd, ke, vv, de = xs
        inter = jnp.einsum('bhcd,bhde->bhce', qd, S)
        return de[..., None] * S + jnp.einsum('bhcd,bhce->bhde', ke, vv), inter

    s_fin, inter = lax.scan(step, state0, (q_dec, k_end, vc, decay_end))
    lower = jnp.tril(jnp.ones((GLA_CHUNK, GLA_CHUNK), dtype=bool))
    att = jnp.einsum('nbhcd,nbhsd->nbhcs', q_dec, kc * jnp.exp(-b))
    intra = jnp.einsum('nbhcs,nbhse->nbhce', jnp.where(lower, att, 0.0), vc)
    out = jnp.transpose(inter + intra, (1, 0, 3, 2, 4)).reshape(bsz, length, nh, dv)
    return out.astype(v.dtype), s_fin

def gla_mixer(h_lat, h_ctx, w_in, gate_w, gate_b, head_gain, w_out, need_ctx):
    bsz = h_lat.shape[0]
    ql, kl, vl, rl, gfl, gbl = gla_project(h_lat, w_in, gate_w, gate_b)
    qc, kc, vc, rc, gfc, gbc = gla_project(h_ctx, w_in, gate_w, gate_b)
    s0 = jnp.zeros((bsz, GLA_HEADS, GLA_DK, GLA_DV), jnp.float32)

    def rev(t):
        return jnp.flip(t, axis=1)

    o_cf, s_f = gla_chunked(qc, kc, vc, gfc, s0, need_ctx)
    o_cb, s_b = gla_chunked(rev(qc), rev(kc), rev(vc), rev(gbc), s0, need_ctx)
    o_lf, _ = gla_chunked(ql, kl, vl, gfl, s_f, True)
    o_lb, _ = gla_chunked(rev(ql), rev(kl), rev(vl), rev(gbl), s_b, True)

    def finish(o, r):
        y = rmsnorm(o, head_gain) * jax.nn.silu(r)
        return y.reshape(bsz, y.shape[1], GLA_VD) @ w_out

    y_lat = finish(o_lf + rev(o_lb), rl)
    y_ctx = finish(o_cf + rev(o_cb), rc) if need_ctx else None
    return y_lat, y_ctx

def peer_ffn(h, w_query, sub_keys, u, v):
    shape = h.shape
    t = h.reshape(-1, shape[-1])
    n_tok = t.shape[0]
    q = (t @ w_query).reshape(n_tok, PEER_HEADS, 2, PEER_HALF)
    s = jnp.einsum('thpd,hpnd->thpn', q, sub_keys).astype(jnp.float32)
    s_top, i_top = lax.top_k(s, PEER_TOPK)
    cand_s = (s_top[:, :, 0, :, None] + s_top[:, :, 1, None, :]).reshape(n_tok, PEER_HEADS, PEER_TOPK * PEER_TOPK)
    cand_i = (i_top[:, :, 0, :, None] * PEER_N_KEYS + i_top[:, :, 1, None, :]).reshape(n_tok, PEER_HEADS, PEER_TOPK * PEER_TOPK)
    best_s, best_pos = lax.top_k(cand_s, PEER_TOPK)
    experts = jnp.take_along_axis(cand_i, best_pos, axis=-1)
    gates = jax.nn.softmax(best_s, axis=-1).astype(h.dtype)
    nb = n_tok // PEER_TOKEN_BLOCK

    def block(args):
        tb, eb, gb = args
        act = jax.nn.gelu(jnp.einsum('td,thkd->thk', tb, jnp.take(u, eb, axis=0)), approximate=False)
        return jnp.einsum('thk,thkd->td', gb * act, jnp.take(v, eb, axis=0))

    out = lax.map(block, (t.reshape(nb, PEER_TOKEN_BLOCK, shape[-1]),
                          experts.reshape(nb, PEER_TOKEN_BLOCK, PEER_HEADS, PEER_TOPK),
                          gates.reshape(nb, PEER_TOKEN_BLOCK, PEER_HEADS, PEER_TOPK)))
    return out.reshape(shape)

def setup_inputs(seed: int = 0) -> dict:
    key = jax.random.key(seed)
    ks = jax.random.split(key, 23)

    def nrm(k, shape, scale):
        return scale * jax.random.normal(k, shape, jnp.float32)

    def gain(k, shape):
        return 1.0 + 0.02 * jax.random.normal(k, shape, jnp.float32)

    return {
        'x': nrm(ks[0], (BATCH, SEQ, D_MODEL), 1.0),
        'c': nrm(ks[1], (BATCH, D_MODEL), 1.0),
        'ctx': nrm(ks[2], (BATCH, CTX_LEN, D_MODEL), 1.0),
        'c_ctx': nrm(ks[3], (D_MODEL,), 1.0),
        'ada_w': nrm(ks[4], (DEPTH, D_MODEL, 6 * D_MODEL), 0.5 * D_MODEL ** -0.5),
        'ada_b': nrm(ks[5], (DEPTH, 6 * D_MODEL), 0.02),
        'norm_mix': gain(ks[6], (DEPTH, D_MODEL)),
        'norm_ffn': gain(ks[7], (DEPTH, D_MODEL)),
        'attn_w_in': nrm(ks[8], (N_EVEN, D_MODEL, ATTN_IN_DIM), D_MODEL ** -0.5),
        'attn_sink': nrm(ks[9], (N_EVEN, A_Q_HEADS), 1.0),
        'attn_q_gain': gain(ks[10], (N_EVEN, HEAD_DIM)),
        'attn_k_gain': gain(ks[11], (N_EVEN, HEAD_DIM)),
        'attn_w_out': nrm(ks[12], (N_EVEN, ATTN_OUT_DIM, D_MODEL), ATTN_OUT_DIM ** -0.5),
        'gla_w_in': nrm(ks[13], (N_ODD, D_MODEL, GLA_IN_DIM), D_MODEL ** -0.5),
        'gla_gate_w': nrm(ks[14], (N_ODD, 2, GLA_RANK, GLA_KD), GLA_RANK ** -0.5),
        'gla_gate_b': nrm(ks[15], (N_ODD, 2, GLA_KD), 0.1),
        'gla_head_gain': gain(ks[16], (N_ODD, GLA_DV)),
        'gla_w_out': nrm(ks[17], (N_ODD, GLA_VD, D_MODEL), GLA_VD ** -0.5),
        'peer_wq': nrm(ks[18], (DEPTH, D_MODEL, PEER_HEADS * PEER_QUERY_DIM), D_MODEL ** -0.5),
        'peer_keys': nrm(ks[19], (DEPTH, PEER_HEADS, 2, PEER_N_KEYS, PEER_HALF), PEER_HALF ** -0.5),
        'peer_u': nrm(ks[20], (DEPTH, PEER_N_EXPERTS, D_MODEL), D_MODEL ** -0.5),
        'peer_v': nrm(ks[21], (DEPTH, PEER_N_EXPERTS, D_MODEL), 1.0),
        'final_norm': gain(ks[22], (D_MODEL,)),
    }

def reference(x, c, ctx, c_ctx, ada_w, ada_b, norm_mix, norm_ffn, attn_w_in, attn_sink, attn_q_gain,
              attn_k_gain, attn_w_out, gla_w_in, gla_gate_w, gla_gate_b, gla_head_gain, gla_w_out,
              peer_wq, peer_keys, peer_u, peer_v, final_norm):
    length = x.shape[1]
    rows = length // GRID_W
    cos, sin = axial_rope_tables(rows)
    x_lat, x_ctx = x, ctx
    for layer in range(DEPTH):
        need_ctx = layer < DEPTH - 1
        sh1, sc1, g1, sh2, sc2, g2 = adaln(c, ada_w[layer], ada_b[layer])
        csh1, csc1, cg1, csh2, csc2, cg2 = adaln(c_ctx[None], ada_w[layer], ada_b[layer])
        h_lat = rmsnorm(x_lat, norm_mix[layer]) * (1.0 + sc1) + sh1
        h_ctx = rmsnorm(x_ctx, norm_mix[layer]) * (1.0 + csc1) + csh1
        j = layer // 2
        if layer % 2 == 0:
            y_lat, y_ctx = attention_mixer(h_lat, h_ctx, attn_w_in[j], attn_w_out[j], attn_sink[j],
                                           attn_q_gain[j], attn_k_gain[j], cos, sin, need_ctx)
        else:
            y_lat, y_ctx = gla_mixer(h_lat, h_ctx, gla_w_in[j], gla_gate_w[j], gla_gate_b[j],
                                     gla_head_gain[j], gla_w_out[j], need_ctx)
        x_lat = x_lat + g1 * y_lat
        f_lat = rmsnorm(x_lat, norm_ffn[layer]) * (1.0 + sc2) + sh2
        x_lat = x_lat + g2 * peer_ffn(f_lat, peer_wq[layer], peer_keys[layer], peer_u[layer], peer_v[layer])
        if need_ctx:
            x_ctx = x_ctx + cg1 * y_ctx
            f_ctx = rmsnorm(x_ctx, norm_ffn[layer]) * (1.0 + csc2) + csh2
            x_ctx = x_ctx + cg2 * peer_ffn(f_ctx, peer_wq[layer], peer_keys[layer], peer_u[layer], peer_v[layer])
    return rmsnorm(x_lat, final_norm)


_drawn_inputs = setup_inputs


def setup_inputs(seed=0):
    import zlib

    import numpy as np

    out = dict(_drawn_inputs(seed))
    spreads = {}
    factors = {'norm_mix': 3.013,
     'attn_sink': 44.948,
     'attn_q_gain': 6.828,
     'attn_k_gain': 5.751,
     'gla_gate_b': 3.124,
     'gla_head_gain': 13.755,
     'final_norm': 7.668}
    for name, (base, spread) in spreads.items():
        noise = np.random.default_rng([zlib.crc32(name.encode()), seed]).standard_normal(out[name].shape)
        drawn = base * np.exp(spread * noise) if base else spread * noise
        out[name] = jnp.asarray(drawn.astype(out[name].dtype))
    for name, factor in factors.items():
        out[name] = (out[name] * factor).astype(out[name].dtype)
    return out
```

```python
from contextlib import ExitStack

import concourse.bass as bass
import numpy as np
from concourse import mybir

F32 = mybir.dt.float32
U32 = mybir.dt.uint32
ALU = mybir.AluOpType
ACT = mybir.ActivationFunctionType
AX_X = mybir.AxisListType.X

P = 128
D = 1024
KC = D // P
SEQ = 256
LAT_TILES = SEQ // P
TILES = 2 * LAT_TILES
WBLK = 512
EPS = 1e-6
LAYERS = 2
SECTIONS = 6
MOD_DIM = SECTIONS * D

HEAD_DIM = 64
GRID_W = 64
ROPE_PAIRS = HEAD_DIM // 4
HEADS_A = 8
ATTN_HEADS = 16
KV_GROUP = 4
ATTN_IN = 1536
ATTN_SCALE = HEAD_DIM**-0.5
B_OFF = 768
WINDOW = 128

GLA_HEADS = 4
DK = 128
DV = 256
KD = GLA_HEADS * DK
VD = GLA_HEADS * DV
RANK = 16
GATE_NORM = 16.0
CHUNK = 64
CHUNKS = SEQ // CHUNK
GLA_IN = 2 * KD + 2 * VD + 2 * RANK

PEER_HEADS = 8
N_KEYS = 128
EXPERTS = N_KEYS * N_KEYS
TOPK = 16
RING = 8
DIAGS = 4
LOWEST = -3.0e38

C_IDENT = 0
C_UPPER = 128
C_LOWER = 256
C_UPPER_STRICT = 384
C_LOWER_STRICT = 512
C_BAND = 640
C_COS = 896
C_SIN = 1024
C_IOTA = 1152
C_CHUNK = 1168
C_COLS = 1170


def shape_constants():
    c = np.zeros((P, C_COLS), np.float32)
    i = np.arange(P)
    same = (i[:, None] // CHUNK) == (i[None, :] // CHUNK)
    c[:, C_IDENT:C_IDENT + P] = np.eye(P)
    c[:, C_UPPER:C_UPPER + P] = same & (i[:, None] <= i[None, :])
    c[:, C_LOWER:C_LOWER + P] = same & (i[:, None] >= i[None, :])
    c[:, C_UPPER_STRICT:C_UPPER_STRICT + P] = same & (i[:, None] < i[None, :])
    c[:, C_LOWER_STRICT:C_LOWER_STRICT + P] = same & (i[:, None] > i[None, :])
    for t in range(LAT_TILES):
        query, key = t * P + i[:, None], (1 - t) * P + i[None, :]
        c[:, C_BAND + t * P:C_BAND + (t + 1) * P] = np.where(np.abs(query - key) <= WINDOW, 0.0, -1e30)
        tok = t * P + i
        pos = np.stack([tok // GRID_W, tok % GRID_W], -1).astype(np.float32)
        inv = (10000.0 ** (-np.arange(ROPE_PAIRS, dtype=np.float32) / ROPE_PAIRS)).astype(np.float32)
        ang = pos[:, :, None] * inv
        cos, sin = np.cos(ang), np.sin(ang)
        w = HEAD_DIM
        c[:, C_COS + t * w:C_COS + (t + 1) * w] = np.stack([cos, cos], 2).reshape(P, w)
        c[:, C_SIN + t * w:C_SIN + (t + 1) * w] = np.stack([-sin, sin], 2).reshape(P, w)
    c[:, C_IOTA:C_IOTA + TOPK] = np.arange(TOPK)
    c[:, C_CHUNK] = i < CHUNK
    c[:, C_CHUNK + 1] = i >= CHUNK
    return c


def build(nc, x, c, ctx, c_ctx, ada_w, ada_b, norm_mix, norm_ffn, attn_w_in, attn_sink, attn_q_gain,
          attn_k_gain, attn_w_out, gla_w_in, gla_gate_w, gla_gate_b, gla_head_gain, gla_w_out,
          peer_wq, peer_keys, peer_u, peer_v, final_norm, consts, out, stop=99):
    mod_dram = nc.dram_tensor("mod_dram", (2, LAYERS, SECTIONS, D), F32, kind="Internal").ap()
    expert_u = peer_u.rearrange("l e d -> (l e) d")
    expert_v = peer_v.rearrange("l e d -> (l e) d")

    blocks = []

    def stream(name, w, n):
        for b in range(-(-n // WBLK)):
            cols = min(WBLK, n - b * WBLK)
            blocks.append((name, b, w.rearrange("(k p) n -> p k n", p=P)[:, :, b * WBLK:b * WBLK + cols], cols))

    for layer in range(LAYERS):
        stream(f"ada{layer}", ada_w[layer], MOD_DIM)
    stream("attn_in", attn_w_in[0], ATTN_IN)
    stream("out0", attn_w_out[0], D)
    stream("query0", peer_wq[0], 2 * D)
    stream("gla_in", gla_w_in[0], GLA_IN)
    stream("out1", gla_w_out[0], D)
    stream("query1", peer_wq[1], 2 * D)
    block_at = {(name, b): n for n, (name, b, _, _) in enumerate(blocks)}
    WSLOTS = 3

    with ExitStack() as es:
        def sb(name, shape, dt=F32):
            return es.enter_context(nc.sbuf_tensor(name, shape, dt))

        def sem(name):
            return es.enter_context(nc.semaphore(name))

        xs = sb("xs", [P, TILES, D])
        wring = sb("wring", [P, WSLOTS, KC, WBLK])
        mod_rows = sb("mod_rows", [P, 2, 2, D])
        gate_rows = sb("gate_rows", [P, 2, D])
        cst = sb("cst", [P, C_COLS])
        work = sb("work", [P, 28672])
        stat = sb("stat", [P, 32])
        diag = sb("diag", [P, DIAGS, P])
        picks_u = sb("picks_u", [P, 80], U32)
        idx_u = sb("idx_u", [P, 2, TOPK], U32)
        idx_v = sb("idx_v", [P, 2, TOPK], U32)
        bank = [es.enter_context(nc.psum_tensor(f"bank{i}", [P, WBLK], F32)) for i in range(8)]

        def at(start, *dims):
            n = int(np.prod(dims))
            v = work[:, start:start + n]
            if len(dims) == 2:
                return v.rearrange("p (a b) -> p a b", a=dims[0])
            if len(dims) == 3:
                return v.rearrange("p (a b c) -> p a b c", a=dims[0], b=dims[1])
            return v

        ident = cst[:, C_IDENT:C_IDENT + P]

        ada_bias = at(0, LAYERS * MOD_DIM)
        mods = at(12288, LAYERS * MOD_DIM)
        norm_gains = at(24576, 4, D)
        proj = at(0, TILES, ATTN_IN)
        qkT = at(6144, 12, TILES * P)
        hT = at(12288, KC, TILES * P)
        h = at(16384, TILES, D)
        kdup = at(20480, 2, 4, P)
        swapped = at(21504, 640)
        turned = at(22144, 640)
        probs = at(21504, 2, TILES * P)
        probsT = at(22784, 2, TILES * P)
        qk_gain = at(23808, 2, HEAD_DIM)
        sinks = at(23936, HEADS_A)
        update = at(9344, 2, WBLK)
        att_stat = at(25984, 4, 4)
        qk_stat = at(26000, 4, TILES * 10)
        cond_in = xs[:, TILES - 1, 0:P]
        cond_act = xs[:, TILES - 1, P:P + 2 * KC]
        cond_tmp = xs[:, TILES - 1, 2 * P:2 * P + 2 * KC]

        scores = at(0, TILES * PEER_HEADS, 2 * N_KEYS)
        ffn_in = at(8192, TILES, D)
        ffn_inT = at(12288, KC, TILES * P)
        keys = at(16384, 16, P)
        keysT = at(18432, 16, P)
        queryT = at(20480, 2, TILES * P)
        u_rows = at(12288, RING, D)
        v_rows = at(20480, RING, D)
        tile_in = [mod_rows[:, 0, par, :] for par in range(2)]
        route = mod_rows[:, 1, :, :].rearrange("p a b -> p (a b)")

        def route_at(start, *dims):
            n = int(np.prod(dims))
            v = route[:, start:start + n]
            return v.rearrange("p (a b) -> p a b", a=dims[0]) if len(dims) == 2 else v

        head_scores = route_at(0, 2, 2 * N_KEYS)
        best = route_at(512, 2, TOPK)
        sums = route_at(768, TOPK * TOPK)
        rest_sums = route_at(1024, TOPK * TOPK)
        one_hot = route_at(1280, 2 * TOPK * TOPK)
        rest_scores = route_at(1280, 2, N_KEYS)
        act_raw = route_at(1792, 2, TOPK)
        act_gelu = route_at(1824, 2, TOPK)
        gate_num = route_at(1856, 2, TOPK)
        pick_weight = route_at(1888, 2, TOPK)
        gate_sum = route_at(1920, 2)
        neg_best = route_at(1922, 2)
        top = route_at(1924, 2, TOPK)
        top_at = route_at(1956, 2, TOPK)
        best_pair = route_at(1988, 2 * TOPK)
        top_at_u = picks_u[:, 0:2 * TOPK].rearrange("p (a b) -> p a b", a=2)
        best_at_u = picks_u[:, 2 * TOPK:3 * TOPK]
        best_pair_u = picks_u[:, 3 * TOPK:5 * TOPK]

        gla_lat = at(0, LAT_TILES, 2 * KD + 2 * VD)
        gla_ctx = at(6144, LAT_TILES, KD + VD)
        gate_low = at(9216, TILES, 2 * RANK)
        log_decay = at(9344, TILES, KD)
        k_end = at(11392, TILES, KD)
        q_dec = at(13440, LAT_TILES, KD)
        k_inv = at(14464, LAT_TILES, KD)
        q_decT = at(15488, GLA_HEADS, SEQ)
        k_invT = at(16512, GLA_HEADS, SEQ)
        states = at(17536, GLA_HEADS, CHUNKS, DV)
        decay_end = at(21632, GLA_HEADS, TILES, 2)
        gla_o = at(21664, LAT_TILES, VD)
        att_masked = at(23712, 4, P)
        head_gain = at(24224, DV)
        gla_hT = at(24576, KC, TILES * P)
        h_gla = at(20480, TILES, D)
        gate_w = at(24576, 2, KD)
        gate_bias = at(25600, 2, KD)
        gate_lowT = at(26624, 2, TILES * P)
        gate_tmp = at(27648, 2, KD)
        silu_r = at(9344, LAT_TILES, VD)

        w_loaded = [sem(f"w_loaded{i}") for i in range(WSLOTS)]
        bank_filled = [sem(f"bank_filled{i}") for i in range(8)]
        bank_drained = [sem(f"bank_drained{i}") for i in range(8)]
        stage_over = sem("stage_over")
        dve_step = sem("dve_step")
        held = sem("held")
        act_step = sem("act_step")
        pool_loads = sem("pool_loads")
        stored = sem("stored")
        cond_exp_ready = sem("cond_exp_ready")
        cond_ready = sem("cond_ready")
        mods_ready = sem("mods_ready")
        sumsq_ready = sem("sumsq_ready")
        mean_ready = sem("mean_ready")
        root_ready = sem("root_ready")
        h_ready = sem("h_ready")
        qk_ready = sem("qk_ready")
        att_max = sem("att_max")
        gate_z = sem("gate_z")
        gate_ln = sem("gate_ln")
        decay_ready = sem("decay_ready")
        exp_ready = sem("exp_ready")
        sink_exp = sem("sink_exp")
        decay_end_ready = sem("decay_end_ready")
        keyed_ready = sem("keyed_ready")
        state_ready = sem("state_ready")
        masked_ready = sem("masked_ready")
        silu_exp = sem("silu_exp")
        out_ready = sem("out_ready")

        u_in = [sem(f"u_in{i}") for i in range(RING)]
        v_in = [sem(f"v_in{i}") for i in range(RING)]
        u_free = sem("u_free")
        v_free = sem("v_free")
        y_free = sem("y_free")
        idx_u_ready = sem("idx_u_ready")
        idx_v_ready = sem("idx_v_ready")
        head_scores_ready = sem("head_scores_ready")
        tile_in_ready = sem("tile_in_ready")
        best_ready = sem("best_ready")
        gate_num_ready = sem("gate_num_ready")
        gelu_ready = sem("gelu_ready")
        weight_ready = sem("weight_ready")
        diag_ready = sem("diag_ready")

        block = es.enter_context(nc.Block())

        class Count:

            def __init__(self):
                self.n = {}

            def next(self, name, more=1):
                self.n[name] = self.n.get(name, 0) + more
                return self.n[name]

        class Steps:

            def __init__(self, eng, done):
                self.eng, self.done, self.base, self.n = eng, done, 0, 0

            def link(self, ins):
                self.n += 1
                ins.then_inc(self.done, 1)
                self.eng.wait_ge(self.done, self.base + self.n)

        def hold(eng):
            eng.sem_inc(held, 1)

        stage_count = {}

        def end_stage(name, eng):
            n = stage_count[name] = stage_count.get(name, 0) + 1
            eng.drain().then_inc(stage_over, 1)
            eng.wait_ge(stage_over, 4 * n)
            return n >= stop

        uses = [0] * 8
        turn = {}
        weights_done = {}

        def open_bank(pe, key, b):
            n = uses[b]
            uses[b] += 1
            turn[key] = (b, n)
            if n:
                pe.wait_ge(bank_drained[b], n)
            return bank[b]

        def wait_bank(eng, key):
            b, n = turn[key]
            eng.wait_ge(bank_filled[b], n + 1)
            return b

        def wait_drained(eng, key):
            b, n = turn[key]
            eng.wait_ge(bank_drained[b], n + 1)

        def wait_weights(pe, name, b):
            n = block_at[name, b]
            pe.wait_ge(w_loaded[n % WSLOTS], 16 * (n // WSLOTS + 1))
            return wring[:, n % WSLOTS, :, :]

        def last_four(name, tiles):
            return [(name, t, half) for t in range(tiles - 2, tiles) for half in range(2)]

        cond_loads = 16 * 8
        first_loads = cond_loads + 16 * 5
        attn_loads = first_loads + 16 * 3
        key_loads = [attn_loads + 16 * 5, 0]
        gla_loads = key_loads[0] + 16 * 7
        key_loads[1] = gla_loads + 16 * 3
        final_loads = key_loads[1] + 16
        final_rows = 3 * TILES + LAT_TILES + LAT_TILES

        attn_steps = [(t, hd) for t in range(TILES) for hd in range(ATTN_HEADS)]
        gla_jobs = [(t, hh) for t in range(LAT_TILES) for hh in range(GLA_HEADS)]
        GATHER_LAYER_STEPS = TILES * PEER_HEADS

        def gla_tiles(n):
            return range(TILES) if n in (1, 2, 3, 6) else range(LAT_TILES)

        def gla_updates(d):
            order = range(CHUNKS) if d == 0 else range(CHUNKS - 1, -1, -1)
            order = list(order)
            out = []
            for n in range(CHUNKS):
                out += [(hh, "ctx", order[n], order[0]) for hh in range(GLA_HEADS)]
            for n in range(CHUNKS - 1):
                out += [(hh, "lat", order[n], order[n + 1]) for hh in range(GLA_HEADS)]
            return out

        @block.tensor
        def _(pe):
            count = Count()

            def conditions():
                pe.wait_ge(pool_loads, cond_loads)
                b = open_bank(pe, "cond", 7)
                pe.transpose(b[:, 0:2 * KC], cond_in[0:2 * KC, :], ident[0:2 * KC, 0:2 * KC]).then_inc(bank_filled[7], 1)
                pe.wait_ge(cond_ready, 1)
                cond = cond_act.rearrange("p (c k) -> p k c", c=2)
                for layer in range(LAYERS):
                    for n in range(MOD_DIM // WBLK):
                        w = wait_weights(pe, f"ada{layer}", n)
                        j = n % 4
                        b = open_bank(pe, ("ada", layer, n), j)
                        for k in range(KC):
                            mm = pe.matmul(b[0:2, :], cond[:, k, :], w[:, k, :], start=(k == 0), stop=(k == KC - 1))
                        mm.then_inc(bank_filled[j], 1)
                        weights_done[f"ada{layer}", n] = turn["ada", layer, n]

            def turn_rows(name, src, tiles, wait):
                for t in range(tiles):
                    if wait:
                        pe.wait_ge(h_ready, count.next("h"))
                    for half in range(2):
                        j = (2 * t + half) % 4
                        b = open_bank(pe, (name, t, half), j)
                        for k in range(4):
                            c0 = (4 * half + k) * P
                            mm = pe.transpose(b[:, k * P:(k + 1) * P], src[:, t, c0:c0 + P], ident)
                        mm.then_inc(bank_filled[j], 1)
                for key in last_four(name, tiles):
                    wait_drained(pe, key)

            def project(name, src, n_cols, tiles_of):
                step = 0
                for n in range(-(-n_cols // WBLK)):
                    cols = min(WBLK, n_cols - n * WBLK)
                    w = wait_weights(pe, name, n)
                    for t in tiles_of(n):
                        j = 4 + step % 2
                        step += 1
                        b = open_bank(pe, (name, n, t), j)
                        for k in range(KC):
                            mm = pe.matmul(b[:, 0:cols], src[:, k, t * P:(t + 1) * P], w[:, k, 0:cols],
                                           start=(k == 0), stop=(k == KC - 1))
                        mm.then_inc(bank_filled[j], 1)
                    weights_done[name, n] = turn[name, n, t]

            def attention():
                for t in range(TILES):
                    pe.wait_ge(qk_ready, t + 1)
                    for g in range(3):
                        j = (3 * t + g) % 4
                        b = open_bank(pe, ("qkT", t, g), j)
                        for k in range(4):
                            if g < 2:
                                c0 = g * B_OFF + k * P
                                src = proj[:, t, c0:c0 + P]
                            else:
                                src = kdup[:, t % 2, k, :]
                            mm = pe.transpose(b[:, k * P:(k + 1) * P], src, ident)
                        mm.then_inc(bank_filled[j], 1)
                for g in range(8, 3 * TILES):
                    wait_drained(pe, ("qkT", g // 3, g % 3))
                for i in range(len(attn_steps) + 2):
                    if i < len(attn_steps):
                        t, hd = attn_steps[i]
                        kind, hh = divmod(hd, HEADS_A)
                        rows = slice(HEAD_DIM * (hh % 2), HEAD_DIM * (hh % 2) + HEAD_DIM)
                        k0 = 0 if t < LAT_TILES else SEQ
                        j = i % 2
                        b = open_bank(pe, ("s", i), j)
                        pe.matmul(b[:, 0:TILES * P - k0], qkT[rows, kind * 4 + hh // 2, t * P:(t + 1) * P],
                                  qkT[rows, 8 + kind * 2 + hh // KV_GROUP, k0:TILES * P],
                                  start=True, stop=True).then_inc(bank_filled[j], 1)
                    if 1 <= i <= len(attn_steps):
                        m = i - 1
                        nk = TILES if attn_steps[m][0] < LAT_TILES else LAT_TILES
                        j = 2 + m % 2
                        b = open_bank(pe, ("pT", m), j)
                        wait_drained(pe, ("s", m))
                        for k in range(nk):
                            mm = pe.transpose(b[:, k * P:(k + 1) * P], probs[:, m % 2, k * P:(k + 1) * P], ident)
                        mm.then_inc(bank_filled[j], 1)
                    if i >= 2:
                        m = i - 2
                        t, hd = attn_steps[m]
                        kind, hh = divmod(hd, HEADS_A)
                        nk = TILES if t < LAT_TILES else LAT_TILES
                        vcol = kind * B_OFF + 640 + (hh // KV_GROUP) * HEAD_DIM
                        j = 4 + m % 2
                        b = open_bank(pe, ("o", m), j)
                        wait_drained(pe, ("pT", m))
                        for k in range(nk):
                            mm = pe.matmul(b[:, 0:HEAD_DIM], probsT[:, m % 2, k * P:(k + 1) * P],
                                           proj[:, TILES - nk + k, vcol:vcol + HEAD_DIM],
                                           start=(k == 0), stop=(k == nk - 1))
                        mm.then_inc(bank_filled[j], 1)

            def gla():
                pe.wait_ge(pool_loads, gla_loads)
                for d in range(2):
                    b = open_bank(pe, ("gateT", d), d)
                    for t in range(TILES):
                        mm = pe.transpose(b[0:RANK, t * P:(t + 1) * P], gate_low[:, t, d * RANK:(d + 1) * RANK], ident)
                    mm.then_inc(bank_filled[d], 1)
                for d in range(2):
                    wait_drained(pe, ("gateT", d))
                for d in range(2):
                    c_incl, c_rest = (C_UPPER, C_LOWER)[d], (C_LOWER_STRICT, C_UPPER_STRICT)[d]
                    for t in range(TILES):
                        j = t % 2
                        b = open_bank(pe, ("z", d, t), j)
                        pe.matmul(b[:, :], gate_lowT[0:RANK, d, t * P:(t + 1) * P], gate_w[0:RANK, d, :],
                                  start=True, stop=True).then_inc(bank_filled[j], 1)
                    for t in range(TILES):
                        pe.wait_ge(decay_ready, count.next("decay"))
                        if t < LAT_TILES:
                            b = open_bank(pe, ("b", d, t), 2)
                            pe.matmul(b[:, :], cst[:, c_incl:c_incl + P], log_decay[:, t, :],
                                      start=True, stop=True).then_inc(bank_filled[2], 1)
                        b = open_bank(pe, ("rest", d, t), 3)
                        pe.matmul(b[:, :], cst[:, c_rest:c_rest + P], log_decay[:, t, :],
                                  start=True, stop=True).then_inc(bank_filled[3], 1)
                    b = open_bank(pe, ("end", d), 4)
                    for hh in range(GLA_HEADS):
                        for t in range(TILES):
                            c0 = (hh * TILES + t) * 2
                            mm = pe.matmul(b[:, c0:c0 + 2], log_decay[:, t, hh * DK:(hh + 1) * DK],
                                           cst[:, C_CHUNK:C_CHUNK + 2], start=True, stop=True)
                    mm.then_inc(bank_filled[4], 1)
                    pe.wait_ge(keyed_ready, count.next("keyed", TILES))
                    for t in range(LAT_TILES):
                        for which, src in enumerate((q_dec, k_inv)):
                            j = 5 + which
                            b = open_bank(pe, ("qkdT", d, t, which), j)
                            for hh in range(GLA_HEADS):
                                mm = pe.transpose(b[:, hh * P:(hh + 1) * P], src[:, t, hh * DK:(hh + 1) * DK], ident)
                            mm.then_inc(bank_filled[j], 1)
                    for n, (hh, kind, chunk, _) in enumerate(gla_updates(d)):
                        t, r = divmod(chunk, 2)
                        rows = slice(CHUNK * r, CHUNK * r + CHUNK)
                        j = n % 2
                        b = open_bank(pe, ("kv", d, n), j)
                        if kind == "ctx":
                            v = gla_ctx[rows, t, KD + hh * DV:KD + (hh + 1) * DV]
                            t += LAT_TILES
                        else:
                            v = gla_lat[rows, t, 2 * KD + hh * DV:2 * KD + (hh + 1) * DV]
                        pe.matmul(b[:, 0:DV], k_end[rows, t, hh * DK:(hh + 1) * DK], v,
                                  start=True, stop=True).then_inc(bank_filled[j], 1)
                    for which in range(2):
                        wait_drained(pe, ("qkdT", d, LAT_TILES - 1, which))
                    pe.wait_ge(state_ready, count.next("state", len(gla_updates(d))))
                    for i in range(len(gla_jobs) + 1):
                        if i < len(gla_jobs):
                            t, hh = gla_jobs[i]
                            j = 2 + i % 2
                            b = open_bank(pe, ("att", d, i), j)
                            cols = slice(t * P, (t + 1) * P)
                            pe.matmul(b[:, 0:P], k_invT[:, hh, cols], q_decT[:, hh, cols],
                                      start=True, stop=True).then_inc(bank_filled[j], 1)
                        if i >= 1:
                            m = i - 1
                            t, hh = gla_jobs[m]
                            j = 4 + m % 2
                            b = open_bank(pe, ("go", d, m), j)
                            pe.wait_ge(masked_ready, count.next("masked"))
                            pe.matmul(b[:, 0:DV], att_masked[:, 2 * d + m % 2, :],
                                      gla_lat[:, t, 2 * KD + hh * DV:2 * KD + (hh + 1) * DV],
                                      start=True, stop=False, skip_group_check=True)
                            for r in range(2):
                                c0 = t * P + r * CHUNK
                                mm = pe.matmul(b[r * CHUNK:(r + 1) * CHUNK, 0:DV], q_decT[:, hh, c0:c0 + CHUNK],
                                               states[:, hh, 2 * t + r, :], start=False, stop=True,
                                               skip_group_check=True)
                            mm.then_inc(bank_filled[j], 1)

            def query_scores(layer, tiles):
                pe.wait_ge(pool_loads, key_loads[layer])
                for g in range(4):
                    b = open_bank(pe, ("keysT", layer, g), g)
                    for k in range(4):
                        mm = pe.transpose(b[:, k * P:(k + 1) * P], keys[:, 4 * g + k, :], ident)
                    mm.then_inc(bank_filled[g], 1)
                for g in range(4):
                    wait_drained(pe, ("keysT", layer, g))
                n_q = 2 * PEER_HEADS
                for i in range(n_q + 1):
                    if i < n_q:
                        j = 4 + i % 2
                        w = wait_weights(pe, f"query{layer}", i // 4)
                        b = open_bank(pe, ("qT", layer, i), j)
                        for k in range(KC):
                            c0 = (i % 4) * P
                            mm = pe.matmul(b[:, 0:tiles * P], w[:, k, c0:c0 + P], ffn_inT[:, k, 0:tiles * P],
                                           start=(k == 0), stop=(k == KC - 1))
                        mm.then_inc(bank_filled[j], 1)
                        weights_done[f"query{layer}", i // 4] = turn["qT", layer, i]
                    if i >= 1:
                        m = i - 1
                        j = 6 + m % 2
                        wait_drained(pe, ("qT", layer, m))
                        b = open_bank(pe, ("sc", layer, m), j)
                        for t in range(tiles):
                            mm = pe.matmul(b[:, t * P:(t + 1) * P], queryT[:, m % 2, t * P:(t + 1) * P],
                                           keysT[:, m, :], start=True, stop=True)
                        mm.then_inc(bank_filled[j], 1)

            def combine(step, par):
                pe.wait_ge(y_free, step + 1)
                for k in range(TOPK):
                    pe.wait_ge(v_in[k % RING], step * 32 + 16 * (k // RING + 1))
                    pe.wait_ge(diag_ready, step * TOPK + (k + 1))
                    for half in range(2):
                        mm = pe.matmul(bank[2 * par + half][:, :], diag[:, k % DIAGS, :],
                                       v_rows[:, k % RING, half * WBLK:(half + 1) * WBLK],
                                       start=(k == 0), stop=(k == TOPK - 1))
                    mm.then_inc(v_free, 1)

            def experts(layer, tiles):
                if layer == 0:
                    pe.sem_inc(v_free, RING)
                with pe.Fori(0, tiles * PEER_HEADS // 2) as pair:
                    combine(pair * 2 + layer * GATHER_LAYER_STEPS, 0)
                    combine(pair * 2 + (layer * GATHER_LAYER_STEPS + 1), 1)

            def program():
                conditions()
                if end_stage("pe", pe):
                    return
                turn_rows("hT0", h, TILES, True)
                project("attn_in", hT, ATTN_IN, lambda n: range(TILES))
                if end_stage("pe", pe):
                    return
                attention()
                if end_stage("pe", pe):
                    return
                turn_rows("oT0", h, TILES, False)
                project("out0", hT, D, lambda n: range(TILES))
                if end_stage("pe", pe):
                    return
                turn_rows("fT0", ffn_in, TILES, True)
                query_scores(0, TILES)
                if end_stage("pe", pe):
                    return
                experts(0, TILES)
                if end_stage("pe", pe):
                    return
                turn_rows("hT1", h_gla, TILES, True)
                project("gla_in", gla_hT, GLA_IN, gla_tiles)
                if end_stage("pe", pe):
                    return
                gla()
                if end_stage("pe", pe):
                    return
                turn_rows("oT1", gla_o, LAT_TILES, False)
                project("out1", gla_hT, D, lambda n: range(LAT_TILES))
                if end_stage("pe", pe):
                    return
                turn_rows("fT1", ffn_in, LAT_TILES, True)
                query_scores(1, LAT_TILES)
                if end_stage("pe", pe):
                    return
                experts(1, LAT_TILES)
                end_stage("pe", pe)

            program()

        @block.sync
        def _(sp):
            for n, (name, b, src, cols) in enumerate(blocks):
                if (name, b) not in weights_done:
                    break
                if n >= WSLOTS:
                    j, m = weights_done[blocks[n - WSLOTS][0], blocks[n - WSLOTS][1]]
                    sp.wait_ge(bank_filled[j], m + 1)
                sp.dma_start(wring[:, n % WSLOTS, :, 0:cols], src).then_inc(w_loaded[n % WSLOTS], 16)

        @block.scalar
        def _(act):
            steps = Steps(act, act_step)
            count = Count()

            def conditions():
                wait_bank(act, "cond")
                act.activation(cond_tmp, bank[7][:, 0:2 * KC], ACT.Exp, scale=-1.0).then_inc(cond_exp_ready, 1)

            def sum_squares(srcs, junk, n):
                for i in range(n):
                    ins = act.activation(junk(i), srcs(i), ACT.Square, accum_out=stat[:, i:i + 1])
                ins.then_inc(sumsq_ready, 1)
                act.wait_ge(mean_ready, count.next("mean"))
                act.activation(stat[:, 16:16 + n], stat[:, 8:8 + n], ACT.Sqrt).then_inc(root_ready, 1)

            def turn_rows(name, dst, tiles):
                for t in range(tiles):
                    for half in range(2):
                        b = wait_bank(act, (name, t, half))
                        act.activation(dst[:, 4 * half:4 * half + 4, t * P:(t + 1) * P],
                                       bank[b][:, :].rearrange("p (k n) -> p k n", k=4),
                                       ACT.Copy).then_inc(bank_drained[b], 1)

            def attn_in():
                for n in range(ATTN_IN // WBLK):
                    for t in range(TILES):
                        b = wait_bank(act, ("attn_in", n, t))
                        act.activation(proj[:, t, n * WBLK:(n + 1) * WBLK], bank[b][:, :],
                                       ACT.Copy).then_inc(bank_drained[b], 1)

            def attention():
                act.wait_ge(mean_ready, count.next("mean"))
                act.activation(qk_stat[:, 2, :], qk_stat[:, 1, :], ACT.Sqrt).then_inc(root_ready, 1)
                for t in range(TILES):
                    for g in range(3):
                        b = wait_bank(act, ("qkT", t, g))
                        act.activation(qkT[:, 4 * g:4 * g + 4, t * P:(t + 1) * P],
                                       bank[b][:, :].rearrange("p (k n) -> p k n", k=4),
                                       ACT.Copy).then_inc(bank_drained[b], 1)
                for i in range(len(attn_steps) + 1):
                    if i < len(attn_steps):
                        t, hd = attn_steps[i]
                        nk = TILES if t < LAT_TILES else LAT_TILES
                        act.wait_ge(att_max, i + 1)
                        if i >= 2:
                            wait_bank(act, ("pT", i - 2))
                        b = turn["s", i][0]
                        ins = act.activation(probs[:, i % 2, 0:nk * P], bank[b][:, 0:nk * P], ACT.Exp,
                                             bias=att_stat[:, i % 4, 1:2], scale=ATTN_SCALE,
                                             accum_out=att_stat[:, i % 4, 2:3])
                        ins.then_inc(bank_drained[b], 1)
                        if hd < HEADS_A:
                            act.activation(att_stat[:, i % 4, 3:4], sinks[:, hd:hd + 1], ACT.Exp,
                                           bias=att_stat[:, i % 4, 1:2]).then_inc(sink_exp, 1)
                    if i >= 1:
                        m = i - 1
                        nk = TILES if attn_steps[m][0] < LAT_TILES else LAT_TILES
                        if m >= 2:
                            wait_bank(act, ("o", m - 2))
                        b = wait_bank(act, ("pT", m))
                        act.activation(probsT[:, m % 2, 0:nk * P], bank[b][:, 0:nk * P],
                                       ACT.Copy).then_inc(bank_drained[b], 1)

            def gla_in():
                for n in range(-(-GLA_IN // WBLK)):
                    for t in gla_tiles(n):
                        b = wait_bank(act, ("gla_in", n, t))
                        if n == 6:
                            dst, cols = gate_low[:, t, :], 2 * RANK
                        elif t < LAT_TILES:
                            dst, cols = gla_lat[:, t, n * WBLK:(n + 1) * WBLK], WBLK
                        else:
                            dst, cols = gla_ctx[:, t - LAT_TILES, (n - 1) * WBLK:n * WBLK], WBLK
                        act.activation(dst, bank[b][:, 0:cols], ACT.Copy).then_inc(bank_drained[b], 1)

            def gla():
                for d in range(2):
                    b = wait_bank(act, ("gateT", d))
                    act.activation(gate_lowT[0:RANK, d, :], bank[b][0:RANK, :], ACT.Copy).then_inc(bank_drained[b], 1)
                for d in range(2):
                    for t in range(TILES):
                        act.wait_ge(gate_z, count.next("z"))
                        steps.link(act.activation(gate_tmp[:, t % 2, :], gate_tmp[:, t % 2, :], ACT.Exp, scale=-1.0))
                        act.activation(gate_tmp[:, t % 2, :], gate_tmp[:, t % 2, :], ACT.Ln,
                                       bias=1.0).then_inc(gate_ln, 1)
                    for t in range(TILES):
                        if t < LAT_TILES:
                            b = wait_bank(act, ("b", d, t))
                            act.activation(q_dec[:, t, :], bank[b][:, :], ACT.Exp).then_inc(exp_ready, 1)
                            act.activation(k_inv[:, t, :], bank[b][:, :], ACT.Exp,
                                           scale=-1.0).then_inc(bank_drained[b], 1)
                        b = wait_bank(act, ("rest", d, t))
                        act.activation(k_end[:, t, :], bank[b][:, :], ACT.Exp).then_inc(bank_drained[b], 1)
                    b = wait_bank(act, ("end", d))
                    act.activation(decay_end.rearrange("p a b c -> p (a b c)"), bank[b][:, 0:32],
                                   ACT.Exp).then_inc(bank_drained[b], 1)
                    for t in range(LAT_TILES):
                        for which, dst in enumerate((q_decT, k_invT)):
                            b = wait_bank(act, ("qkdT", d, t, which))
                            act.activation(dst[:, :, t * P:(t + 1) * P],
                                           bank[b][:, :].rearrange("p (k n) -> p k n", k=4),
                                           ACT.Copy).then_inc(bank_drained[b], 1)
                act.wait_ge(out_ready, 1)
                sum_squares(lambda i: gla_o[:, i // GLA_HEADS, (i % GLA_HEADS) * DV:(i % GLA_HEADS + 1) * DV],
                            lambda i: silu_r[:, i // GLA_HEADS, (i % GLA_HEADS) * DV:(i % GLA_HEADS + 1) * DV],
                            len(gla_jobs))
                for t in range(LAT_TILES):
                    act.activation(silu_r[:, t, :], gla_lat[:, t, 2 * KD + VD:2 * KD + 2 * VD], ACT.Exp,
                                   scale=-1.0).then_inc(silu_exp, 1)

            def query_scores(layer, tiles):
                for g in range(4):
                    b = wait_bank(act, ("keysT", layer, g))
                    act.activation(keysT[:, 4 * g:4 * g + 4, :].rearrange("p a b -> p (a b)"), bank[b][:, :],
                                   ACT.Copy).then_inc(bank_drained[b], 1)
                for i in range(2 * PEER_HEADS):
                    if i >= 2:
                        wait_bank(act, ("sc", layer, i - 2))
                    b = wait_bank(act, ("qT", layer, i))
                    act.activation(queryT[:, i % 2, 0:tiles * P], bank[b][:, 0:tiles * P],
                                   ACT.Copy).then_inc(bank_drained[b], 1)

            def tile_of(step, most):
                if isinstance(step, int):
                    return bass.ds(step // PEER_HEADS, 1)
                return bass.ds(nc.s_assert_within(step >> 3, 0, most), 1)

            def experts(layer, tiles):
                n, base = tiles * PEER_HEADS, layer * GATHER_LAYER_STEPS

                def load_step(i, par, dots):
                    if dots is not None:
                        act.wait_ge(u_free, dots)
                    act.activation(tile_in[par], ffn_in[:, tile_of(i, tiles - 1), :].rearrange("p a b -> p (a b)"),
                                   ACT.Copy).then_inc(tile_in_ready, 1)
                    act.activation(head_scores[:, par, :],
                                   scores[:, bass.ds(i, 1), :].rearrange("p a b -> p (a b)"),
                                   ACT.Copy).then_inc(head_scores_ready, 1)

                def gate(g, par):
                    act.wait_ge(best_ready, g + 1)
                    act.activation(gate_num[:, par, :], best[:, par, :], ACT.Exp, bias=neg_best[:, par:par + 1],
                                   accum_out=gate_sum[:, par:par + 1]).then_inc(gate_num_ready, 1)

                def gelu(g, par):
                    act.wait_ge(u_free, (g + 1) * TOPK + RING)
                    act.activation(act_gelu[:, par, :], act_raw[:, par, :], ACT.Gelu).then_inc(gelu_ready, 1)

                def diags(g, par):
                    act.wait_ge(weight_ready, g + 1)
                    for k in range(TOPK):
                        act.wait_ge(v_free, g * TOPK + (k + 1 - DIAGS + RING))
                        act.activation(diag[:, k % DIAGS, :], ident, ACT.Copy,
                                       scale=pick_weight[:, par, k:k + 1]).then_inc(diag_ready, 1)

                def body(i, par, prev, nxt):
                    g = i + base
                    if nxt:
                        if isinstance(i, int) and i == 0:
                            load_step(1, 1, None)
                        else:
                            load_step(i + 1, 1 - par, g * TOPK + RING)
                    if prev:
                        gelu(g + (-1), 1 - par)
                        diags(g + (-1), 1 - par)
                    if nxt:
                        gate(g + 1, 1 - par)

                load_step(0, 0, None)
                gate(base, 0)
                body(0, 0, False, True)
                with act.Fori(0, n // 2 - 1) as pair:
                    body(pair * 2 + 1, 1, True, True)
                    body(pair * 2 + 2, 0, True, True)
                body(n - 1, 1, True, False)
                gelu(base + n - 1, 1)
                diags(base + n - 1, 1)

            def program():
                conditions()
                if end_stage("act", act):
                    return
                act.wait_ge(pool_loads, first_loads)
                sum_squares(lambda t: xs[:, t, :], lambda t: h[:, t, :], TILES)
                turn_rows("hT0", hT, TILES)
                attn_in()
                if end_stage("act", act):
                    return
                attention()
                if end_stage("act", act):
                    return
                turn_rows("oT0", hT, TILES)
                if end_stage("act", act):
                    return
                sum_squares(lambda t: xs[:, t, :], lambda t: ffn_in[:, t, :], TILES)
                turn_rows("fT0", ffn_inT, TILES)
                query_scores(0, TILES)
                if end_stage("act", act):
                    return
                experts(0, TILES)
                if end_stage("act", act):
                    return
                sum_squares(lambda t: xs[:, t, :], lambda t: h_gla[:, t, :], TILES)
                turn_rows("hT1", gla_hT, TILES)
                gla_in()
                if end_stage("act", act):
                    return
                gla()
                if end_stage("act", act):
                    return
                turn_rows("oT1", gla_hT, LAT_TILES)
                if end_stage("act", act):
                    return
                sum_squares(lambda t: xs[:, t, :], lambda t: ffn_in[:, t, :], LAT_TILES)
                turn_rows("fT1", ffn_inT, LAT_TILES)
                query_scores(1, LAT_TILES)
                if end_stage("act", act):
                    return
                experts(1, LAT_TILES)
                end_stage("act", act)
                sum_squares(lambda t: xs[:, t, :], lambda t: ffn_in[:, t, :], LAT_TILES)

            program()

        @block.gpsimd
        def _(pool):
            def load(dst, src):
                pool.dma_start(dst, src).then_inc(pool_loads, 16)

            def row(src, n, parts=P):
                return src.rearrange("(a n) -> a n", a=1).to_broadcast((parts, n))

            def modulation(layer, section, conds, gate):
                for cond in range(conds):
                    src = mod_dram[cond, layer, section:section + 2, :].rearrange("a b -> (a b)")
                    load(mod_rows[:, cond, :, :].rearrange("p a b -> p (a b)"), row(src, 2 * D))
                    load(gate_rows[:, cond, :], row(mod_dram[cond, layer, gate, :], D))

            def experts(layer, tiles):
                n, base = tiles * PEER_HEADS, layer * GATHER_LAYER_STEPS

                def gather_u(g, par, k):
                    pool.wait_ge(u_free, g * TOPK + (k + 1))
                    hold(pool)
                    pool.indirect_dma_start(u_rows[:, k % RING, :], None, expert_u,
                                            bass.IndirectOffsetOnAxis(idx_u[:, par, k:k + 1], 0)
                                            ).then_inc(u_in[k % RING], 16)

                def gather_v(g, par, k):
                    pool.wait_ge(v_free, g * TOPK + (k + 1))
                    hold(pool)
                    pool.indirect_dma_start(v_rows[:, k % RING, :], None, expert_v,
                                            bass.IndirectOffsetOnAxis(idx_v[:, par, k:k + 1], 0)
                                            ).then_inc(v_in[k % RING], 16)

                def body(g, par):
                    pool.wait_ge(idx_u_ready, g + 1)
                    pool.wait_ge(idx_v_ready, g)
                    for k in range(TOPK):
                        gather_u(g, par, k)
                        gather_v(g + (-1), 1 - par, k)

                pool.wait_ge(idx_u_ready, base + 1)
                for k in range(TOPK):
                    gather_u(base, 0, k)
                with pool.Fori(0, n // 2 - 1) as pair:
                    body(pair * 2 + (base + 1), 1)
                    body(pair * 2 + (base + 2), 0)
                body(base + n - 1, 1)
                pool.wait_ge(idx_v_ready, base + n)
                for k in range(TOPK):
                    gather_v(base + n - 1, 1, k)

            def program():
                load(cst[:, :], consts)
                load(cond_in[0:KC, :], c.rearrange("b (k p) -> (b k) p", p=P))
                load(cond_in[KC:2 * KC, :], c_ctx.rearrange("(k p) -> k p", p=P))
                load(ada_bias[0:2, :], row(ada_b.rearrange("l n -> (l n)"), LAYERS * MOD_DIM, 2))
                load(norm_gains[0:2, 0:2, :].rearrange("p a b -> p (a b)"),
                     row(norm_mix.rearrange("l n -> (l n)"), LAYERS * D, 2))
                load(norm_gains[0:2, 2:4, :].rearrange("p a b -> p (a b)"),
                     row(norm_ffn.rearrange("l n -> (l n)"), LAYERS * D, 2))
                load(xs[:, 0:LAT_TILES, :], x[0].rearrange("(t p) d -> p t d", p=P))
                load(xs[:, LAT_TILES, :], ctx[0, 0:P, :])
                pool.wait_ge(mods_ready, 1)
                pool.dma_start(mod_dram.rearrange("c l s d -> c (l s d)"), mods[0:2, :]).then_inc(stored, 16)
                pool.wait_ge(stored, 16)
                load(xs[:, TILES - 1, :], ctx[0, P:SEQ, :])
                modulation(0, 0, 2, 2)
                if end_stage("pool", pool):
                    return
                load(qk_gain[:, 0, :], row(attn_q_gain[0], HEAD_DIM))
                load(qk_gain[:, 1, :], row(attn_k_gain[0], HEAD_DIM))
                load(sinks, row(attn_sink[0], HEADS_A))
                for _ in range(3):
                    if end_stage("pool", pool):
                        return
                modulation(0, 3, 2, 5)
                load(keys, peer_keys[0].rearrange("h s n d -> n (h s) d"))
                if end_stage("pool", pool):
                    return
                experts(0, TILES)
                if end_stage("pool", pool):
                    return
                modulation(1, 0, 2, 2)
                if end_stage("pool", pool):
                    return
                load(gate_w[0:RANK, :, :], gla_gate_w[0].rearrange("d r n -> r d n"))
                load(gate_bias.rearrange("p a b -> p (a b)"), row(gla_gate_b[0].rearrange("d n -> (d n)"), 2 * KD))
                load(head_gain, row(gla_head_gain[0], DV))
                for _ in range(2):
                    if end_stage("pool", pool):
                        return
                modulation(1, 3, 1, 5)
                load(keys, peer_keys[1].rearrange("h s n d -> n (h s) d"))
                if end_stage("pool", pool):
                    return
                experts(1, LAT_TILES)
                end_stage("pool", pool)
                load(mod_rows[:, 0, 0, :], row(final_norm, D))
                pool.wait_ge(h_ready, final_rows)
                pool.dma_start(out[0].rearrange("(t p) d -> p t d", p=P), ffn_in[:, 0:LAT_TILES, :]).then_inc(stored, 16)
                pool.wait_ge(stored, 32)

            program()

        @block.vector
        def _(dve):
            steps = Steps(dve, dve_step)
            link = steps.link
            count = Count()

            def conditions():
                dve.wait_ge(cond_exp_ready, 1)
                link(dve.tensor_scalar_add(cond_tmp, cond_tmp, 1.0))
                link(dve.reciprocal(cond_tmp, cond_tmp))
                dve.tensor_tensor(cond_act, bank[7][:, 0:2 * KC], cond_tmp, ALU.mult).then_inc(cond_ready, 1)
                dve.wait_ge(cond_ready, 1)
                dve.sem_inc(bank_drained[7], 1)
                dve.wait_ge(pool_loads, cond_loads)
                for layer in range(LAYERS):
                    for n in range(MOD_DIM // WBLK):
                        b = wait_bank(dve, ("ada", layer, n))
                        c0 = layer * MOD_DIM + n * WBLK
                        dve.tensor_tensor(mods[0:2, c0:c0 + WBLK], bank[b][0:2, :], ada_bias[0:2, c0:c0 + WBLK],
                                          ALU.add).then_inc(bank_drained[b], 1)
                        wait_drained(dve, ("ada", layer, n))
                for layer in range(LAYERS):
                    for section, gains in ((1, 0), (4, 2)):
                        c0 = layer * MOD_DIM + section * D
                        link(dve.scalar_tensor_tensor(mods[0:2, c0:c0 + D], mods[0:2, c0:c0 + D], 1.0,
                                                      norm_gains[0:2, gains + layer, :], ALU.add, ALU.mult))
                dve.sem_inc(mods_ready, 1)

            def inverse_root(n, width):
                dve.wait_ge(sumsq_ready, count.next("sumsq"))
                dve.tensor_scalar(stat[:, 8:8 + n], stat[:, 0:n], 1.0 / width, EPS, ALU.mult,
                                  ALU.add).then_inc(mean_ready, 1)
                dve.wait_ge(root_ready, count.next("root"))
                link(dve.reciprocal(stat[:, 24:24 + n], stat[:, 16:16 + n]))

            def modulate(dst, tiles, loads):
                inverse_root(tiles, D)
                dve.wait_ge(pool_loads, loads)
                for t in range(tiles):
                    cond = t // LAT_TILES
                    link(dve.scalar_tensor_tensor(dst[:, t, :], xs[:, t, :], stat[:, 24 + t:25 + t],
                                                  mod_rows[:, cond, 1, :], ALU.mult, ALU.mult))
                    dve.tensor_tensor(dst[:, t, :], dst[:, t, :], mod_rows[:, cond, 0, :],
                                      ALU.add).then_inc(h_ready, 1)

            def rotate(rows, t):
                heads = rows.rearrange("p (h a s r) -> p (h a) s r", h=10, a=2, s=2)
                swap = swapped.rearrange("p (h a s r) -> p (h a) s r", h=10, a=2, s=2)
                for s in range(2):
                    ins = dve.tensor_copy(swap[:, :, s, :], heads[:, :, 1 - s, :])
                link(ins)
                w = HEAD_DIM
                cos = cst[:, C_COS + t * w:C_COS + (t + 1) * w].unsqueeze(1).to_broadcast([P, 10, w])
                sin = cst[:, C_SIN + t * w:C_SIN + (t + 1) * w].unsqueeze(1).to_broadcast([P, 10, w])
                by_head = rows.rearrange("p (h n) -> p h n", h=10)
                sw = swapped.rearrange("p (h n) -> p h n", h=10)
                dve.tensor_tensor(by_head, by_head, cos, ALU.mult)
                link(dve.tensor_tensor(sw, sw, sin, ALU.mult))
                link(dve.tensor_tensor(by_head, by_head, sw, ALU.add))

            def attention():
                dve.wait_ge(pool_loads, attn_loads)
                for t in range(TILES):
                    rows = proj[:, t, B_OFF:B_OFF + 640]
                    link(dve.tensor_tensor(turned, rows, rows, ALU.mult))
                    link(dve.tensor_reduce(qk_stat[:, 0, 10 * t:10 * t + 10], turned.rearrange("p (h n) -> p h n", h=10),
                                           AX_X, ALU.add))
                dve.tensor_scalar(qk_stat[:, 1, :], qk_stat[:, 0, :], 1.0 / HEAD_DIM, EPS, ALU.mult,
                                  ALU.add).then_inc(mean_ready, 1)
                dve.wait_ge(root_ready, count.next("root"))
                link(dve.reciprocal(qk_stat[:, 3, :], qk_stat[:, 2, :]))
                for t in range(TILES):
                    rows = proj[:, t, B_OFF:B_OFF + 640].rearrange("p (h n) -> p h n", h=10)
                    link(dve.tensor_tensor(rows, rows, qk_stat[:, 3, 10 * t:10 * t + 10].unsqueeze(2).to_broadcast(
                        [P, 10, HEAD_DIM]), ALU.mult))
                    dve.tensor_tensor(rows[:, 0:8, :], rows[:, 0:8, :],
                                      qk_gain[:, 0:1, :].to_broadcast([P, 8, HEAD_DIM]), ALU.mult)
                    link(dve.tensor_tensor(rows[:, 8:10, :], rows[:, 8:10, :],
                                           qk_gain[:, 1:2, :].to_broadcast([P, 2, HEAD_DIM]), ALU.mult))
                    if t < LAT_TILES:
                        rotate(proj[:, t, 0:640], t)
                        rotate(proj[:, t, B_OFF:B_OFF + 640], t)
                    if t >= 2:
                        wait_bank(dve, ("qkT", t - 2, 2))
                    for kind in range(2):
                        k0 = kind * B_OFF + 512
                        for kv in range(2):
                            src = proj[:, t, k0 + kv * HEAD_DIM:k0 + (kv + 1) * HEAD_DIM]
                            ins = dve.tensor_copy(kdup[:, t % 2, 2 * kind + kv, :].rearrange("p (a b) -> p a b", a=2),
                                                  src.unsqueeze(1).to_broadcast([P, 2, HEAD_DIM]))
                    ins.then_inc(qk_ready, 1)
                for i in range(len(attn_steps) + 2):
                    if i < len(attn_steps):
                        t, hd = attn_steps[i]
                        nk = TILES if t < LAT_TILES else LAT_TILES
                        st = att_stat[:, i % 4, :]
                        b = wait_bank(dve, ("s", i))
                        if hd < HEADS_A and t < LAT_TILES:
                            cols = bank[b][:, (1 - t) * P:(2 - t) * P]
                            link(dve.tensor_tensor(cols, cols, cst[:, C_BAND + t * P:C_BAND + (t + 1) * P], ALU.add))
                        link(dve.tensor_reduce(st[:, 0:1], bank[b][:, 0:nk * P], AX_X, ALU.max))
                        if hd < HEADS_A:
                            link(dve.tensor_scalar(st[:, 0:1], st[:, 0:1], ATTN_SCALE, sinks[:, hd:hd + 1], ALU.mult,
                                                   ALU.max))
                            dve.tensor_scalar(st[:, 1:2], st[:, 0:1], -1.0, None, ALU.mult).then_inc(att_max, 1)
                        else:
                            dve.tensor_scalar(st[:, 1:2], st[:, 0:1], -ATTN_SCALE, None, ALU.mult).then_inc(att_max, 1)
                    if i >= 2:
                        m = i - 2
                        t, hd = attn_steps[m]
                        st = att_stat[:, m % 4, :]
                        wait_drained(dve, ("s", m))
                        if hd < HEADS_A:
                            dve.wait_ge(sink_exp, count.next("sink"))
                            link(dve.tensor_tensor(st[:, 2:3], st[:, 2:3], st[:, 3:4], ALU.add))
                        link(dve.reciprocal(st[:, 2:3], st[:, 2:3]))
                        b = wait_bank(dve, ("o", m))
                        dve.tensor_scalar(h[:, t, hd * HEAD_DIM:(hd + 1) * HEAD_DIM], bank[b][:, 0:HEAD_DIM],
                                          st[:, 2:3], None, ALU.mult).then_inc(bank_drained[b], 1)

            def residual(name, tiles):
                for n in range(D // WBLK):
                    for t in range(tiles):
                        b = wait_bank(dve, (name, n, t))
                        cols = slice(n * WBLK, (n + 1) * WBLK)
                        link(dve.tensor_tensor(update[:, t % 2, :], bank[b][:, :],
                                               gate_rows[:, t // LAT_TILES, cols], ALU.mult))
                        dve.sem_inc(bank_drained[b], 1)
                        dve.tensor_tensor(xs[:, t, cols], xs[:, t, cols], update[:, t % 2, :], ALU.add)

            def gla():
                dve.wait_ge(pool_loads, gla_loads)
                ins = dve.memset(att_masked, 0.0)
                link(ins)
                for d in range(2):
                    for t in range(TILES + 1):
                        if t < TILES:
                            z = gate_tmp[:, t % 2, :]
                            b = wait_bank(dve, ("z", d, t))
                            dve.tensor_tensor(z, bank[b][:, :], gate_bias[:, d, :], ALU.add).then_inc(bank_drained[b], 1)
                            wait_drained(dve, ("z", d, t))
                            dve.tensor_scalar(log_decay[:, t, :], z, 0.0, 1.0 / GATE_NORM, ALU.min, ALU.mult)
                            link(dve.scalar_tensor_tensor(z, z, -1.0, z, ALU.mult, ALU.max))
                            dve.sem_inc(gate_z, 1)
                        if t >= 1:
                            m = t - 1
                            dve.wait_ge(gate_ln, count.next("ln"))
                            dve.scalar_tensor_tensor(log_decay[:, m, :], gate_tmp[:, m % 2, :], -1.0 / GATE_NORM,
                                                     log_decay[:, m, :], ALU.mult, ALU.add).then_inc(decay_ready, 1)
                            dve.wait_ge(decay_ready, TILES * d + t)
                    for t in range(TILES):
                        if t < LAT_TILES:
                            q, k = gla_lat[:, t, 0:KD], gla_lat[:, t, KD:2 * KD]
                            dve.wait_ge(exp_ready, count.next("exp"))
                            dve.scalar_tensor_tensor(q_dec[:, t, :], q, DK**-0.5, q_dec[:, t, :], ALU.mult, ALU.mult)
                            wait_drained(dve, ("b", d, t))
                            dve.tensor_tensor(k_inv[:, t, :], k_inv[:, t, :], k, ALU.mult)
                        else:
                            k = gla_ctx[:, t - LAT_TILES, 0:KD]
                        wait_drained(dve, ("rest", d, t))
                        dve.tensor_tensor(k_end[:, t, :], k_end[:, t, :], k, ALU.mult).then_inc(keyed_ready, 1)
                    wait_drained(dve, ("end", d))
                    done = {}
                    for n, (hh, kind, chunk, slot) in enumerate(gla_updates(d)):
                        b = wait_bank(dve, ("kv", d, n))
                        new = states[:, hh, slot, :]
                        if hh not in done:
                            ins = dve.tensor_copy(new, bank[b][:, 0:DV])
                        else:
                            tile = chunk // 2 + (LAT_TILES if kind == "ctx" else 0)
                            ins = dve.scalar_tensor_tensor(new, states[:, hh, done[hh], :],
                                                           decay_end[:, hh, tile, chunk % 2:chunk % 2 + 1],
                                                           bank[b][:, 0:DV], ALU.mult, ALU.add)
                        done[hh] = slot
                        ins.then_inc(state_ready, 1)
                        dve.wait_ge(state_ready, count.next("state"))
                        dve.sem_inc(bank_drained[b], 1)
                    mask = cst[:, (C_UPPER, C_LOWER)[d]:(C_UPPER, C_LOWER)[d] + P].bitcast(U32)
                    for i in range(len(gla_jobs) + 1):
                        if i < len(gla_jobs):
                            b = wait_bank(dve, ("att", d, i))
                            if i >= 2:
                                wait_bank(dve, ("go", d, i - 2))
                            dve.copy_predicated(att_masked[:, 2 * d + i % 2, :], mask,
                                                bank[b][:, 0:P]).then_inc(masked_ready, 1)
                            dve.wait_ge(masked_ready, count.next("masked"))
                            dve.sem_inc(bank_drained[b], 1)
                        if i >= 1:
                            m = i - 1
                            t, hh = gla_jobs[m]
                            o = gla_o[:, t, hh * DV:(hh + 1) * DV]
                            b = wait_bank(dve, ("go", d, m))
                            if d == 0:
                                ins = dve.tensor_copy(o, bank[b][:, 0:DV])
                            else:
                                ins = dve.tensor_tensor(o, bank[b][:, 0:DV], o, ALU.add)
                            ins.then_inc(bank_drained[b], 1)
                dve.drain().then_inc(out_ready, 1)
                inverse_root(len(gla_jobs), DV)
                for t in range(LAT_TILES):
                    dve.wait_ge(silu_exp, t + 1)
                    e = silu_r[:, t, :]
                    link(dve.tensor_scalar_add(e, e, 1.0))
                    link(dve.reciprocal(e, e))
                    link(dve.tensor_tensor(e, e, gla_lat[:, t, 2 * KD + VD:2 * KD + 2 * VD], ALU.mult))
                    for hh in range(GLA_HEADS):
                        o = gla_o[:, t, hh * DV:(hh + 1) * DV]
                        j = 24 + t * GLA_HEADS + hh
                        link(dve.scalar_tensor_tensor(o, o, stat[:, j:j + 1], head_gain, ALU.mult, ALU.mult))
                    dve.tensor_tensor(gla_o[:, t, :], gla_o[:, t, :], e, ALU.mult)

            def query_scores(layer, tiles):
                by_head = scores.rearrange("p (t h) n -> p t h n", t=TILES)
                for i in range(2 * PEER_HEADS):
                    b = wait_bank(dve, ("sc", layer, i))
                    dve.tensor_copy(by_head[:, 0:tiles, i // 2, (i % 2) * P:(i % 2 + 1) * P],
                                    bank[b][:, 0:tiles * P].rearrange("p (t n) -> p t n", t=tiles)
                                    ).then_inc(bank_drained[b], 1)

            def largest(values, at_u, src, rest):
                hold(dve)
                link(dve.max(values[:, 0:8], src))
                hold(dve)
                dve.max_index(at_u[:, 0:8], values[:, 0:8], src)
                link(dve.match_replace(rest, values[:, 0:8], src, LOWEST))
                hold(dve)
                link(dve.max(values[:, 8:16], rest))
                hold(dve)
                link(dve.max_index(at_u[:, 8:16], values[:, 8:16], rest))

            def route_half(g, par, half):
                if half == 0:
                    dve.wait_ge(head_scores_ready, g + 1)
                largest(top[:, half, :], top_at_u[:, half, :],
                        head_scores[:, par, half * N_KEYS:(half + 1) * N_KEYS], rest_scores[:, half, :])

            def route_sums():
                dve.tensor_tensor(sums.rearrange("p (a b) -> p a b", a=TOPK),
                                  top[:, 0, :].unsqueeze(2).to_broadcast([P, TOPK, TOPK]),
                                  top[:, 1:2, :].to_broadcast([P, TOPK, TOPK]), ALU.add)
                link(dve.tensor_copy(top_at, top_at_u))

            def route_best(g, par, layer):
                largest(best[:, par, :], best_at_u, sums, rest_sums)
                dve.tensor_scalar(neg_best[:, par:par + 1], best[:, par, 0:1], -1.0, None, ALU.mult).then_inc(best_ready, 1)
                link(dve.tensor_scalar(top_at[:, 0, :], top_at[:, 0, :], float(N_KEYS), float(layer * EXPERTS),
                                       ALU.mult, ALU.add))

            def route_experts(g, par):
                pair_u = best_pair_u.rearrange("p (k s) -> p k s", s=2)
                dve.tensor_scalar(pair_u[:, :, 0], best_at_u, 4, None, ALU.logical_shift_right)
                link(dve.tensor_scalar(pair_u[:, :, 1], best_at_u, 15, None, ALU.bitwise_and))
                link(dve.tensor_copy(best_pair, best_pair_u))
                hot = one_hot.rearrange("p (k s j) -> p k s j", k=TOPK, s=2)
                link(dve.tensor_tensor(one_hot.rearrange("p (k j) -> p k j", j=TOPK),
                                       best_pair.unsqueeze(2).to_broadcast([P, 2 * TOPK, TOPK]),
                                       cst[:, C_IOTA:C_IOTA + TOPK].unsqueeze(1).to_broadcast([P, 2 * TOPK, TOPK]),
                                       ALU.is_equal))
                link(dve.tensor_tensor(hot, hot, top_at.unsqueeze(1).to_broadcast([P, TOPK, 2, TOPK]), ALU.mult))
                link(dve.tensor_reduce(best_pair[:, 0:TOPK], one_hot.rearrange("p (k j) -> p k j", k=TOPK), AX_X,
                                       ALU.add))
                dve.tensor_copy(idx_u[:, par, :], best_pair[:, 0:TOPK]).then_inc(idx_u_ready, 1)

            def route_all(g, par, layer):
                route_half(g, par, 0)
                route_half(g, par, 1)
                route_sums()
                route_best(g, par, layer)
                route_experts(g, par)

            def weigh(g, par):
                dve.wait_ge(gate_num_ready, g + 1)
                link(dve.reciprocal(gate_sum[:, par:par + 1], gate_sum[:, par:par + 1]))
                dve.wait_ge(gelu_ready, g + 1)
                dve.scalar_tensor_tensor(pick_weight[:, par, :], act_gelu[:, par, :], gate_sum[:, par:par + 1],
                                         gate_num[:, par, :], ALU.mult, ALU.mult).then_inc(weight_ready, 1)

            def add_y(i, g, par, tiles):
                dve.wait_ge(v_free, g * TOPK + (TOPK + RING))
                if isinstance(i, int):
                    tile = bass.ds(i // PEER_HEADS, 1)
                    cond = bass.ds(i // (PEER_HEADS * LAT_TILES), 1)
                else:
                    tile = bass.ds(nc.s_assert_within(i >> 3, 0, tiles - 1), 1)
                    cond = bass.ds(nc.s_assert_within(i >> 4, 0, (tiles - 1) // LAT_TILES), 1)
                for half in range(2):
                    cols = slice(half * WBLK, (half + 1) * WBLK)
                    b = bank[2 * par + half]
                    link(dve.tensor_tensor(b[:, :], b[:, :], gate_rows[:, cond, cols].rearrange("p a b -> p (a b)"),
                                           ALU.mult))
                    rows = xs[:, tile, cols].rearrange("p a b -> p (a b)")
                    ins = dve.tensor_tensor(rows, rows, b[:, :], ALU.add)
                    if half == 0:
                        link(ins)
                ins.then_inc(y_free, 1)

            def body(i, base, par, layer, tiles, prev, done, nxt):
                g = i + base
                dve.wait_ge(tile_in_ready, g + 1)
                for k in range(TOPK):
                    dve.wait_ge(u_in[k % RING], g * 32 + 16 * (k // RING + 1))
                    dve.tensor_tensor_reduce(u_rows[:, k % RING, :], u_rows[:, k % RING, :], tile_in[par], 1.0, 0.0,
                                             ALU.mult, ALU.add, act_raw[:, par, k:k + 1]).then_inc(u_free, 1)
                    if k == 1 and prev:
                        weigh(g + (-1), 1 - par)
                    if k == 3 and nxt:
                        route_half(g + 1, 1 - par, 0)
                    if k == 5 and nxt:
                        route_half(g + 1, 1 - par, 1)
                    if k == 6 and done:
                        add_y(i + (-2), g + (-2), par, tiles)
                    if k == 7 and nxt:
                        route_sums()
                    if k == 9 and nxt:
                        route_best(g + 1, 1 - par, layer)
                    if k == 10:
                        if prev or layer:
                            dve.wait_ge(v_free, g * TOPK + (RING - TOPK))
                        dve.tensor_copy(idx_v[:, par, :], idx_u[:, par, :]).then_inc(idx_v_ready, 1)
                    if k == 12 and nxt:
                        route_experts(g + 1, 1 - par)

            LINKS = 23

            def experts(layer, tiles):
                n, base = tiles * PEER_HEADS, layer * GATHER_LAYER_STEPS
                if layer == 0:
                    dve.sem_inc(u_free, RING)
                    dve.sem_inc(y_free, 2)
                route_all(base, 0, layer)
                body(0, base, 0, layer, tiles, False, False, True)
                body(1, base, 1, layer, tiles, True, False, True)
                steps_before = steps.n
                steps.n = 0
                with dve.Fori(0, n // 2 - 2) as pair:
                    steps.base = pair * (2 * LINKS) + steps_before
                    body(pair * 2 + 2, base, 0, layer, tiles, True, True, True)
                    body(pair * 2 + 3, base, 1, layer, tiles, True, True, True)
                assert steps.n == 2 * LINKS, steps.n
                steps.base, steps.n = 0, steps_before + (n - 4) * LINKS
                body(n - 2, base, 0, layer, tiles, True, True, True)
                body(n - 1, base, 1, layer, tiles, True, True, False)
                weigh(base + n - 1, 1)
                add_y(n - 2, base + n - 2, 0, tiles)
                add_y(n - 1, base + n - 1, 1, tiles)

            def final():
                inverse_root(LAT_TILES, D)
                dve.wait_ge(pool_loads, final_loads)
                for t in range(LAT_TILES):
                    dve.scalar_tensor_tensor(ffn_in[:, t, :], xs[:, t, :], stat[:, 24 + t:25 + t],
                                             mod_rows[:, 0, 0, :], ALU.mult, ALU.mult).then_inc(h_ready, 1)

            def program():
                conditions()
                if end_stage("dve", dve):
                    return
                modulate(h, TILES, first_loads)
                if end_stage("dve", dve):
                    return
                attention()
                if end_stage("dve", dve):
                    return
                residual("out0", TILES)
                if end_stage("dve", dve):
                    return
                modulate(ffn_in, TILES, key_loads[0])
                query_scores(0, TILES)
                if end_stage("dve", dve):
                    return
                experts(0, TILES)
                if end_stage("dve", dve):
                    return
                modulate(h_gla, TILES, gla_loads - 48)
                if end_stage("dve", dve):
                    return
                gla()
                if end_stage("dve", dve):
                    return
                residual("out1", LAT_TILES)
                if end_stage("dve", dve):
                    return
                modulate(ffn_in, LAT_TILES, key_loads[1])
                query_scores(1, LAT_TILES)
                if end_stage("dve", dve):
                    return
                experts(1, LAT_TILES)
                end_stage("dve", dve)
                final()

            program()


_INS = ["x", "c", "ctx", "c_ctx", "ada_w", "ada_b", "norm_mix", "norm_ffn", "attn_w_in", "attn_sink",
        "attn_q_gain", "attn_k_gain", "attn_w_out", "gla_w_in", "gla_gate_w", "gla_gate_b", "gla_head_gain",
        "gla_w_out", "peer_wq", "peer_keys", "peer_u", "peer_v", "final_norm"]


def kernel(**inputs):
    import concourse.bacc as bacc
    from concourse.bass_utils import run_bass_kernel_spmd

    nc = bacc.Bacc("TRN2", target_bir_lowering=False, num_devices=1)
    arrays, args = {}, []
    for name in _INS:
        arrays[f"in_{name}"] = np.ascontiguousarray(inputs[name])
    arrays["in_consts"] = shape_constants()
    for name, a in arrays.items():
        args.append(nc.dram_tensor(name, a.shape, mybir.dt.from_np(a.dtype), kind="ExternalInput").ap())
    args.append(nc.dram_tensor("out", (1, SEQ, D), F32, kind="ExternalOutput").ap())
    build(nc, *args)
    r = run_bass_kernel_spmd(nc, [arrays], core_ids=[0])
    return r.results[0]["out"]
```

```python
from contextlib import ExitStack

import concourse.bass as bass
import numpy as np
from concourse import mybir

F32 = mybir.dt.float32
U32 = mybir.dt.uint32
ALU = mybir.AluOpType
ACT = mybir.ActivationFunctionType
AX_X = mybir.AxisListType.X

P = 128
D = 1024
KC = D // P
SEQ = 256
LAT_TILES = SEQ // P
TILES = 2 * LAT_TILES
WBLK = 512
EPS = 1e-6
LAYERS = 2
SECTIONS = 6
MOD_DIM = SECTIONS * D

HEAD_DIM = 64
GRID_W = 64
ROPE_PAIRS = HEAD_DIM // 4
HEADS_A = 8
ATTN_HEADS = 16
KV_GROUP = 4
ATTN_IN = 1536
ATTN_SCALE = HEAD_DIM**-0.5
B_OFF = 768
WINDOW = 128

GLA_HEADS = 4
DK = 128
DV = 256
KD = GLA_HEADS * DK
VD = GLA_HEADS * DV
RANK = 16
GATE_NORM = 16.0
CHUNK = 64
CHUNKS = SEQ // CHUNK
GLA_IN = 2 * KD + 2 * VD + 2 * RANK

PEER_HEADS = 8
N_KEYS = 128
EXPERTS = N_KEYS * N_KEYS
TOPK = 16
RING = 8
DIAGS = 4
LOWEST = -3.0e38

C_IDENT = 0
C_UPPER = 128
C_LOWER = 256
C_UPPER_STRICT = 384
C_LOWER_STRICT = 512
C_BAND = 640
C_COS = 896
C_SIN = 1024
C_IOTA = 1152
C_CHUNK = 1168
C_COLS = 1170


def shape_constants():
    c = np.zeros((P, C_COLS), np.float32)
    i = np.arange(P)
    same = (i[:, None] // CHUNK) == (i[None, :] // CHUNK)
    c[:, C_IDENT:C_IDENT + P] = np.eye(P)
    c[:, C_UPPER:C_UPPER + P] = same & (i[:, None] <= i[None, :])
    c[:, C_LOWER:C_LOWER + P] = same & (i[:, None] >= i[None, :])
    c[:, C_UPPER_STRICT:C_UPPER_STRICT + P] = same & (i[:, None] < i[None, :])
    c[:, C_LOWER_STRICT:C_LOWER_STRICT + P] = same & (i[:, None] > i[None, :])
    for t in range(LAT_TILES):
        query, key = t * P + i[:, None], (1 - t) * P + i[None, :]
        c[:, C_BAND + t * P:C_BAND + (t + 1) * P] = np.where(np.abs(query - key) <= WINDOW, 0.0, -1e30)
        tok = t * P + i
        pos = np.stack([tok // GRID_W, tok % GRID_W], -1).astype(np.float32)
        inv = (10000.0 ** (-np.arange(ROPE_PAIRS, dtype=np.float32) / ROPE_PAIRS)).astype(np.float32)
        ang = pos[:, :, None] * inv
        cos, sin = np.cos(ang), np.sin(ang)
        w = HEAD_DIM
        c[:, C_COS + t * w:C_COS + (t + 1) * w] = np.stack([cos, cos], 2).reshape(P, w)
        c[:, C_SIN + t * w:C_SIN + (t + 1) * w] = np.stack([-sin, sin], 2).reshape(P, w)
    c[:, C_IOTA:C_IOTA + TOPK] = np.arange(TOPK)
    c[:, C_CHUNK] = i < CHUNK
    c[:, C_CHUNK + 1] = i >= CHUNK
    return c


def build(nc, x, c, ctx, c_ctx, ada_w, ada_b, norm_mix, norm_ffn, attn_w_in, attn_sink, attn_q_gain,
          attn_k_gain, attn_w_out, gla_w_in, gla_gate_w, gla_gate_b, gla_head_gain, gla_w_out,
          peer_wq, peer_keys, peer_u, peer_v, final_norm, consts, out, stop=99):
    mod_dram = nc.dram_tensor("mod_dram", (2, LAYERS, SECTIONS, D), F32, kind="Internal").ap()
    expert_u = peer_u.rearrange("l e d -> (l e) d")
    expert_v = peer_v.rearrange("l e d -> (l e) d")

    blocks = []

    def stream(name, w, n):
        for b in range(-(-n // WBLK)):
            cols = min(WBLK, n - b * WBLK)
            blocks.append((name, b, w.rearrange("(k p) n -> p k n", p=P)[:, :, b * WBLK:b * WBLK + cols], cols))

    for layer in range(LAYERS):
        stream(f"ada{layer}", ada_w[layer], MOD_DIM)
    stream("attn_in", attn_w_in[0], ATTN_IN)
    stream("out0", attn_w_out[0], D)
    stream("gla_in", gla_w_in[0], GLA_IN)
    stream("out1", gla_w_out[0], D)
    block_at = {(name, b): n for n, (name, b, _, _) in enumerate(blocks)}
    WSLOTS = 3
    slot_of, load_no, slot_before = [], [], []
    n_ada = LAYERS * MOD_DIM // WBLK
    for n in range(len(blocks)):
        slot = n % WSLOTS if n < n_ada else (n - n_ada) % (WSLOTS - 1)
        same = [m for m in range(n) if slot_of[m] == slot]
        slot_of.append(slot)
        load_no.append(len(same))
        slot_before.append(same[-1] if same else None)

    with ExitStack() as es:
        def sb(name, shape, dt=F32):
            return es.enter_context(nc.sbuf_tensor(name, shape, dt))

        def sem(name):
            return es.enter_context(nc.semaphore(name))

        xs = sb("xs", [P, TILES, D])
        wring = sb("wring", [P, WSLOTS, KC, WBLK])
        mod_rows = sb("mod_rows", [P, 2, 2, D])
        gate_rows = sb("gate_rows", [P, 2, D])
        cst = sb("cst", [P, C_COLS])
        work = sb("work", [P, 28672])
        stat = sb("stat", [P, 32])
        diag = sb("diag", [P, DIAGS, P])
        picks_u = sb("picks_u", [P, 80], U32)
        idx_u = sb("idx_u", [P, 2, TOPK], U32)
        idx_v = sb("idx_v", [P, 2, TOPK], U32)
        query_w = wring[:, WSLOTS - 1, :, :].rearrange("p k (s n) -> p s k n", s=2)
        bank = [es.enter_context(nc.psum_tensor(f"bank{i}", [P, WBLK], F32)) for i in range(8)]

        def at(start, *dims):
            n = int(np.prod(dims))
            v = work[:, start:start + n]
            if len(dims) == 2:
                return v.rearrange("p (a b) -> p a b", a=dims[0])
            if len(dims) == 3:
                return v.rearrange("p (a b c) -> p a b c", a=dims[0], b=dims[1])
            return v

        ident = cst[:, C_IDENT:C_IDENT + P]

        mods = at(0, LAYERS * MOD_DIM)
        norm_gains = at(12288, 4, D)
        proj = at(0, TILES, ATTN_IN)
        qkT = at(6144, 12, TILES * P)
        hT = at(12288, KC, TILES * P)
        h = at(16384, TILES, D)
        kdup = at(20480, 2, 4, P)
        swapped = at(21504, 640)
        turned = at(22144, 640)
        probs = at(21504, 2, TILES * P)
        probsT = at(22784, 2, TILES * P)
        qk_gain = at(23808, 2, HEAD_DIM)
        sinks = at(23936, HEADS_A)
        update = at(9344, 2, WBLK)
        att_stat = at(25984, 4, 4)
        qk_stat = at(26000, 4, TILES * 10)
        cond_in = at(24576, P)
        cond_act = at(24704, 2 * KC)
        cond_tmp = at(24720, 2 * KC)
        hT0 = at(20480, KC, TILES * P)

        ffn_in = at(0, TILES, D)
        ffn_inT = at(4096, KC, TILES * P)
        keysT = at(8192, 2 * PEER_HEADS, P)
        query_rows = at(10240, 2, P)
        queryT = at(10496, 2, P)
        keys = at(12288, 2 * PEER_HEADS, P)
        u_rows = at(12288, RING, D)
        v_rows = at(20480, RING, D)
        route = mod_rows[:, 1, :, :].rearrange("p a b -> p (a b)")

        def route_at(start, *dims):
            n = int(np.prod(dims))
            v = route[:, start:start + n]
            return v.rearrange("p (a b) -> p a b", a=dims[0]) if len(dims) == 2 else v

        head_scores = route_at(0, 2, 2 * N_KEYS)
        best = route_at(512, 2, TOPK)
        sums = route_at(768, TOPK * TOPK)
        rest_sums = route_at(1024, TOPK * TOPK)
        one_hot = route_at(1280, 2 * TOPK * TOPK)
        rest_scores = route_at(1280, 2, N_KEYS)
        act_raw = route_at(1792, 2, TOPK)
        act_gelu = route_at(1824, 2, TOPK)
        gate_num = route_at(1856, 2, TOPK)
        pick_weight = route_at(1888, 2, TOPK)
        gate_sum = route_at(1920, 2)
        neg_best = route_at(1922, 2)
        top = route_at(1924, 2, TOPK)
        top_at = route_at(1956, 2, TOPK)
        best_pair = route_at(1988, 2 * TOPK)
        top_at_u = picks_u[:, 0:2 * TOPK].rearrange("p (a b) -> p a b", a=2)
        best_at_u = picks_u[:, 2 * TOPK:3 * TOPK]
        best_pair_u = picks_u[:, 3 * TOPK:5 * TOPK]

        gla_lat = at(0, LAT_TILES, 2 * KD + 2 * VD)
        gla_ctx = at(6144, LAT_TILES, KD + VD)
        gate_low = at(9216, TILES, 2 * RANK)
        log_decay = at(9344, TILES, KD)
        k_end = at(11392, TILES, KD)
        q_dec = at(13440, LAT_TILES, KD)
        k_inv = at(14464, LAT_TILES, KD)
        q_decT = at(15488, GLA_HEADS, SEQ)
        k_invT = at(16512, GLA_HEADS, SEQ)
        states = at(17536, GLA_HEADS, CHUNKS, DV)
        decay_end = at(21632, GLA_HEADS, TILES, 2)
        gla_o = at(21664, LAT_TILES, VD)
        att_masked = at(23712, 4, P)
        head_gain = at(24224, DV)
        gla_hT = at(24576, KC, TILES * P)
        h_gla = at(20480, TILES, D)
        gate_w = at(24576, 2, KD)
        gate_bias = at(25600, 2, KD)
        gate_lowT = at(26624, 2, TILES * P)
        gate_tmp = at(27648, 2, KD)
        silu_r = at(9344, LAT_TILES, VD)

        w_loaded = [sem(f"w_loaded{i}") for i in range(WSLOTS)]
        bank_filled = [sem(f"bank_filled{i}") for i in range(8)]
        bank_drained = [sem(f"bank_drained{i}") for i in range(8)]
        stage_over = sem("stage_over")
        dve_step = sem("dve_step")
        held = sem("held")
        act_step = sem("act_step")
        pool_loads = sem("pool_loads")
        stored = sem("stored")
        cond_in_ready = sem("cond_in_ready")
        cond_exp_ready = sem("cond_exp_ready")
        cond_ready = sem("cond_ready")
        mods_ready = sem("mods_ready")
        sumsq_ready = sem("sumsq_ready")
        mean_ready = sem("mean_ready")
        root_ready = sem("root_ready")
        h_ready = sem("h_ready")
        qk_ready = sem("qk_ready")
        att_max = sem("att_max")
        gate_z = sem("gate_z")
        gate_ln = sem("gate_ln")
        decay_ready = sem("decay_ready")
        exp_ready = sem("exp_ready")
        sink_exp = sem("sink_exp")
        decay_end_ready = sem("decay_end_ready")
        keyed_ready = sem("keyed_ready")
        state_ready = sem("state_ready")
        masked_ready = sem("masked_ready")
        silu_exp = sem("silu_exp")
        out_ready = sem("out_ready")

        u_in = [sem(f"u_in{i}") for i in range(RING)]
        v_in = [sem(f"v_in{i}") for i in range(RING)]
        u_free = sem("u_free")
        v_free = sem("v_free")
        y_free = sem("y_free")
        idx_u_ready = sem("idx_u_ready")
        idx_v_ready = sem("idx_v_ready")
        head_scores_ready = sem("head_scores_ready")
        query_loaded = sem("query_loaded")
        query_done = sem("query_done")
        query_rows_ready = sem("query_rows_ready")
        query_turned = sem("query_turned")
        queryT_ready = sem("queryT_ready")
        scores_done = sem("scores_done")
        best_ready = sem("best_ready")
        gate_num_ready = sem("gate_num_ready")
        gelu_ready = sem("gelu_ready")
        weight_ready = sem("weight_ready")
        diag_ready = sem("diag_ready")

        block = es.enter_context(nc.Block())

        class Count:

            def __init__(self):
                self.n = {}

            def next(self, name, more=1):
                self.n[name] = self.n.get(name, 0) + more
                return self.n[name]

        class Steps:

            def __init__(self, eng, done):
                self.eng, self.done, self.base, self.n = eng, done, 0, 0

            def link(self, ins):
                self.n += 1
                ins.then_inc(self.done, 1)
                self.eng.wait_ge(self.done, self.base + self.n)

        def hold(eng):
            eng.sem_inc(held, 1)

        stage_count = {}

        def end_stage(name, eng):
            n = stage_count[name] = stage_count.get(name, 0) + 1
            eng.drain().then_inc(stage_over, 1)
            eng.wait_ge(stage_over, 4 * n)
            return n >= stop

        uses = [0] * 8
        turn = {}
        weights_done = {}

        def open_bank(pe, key, b):
            n = uses[b]
            uses[b] += 1
            turn[key] = (b, n)
            if n:
                pe.wait_ge(bank_drained[b], n)
            return bank[b]

        def wait_bank(eng, key):
            b, n = turn[key]
            eng.wait_ge(bank_filled[b], n + 1)
            return b

        def wait_drained(eng, key):
            b, n = turn[key]
            eng.wait_ge(bank_drained[b], n + 1)

        def wait_weights(pe, name, b):
            n = block_at[name, b]
            pe.wait_ge(w_loaded[slot_of[n]], 16 * (load_no[n] + 1))
            return wring[:, slot_of[n], :, :]

        def last_four(name, tiles):
            return [(name, t, half) for t in range(tiles - 2, tiles) for half in range(2)]

        cond_loads = 16 * 5
        first_loads = cond_loads + 16 * 4
        attn_loads = first_loads + 16 * 3
        key_loads = [attn_loads + 16 * 5, 0]
        gla_loads = key_loads[0] + 16 * 7
        key_loads[1] = gla_loads + 16 * 3
        final_loads = key_loads[1] + 16
        final_rows = 3 * TILES + LAT_TILES + LAT_TILES

        attn_steps = [(t, hd) for t in range(TILES) for hd in range(ATTN_HEADS)]
        gla_jobs = [(t, hh) for t in range(LAT_TILES) for hh in range(GLA_HEADS)]
        GATHER_LAYER_STEPS = TILES * PEER_HEADS

        def gla_tiles(n):
            return range(TILES) if n in (1, 2, 3, 6) else range(LAT_TILES)

        def gla_updates(d):
            order = range(CHUNKS) if d == 0 else range(CHUNKS - 1, -1, -1)
            order = list(order)
            out = []
            for n in range(CHUNKS):
                out += [(hh, "ctx", order[n], order[0]) for hh in range(GLA_HEADS)]
            for n in range(CHUNKS - 1):
                out += [(hh, "lat", order[n], order[n + 1]) for hh in range(GLA_HEADS)]
            return out

        @block.tensor
        def _(pe):
            count = Count()

            def conditions():
                pe.wait_ge(cond_in_ready, 48)
                b = open_bank(pe, "cond", 7)
                pe.transpose(b[:, 0:2 * KC], cond_in[0:2 * KC, :], ident[0:2 * KC, 0:2 * KC]).then_inc(bank_filled[7], 1)
                pe.wait_ge(cond_ready, 1)
                cond = cond_act.rearrange("p (c k) -> p k c", c=2)
                for layer in range(LAYERS):
                    for n in range(MOD_DIM // WBLK):
                        w = wait_weights(pe, f"ada{layer}", n)
                        j = n % 4
                        b = open_bank(pe, ("ada", layer, n), j)
                        for k in range(KC):
                            mm = pe.matmul(b[0:2, :], cond[:, k, :], w[:, k, :], start=(k == 0), stop=(k == KC - 1))
                        mm.then_inc(bank_filled[j], 1)
                        weights_done[f"ada{layer}", n] = turn["ada", layer, n]

            def turn_rows(name, src, tiles, wait):
                for t in range(tiles):
                    if wait:
                        pe.wait_ge(h_ready, count.next("h"))
                    for half in range(2):
                        j = (2 * t + half) % 4
                        b = open_bank(pe, (name, t, half), j)
                        for k in range(4):
                            c0 = (4 * half + k) * P
                            mm = pe.transpose(b[:, k * P:(k + 1) * P], src[:, t, c0:c0 + P], ident)
                        mm.then_inc(bank_filled[j], 1)
                for key in last_four(name, tiles):
                    wait_drained(pe, key)

            def project(name, src, n_cols, tiles_of):
                step = 0
                for n in range(-(-n_cols // WBLK)):
                    cols = min(WBLK, n_cols - n * WBLK)
                    w = wait_weights(pe, name, n)
                    for t in tiles_of(n):
                        j = 4 + step % 2
                        step += 1
                        b = open_bank(pe, (name, n, t), j)
                        for k in range(KC):
                            mm = pe.matmul(b[:, 0:cols], src[:, k, t * P:(t + 1) * P], w[:, k, 0:cols],
                                           start=(k == 0), stop=(k == KC - 1))
                        mm.then_inc(bank_filled[j], 1)
                    weights_done[name, n] = turn[name, n, t]

            def attention():
                for t in range(TILES):
                    pe.wait_ge(qk_ready, t + 1)
                    for g in range(3):
                        j = (3 * t + g) % 4
                        b = open_bank(pe, ("qkT", t, g), j)
                        for k in range(4):
                            if g < 2:
                                c0 = g * B_OFF + k * P
                                src = proj[:, t, c0:c0 + P]
                            else:
                                src = kdup[:, t % 2, k, :]
                            mm = pe.transpose(b[:, k * P:(k + 1) * P], src, ident)
                        mm.then_inc(bank_filled[j], 1)
                for g in range(8, 3 * TILES):
                    wait_drained(pe, ("qkT", g // 3, g % 3))
                for i in range(len(attn_steps) + 2):
                    if i < len(attn_steps):
                        t, hd = attn_steps[i]
                        kind, hh = divmod(hd, HEADS_A)
                        rows = slice(HEAD_DIM * (hh % 2), HEAD_DIM * (hh % 2) + HEAD_DIM)
                        k0 = 0 if t < LAT_TILES else SEQ
                        j = i % 2
                        b = open_bank(pe, ("s", i), j)
                        pe.matmul(b[:, 0:TILES * P - k0], qkT[rows, kind * 4 + hh // 2, t * P:(t + 1) * P],
                                  qkT[rows, 8 + kind * 2 + hh // KV_GROUP, k0:TILES * P],
                                  start=True, stop=True).then_inc(bank_filled[j], 1)
                    if 1 <= i <= len(attn_steps):
                        m = i - 1
                        nk = TILES if attn_steps[m][0] < LAT_TILES else LAT_TILES
                        j = 2 + m % 2
                        b = open_bank(pe, ("pT", m), j)
                        wait_drained(pe, ("s", m))
                        for k in range(nk):
                            mm = pe.transpose(b[:, k * P:(k + 1) * P], probs[:, m % 2, k * P:(k + 1) * P], ident)
                        mm.then_inc(bank_filled[j], 1)
                    if i >= 2:
                        m = i - 2
                        t, hd = attn_steps[m]
                        kind, hh = divmod(hd, HEADS_A)
                        nk = TILES if t < LAT_TILES else LAT_TILES
                        vcol = kind * B_OFF + 640 + (hh // KV_GROUP) * HEAD_DIM
                        j = 4 + m % 2
                        b = open_bank(pe, ("o", m), j)
                        wait_drained(pe, ("pT", m))
                        for k in range(nk):
                            mm = pe.matmul(b[:, 0:HEAD_DIM], probsT[:, m % 2, k * P:(k + 1) * P],
                                           proj[:, TILES - nk + k, vcol:vcol + HEAD_DIM],
                                           start=(k == 0), stop=(k == nk - 1))
                        mm.then_inc(bank_filled[j], 1)

            def gla():
                pe.wait_ge(pool_loads, gla_loads)
                for d in range(2):
                    b = open_bank(pe, ("gateT", d), d)
                    for t in range(TILES):
                        mm = pe.transpose(b[0:RANK, t * P:(t + 1) * P], gate_low[:, t, d * RANK:(d + 1) * RANK], ident)
                    mm.then_inc(bank_filled[d], 1)
                for d in range(2):
                    wait_drained(pe, ("gateT", d))
                for d in range(2):
                    c_incl, c_rest = (C_UPPER, C_LOWER)[d], (C_LOWER_STRICT, C_UPPER_STRICT)[d]
                    for t in range(TILES):
                        j = t % 2
                        b = open_bank(pe, ("z", d, t), j)
                        pe.matmul(b[:, :], gate_lowT[0:RANK, d, t * P:(t + 1) * P], gate_w[0:RANK, d, :],
                                  start=True, stop=True).then_inc(bank_filled[j], 1)
                    for t in range(TILES):
                        pe.wait_ge(decay_ready, count.next("decay"))
                        if t < LAT_TILES:
                            b = open_bank(pe, ("b", d, t), 2)
                            pe.matmul(b[:, :], cst[:, c_incl:c_incl + P], log_decay[:, t, :],
                                      start=True, stop=True).then_inc(bank_filled[2], 1)
                        b = open_bank(pe, ("rest", d, t), 3)
                        pe.matmul(b[:, :], cst[:, c_rest:c_rest + P], log_decay[:, t, :],
                                  start=True, stop=True).then_inc(bank_filled[3], 1)
                    b = open_bank(pe, ("end", d), 4)
                    for hh in range(GLA_HEADS):
                        for t in range(TILES):
                            c0 = (hh * TILES + t) * 2
                            mm = pe.matmul(b[:, c0:c0 + 2], log_decay[:, t, hh * DK:(hh + 1) * DK],
                                           cst[:, C_CHUNK:C_CHUNK + 2], start=True, stop=True)
                    mm.then_inc(bank_filled[4], 1)
                    pe.wait_ge(keyed_ready, count.next("keyed", TILES))
                    for t in range(LAT_TILES):
                        for which, src in enumerate((q_dec, k_inv)):
                            j = 5 + which
                            b = open_bank(pe, ("qkdT", d, t, which), j)
                            for hh in range(GLA_HEADS):
                                mm = pe.transpose(b[:, hh * P:(hh + 1) * P], src[:, t, hh * DK:(hh + 1) * DK], ident)
                            mm.then_inc(bank_filled[j], 1)
                    for n, (hh, kind, chunk, _) in enumerate(gla_updates(d)):
                        t, r = divmod(chunk, 2)
                        rows = slice(CHUNK * r, CHUNK * r + CHUNK)
                        j = n % 2
                        b = open_bank(pe, ("kv", d, n), j)
                        if kind == "ctx":
                            v = gla_ctx[rows, t, KD + hh * DV:KD + (hh + 1) * DV]
                            t += LAT_TILES
                        else:
                            v = gla_lat[rows, t, 2 * KD + hh * DV:2 * KD + (hh + 1) * DV]
                        pe.matmul(b[:, 0:DV], k_end[rows, t, hh * DK:(hh + 1) * DK], v,
                                  start=True, stop=True).then_inc(bank_filled[j], 1)
                    for which in range(2):
                        wait_drained(pe, ("qkdT", d, LAT_TILES - 1, which))
                    pe.wait_ge(state_ready, count.next("state", len(gla_updates(d))))
                    for i in range(len(gla_jobs) + 1):
                        if i < len(gla_jobs):
                            t, hh = gla_jobs[i]
                            j = 2 + i % 2
                            b = open_bank(pe, ("att", d, i), j)
                            cols = slice(t * P, (t + 1) * P)
                            pe.matmul(b[:, 0:P], k_invT[:, hh, cols], q_decT[:, hh, cols],
                                      start=True, stop=True).then_inc(bank_filled[j], 1)
                        if i >= 1:
                            m = i - 1
                            t, hh = gla_jobs[m]
                            j = 4 + m % 2
                            b = open_bank(pe, ("go", d, m), j)
                            pe.wait_ge(masked_ready, count.next("masked"))
                            pe.matmul(b[:, 0:DV], att_masked[:, 2 * d + m % 2, :],
                                      gla_lat[:, t, 2 * KD + hh * DV:2 * KD + (hh + 1) * DV],
                                      start=True, stop=False, skip_group_check=True)
                            for r in range(2):
                                c0 = t * P + r * CHUNK
                                mm = pe.matmul(b[r * CHUNK:(r + 1) * CHUNK, 0:DV], q_decT[:, hh, c0:c0 + CHUNK],
                                               states[:, hh, 2 * t + r, :], start=False, stop=True,
                                               skip_group_check=True)
                            mm.then_inc(bank_filled[j], 1)

            def turn_keys(layer):
                pe.wait_ge(pool_loads, key_loads[layer])
                for g in range(4):
                    b = open_bank(pe, ("keysT", layer, g), g)
                    for k in range(4):
                        mm = pe.transpose(b[:, k * P:(k + 1) * P], keys[:, 4 * g + k, :], ident)
                    mm.then_inc(bank_filled[g], 1)
                for g in range(4):
                    wait_drained(pe, ("keysT", layer, g))

            def wait_query(head, layer):
                pe.wait_ge(query_loaded, head * 16 + (layer * PEER_HEADS + 1) * 16)

            def query_product(step, tile, slot):
                if not (isinstance(step, int) and step == 0):
                    pe.wait_ge(query_rows_ready, step)
                for k in range(KC):
                    w = query_w[:, slot, k, :]
                    mm = pe.matmul(bank[4][:, 0:2 * P], ffn_inT[:, k, tile * P:(tile + 1) * P],
                                   w if isinstance(slot, int) else w.rearrange("p a n -> p (a n)"),
                                   start=(k == 0), stop=(k == KC - 1))
                mm.then_inc(query_done, 1)

            def combine_start(g):
                pe.wait_ge(y_free, g)

            def combine(step, par, k):
                pe.wait_ge(v_in[k % RING], step * 32 + 16 * (k // RING + 1))
                pe.wait_ge(diag_ready, step * TOPK + (k + 1))
                for half in range(2):
                    mm = pe.matmul(bank[2 * par + half][:, :], diag[:, k % DIAGS, :],
                                   v_rows[:, k % RING, half * WBLK:(half + 1) * WBLK],
                                   start=(k == 0), stop=(k == TOPK - 1), skip_group_check=True)
                mm.then_inc(v_free, 1)

            def query_turn(step):
                pe.wait_ge(query_rows_ready, step + 1)
                for half in range(2):
                    mm = pe.transpose(bank[5][:, half * P:(half + 1) * P], query_rows[:, half, :], ident)
                mm.then_inc(query_turned, 1)

            def query_scores(step, head, par):
                pe.wait_ge(queryT_ready, step + 1)
                if not (isinstance(step, int) and step < 2):
                    pe.wait_ge(head_scores_ready, step + (-1))
                for half in range(2):
                    mm = pe.matmul(bank[6 + par][:, half * P:(half + 1) * P], queryT[:, half, :],
                                   keysT[:, bass.ds(head * 2 + half, 1), :].rearrange("p a b -> p (a b)"),
                                   start=True, stop=True)
                mm.then_inc(scores_done, 1)

            def experts(layer, tiles):
                base = layer * GATHER_LAYER_STEPS
                last = PEER_HEADS - 1

                def body(head, hpar, t, prev, nxt):
                    g = head * tiles + (base + t)
                    j, jt = g + 2, (t + 2) % tiles
                    carry = (t + 2) // tiles
                    jhead = head + carry
                    slot = jhead % 2 if isinstance(head, int) else bass.ds(jhead & 1, 1)
                    if prev:
                        combine_start(g)
                        for k in range(0, 4):
                            combine(g + (-1), 1 - t % 2, k)
                    if nxt:
                        if jt == 0:
                            wait_query(jhead, layer)
                        query_product(j, jt, slot)
                    if prev:
                        for k in range(4, 9):
                            combine(g + (-1), 1 - t % 2, k)
                    if nxt:
                        query_turn(j)
                    if prev:
                        for k in range(9, 14):
                            combine(g + (-1), 1 - t % 2, k)
                    if nxt:
                        query_scores(j, jhead, t % 2)
                    if prev:
                        for k in range(14, TOPK):
                            combine(g + (-1), 1 - t % 2, k)

                if layer == 0:
                    pe.sem_inc(v_free, RING)
                for t in range(2):
                    if t == 0:
                        wait_query(0, layer)
                    query_product(base + t, t, 0)
                    query_turn(base + t)
                    query_scores(base + t, 0, t)
                for t in range(tiles):
                    body(0, 0, t, t > 0, True)
                with pe.Fori(1, last) as head:
                    for t in range(tiles):
                        body(head, None, t, True, True)
                for t in range(tiles):
                    body(last, 1, t, True, t + 2 < tiles)
                g = base + tiles * PEER_HEADS
                combine_start(g)
                for k in range(TOPK):
                    combine(g - 1, 1, k)

            def program():
                conditions()
                turn_rows("hT0", h, TILES, True)
                project("attn_in", hT0, ATTN_IN, lambda n: range(TILES))
                if end_stage("pe", pe):
                    return
                attention()
                if end_stage("pe", pe):
                    return
                turn_rows("oT0", h, TILES, False)
                project("out0", hT, D, lambda n: range(TILES))
                if end_stage("pe", pe):
                    return
                turn_rows("fT0", ffn_in, TILES, True)
                turn_keys(0)
                if end_stage("pe", pe):
                    return
                experts(0, TILES)
                if end_stage("pe", pe):
                    return
                turn_rows("hT1", h_gla, TILES, True)
                project("gla_in", gla_hT, GLA_IN, gla_tiles)
                if end_stage("pe", pe):
                    return
                gla()
                if end_stage("pe", pe):
                    return
                turn_rows("oT1", gla_o, LAT_TILES, False)
                project("out1", gla_hT, D, lambda n: range(LAT_TILES))
                if end_stage("pe", pe):
                    return
                turn_rows("fT1", ffn_in, LAT_TILES, True)
                turn_keys(1)
                if end_stage("pe", pe):
                    return
                experts(1, LAT_TILES)
                end_stage("pe", pe)

            program()

        @block.sync
        def _(sp):
            sp.dma_start(cst[:, :], consts).then_inc(cond_in_ready, 16)
            sp.dma_start(cond_in[0:KC, :], c.rearrange("b (k p) -> (b k) p", p=P)).then_inc(cond_in_ready, 16)
            sp.dma_start(cond_in[KC:2 * KC, :], c_ctx.rearrange("(k p) -> k p", p=P)).then_inc(cond_in_ready, 16)

            def load_query(layer, tiles, head, slot):
                src = peer_wq[layer].rearrange("(k p) n -> p k n", p=P)[:, :, bass.ds(head * 2 * P, 2 * P)]
                sp.wait_ge(query_loaded, head * 16 + layer * PEER_HEADS * 16)
                sp.dma_start(query_w[:, slot, :, :], src).then_inc(query_loaded, 16)

            def queries(layer, tiles):
                base = layer * GATHER_LAYER_STEPS
                if layer == 0:
                    j, m = weights_done[blocks[n_ada - 1][0], blocks[n_ada - 1][1]]
                    sp.wait_ge(bank_filled[j], m + 1)
                for head in range(2):
                    src = peer_wq[layer].rearrange("(k p) n -> p k n", p=P)[:, :, head * 2 * P:(head + 1) * 2 * P]
                    if layer + head:
                        sp.wait_ge(query_loaded, 16 * (layer * PEER_HEADS + head))
                    if layer:
                        sp.wait_ge(query_done, base)
                    sp.dma_start(query_w[:, head, :, :], src).then_inc(query_loaded, 16)
                with sp.Fori(1, PEER_HEADS // 2) as pair:
                    for slot in range(2):
                        sp.wait_ge(query_done, pair * (2 * tiles) + (base + (slot - 1) * tiles))
                        load_query(layer, tiles, pair * 2 + slot, slot)

            for n, (name, b, src, cols) in enumerate(blocks):
                if (name, b) not in weights_done:
                    break
                before = slot_before[n]
                if before is not None:
                    j, m = weights_done[blocks[before][0], blocks[before][1]]
                    sp.wait_ge(bank_filled[j], m + 1)
                sp.dma_start(wring[:, slot_of[n], :, 0:cols], src).then_inc(w_loaded[slot_of[n]], 16)
                if (name, b) == ("out0", 1) and stop >= 5:
                    queries(0, TILES)
                if (name, b) == ("out1", 1) and stop >= 10:
                    queries(1, LAT_TILES)

        @block.scalar
        def _(act):
            steps = Steps(act, act_step)
            count = Count()

            def conditions():
                wait_bank(act, "cond")
                act.activation(cond_tmp, bank[7][:, 0:2 * KC], ACT.Exp, scale=-1.0).then_inc(cond_exp_ready, 1)

            def sum_squares(srcs, junk, n):
                for i in range(n):
                    ins = act.activation(junk(i), srcs(i), ACT.Square, accum_out=stat[:, i:i + 1])
                ins.then_inc(sumsq_ready, 1)
                act.wait_ge(mean_ready, count.next("mean"))
                act.activation(stat[:, 16:16 + n], stat[:, 8:8 + n], ACT.Sqrt).then_inc(root_ready, 1)

            def turn_rows(name, dst, tiles):
                for t in range(tiles):
                    for half in range(2):
                        b = wait_bank(act, (name, t, half))
                        act.activation(dst[:, 4 * half:4 * half + 4, t * P:(t + 1) * P],
                                       bank[b][:, :].rearrange("p (k n) -> p k n", k=4),
                                       ACT.Copy).then_inc(bank_drained[b], 1)

            def attn_in():
                for n in range(ATTN_IN // WBLK):
                    for t in range(TILES):
                        b = wait_bank(act, ("attn_in", n, t))
                        act.activation(proj[:, t, n * WBLK:(n + 1) * WBLK], bank[b][:, :],
                                       ACT.Copy).then_inc(bank_drained[b], 1)

            def attention():
                act.wait_ge(mean_ready, count.next("mean"))
                act.activation(qk_stat[:, 2, :], qk_stat[:, 1, :], ACT.Sqrt).then_inc(root_ready, 1)
                for t in range(TILES):
                    for g in range(3):
                        b = wait_bank(act, ("qkT", t, g))
                        act.activation(qkT[:, 4 * g:4 * g + 4, t * P:(t + 1) * P],
                                       bank[b][:, :].rearrange("p (k n) -> p k n", k=4),
                                       ACT.Copy).then_inc(bank_drained[b], 1)
                for i in range(len(attn_steps) + 1):
                    if i < len(attn_steps):
                        t, hd = attn_steps[i]
                        nk = TILES if t < LAT_TILES else LAT_TILES
                        act.wait_ge(att_max, i + 1)
                        if i >= 2:
                            wait_bank(act, ("pT", i - 2))
                        b = turn["s", i][0]
                        ins = act.activation(probs[:, i % 2, 0:nk * P], bank[b][:, 0:nk * P], ACT.Exp,
                                             bias=att_stat[:, i % 4, 1:2], scale=ATTN_SCALE,
                                             accum_out=att_stat[:, i % 4, 2:3])
                        ins.then_inc(bank_drained[b], 1)
                        if hd < HEADS_A:
                            act.activation(att_stat[:, i % 4, 3:4], sinks[:, hd:hd + 1], ACT.Exp,
                                           bias=att_stat[:, i % 4, 1:2]).then_inc(sink_exp, 1)
                    if i >= 1:
                        m = i - 1
                        nk = TILES if attn_steps[m][0] < LAT_TILES else LAT_TILES
                        if m >= 2:
                            wait_bank(act, ("o", m - 2))
                        b = wait_bank(act, ("pT", m))
                        act.activation(probsT[:, m % 2, 0:nk * P], bank[b][:, 0:nk * P],
                                       ACT.Copy).then_inc(bank_drained[b], 1)

            def gla_in():
                for n in range(-(-GLA_IN // WBLK)):
                    for t in gla_tiles(n):
                        b = wait_bank(act, ("gla_in", n, t))
                        if n == 6:
                            dst, cols = gate_low[:, t, :], 2 * RANK
                        elif t < LAT_TILES:
                            dst, cols = gla_lat[:, t, n * WBLK:(n + 1) * WBLK], WBLK
                        else:
                            dst, cols = gla_ctx[:, t - LAT_TILES, (n - 1) * WBLK:n * WBLK], WBLK
                        act.activation(dst, bank[b][:, 0:cols], ACT.Copy).then_inc(bank_drained[b], 1)

            def gla():
                for d in range(2):
                    b = wait_bank(act, ("gateT", d))
                    act.activation(gate_lowT[0:RANK, d, :], bank[b][0:RANK, :], ACT.Copy).then_inc(bank_drained[b], 1)
                for d in range(2):
                    for t in range(TILES):
                        act.wait_ge(gate_z, count.next("z"))
                        steps.link(act.activation(gate_tmp[:, t % 2, :], gate_tmp[:, t % 2, :], ACT.Exp, scale=-1.0))
                        act.activation(gate_tmp[:, t % 2, :], gate_tmp[:, t % 2, :], ACT.Ln,
                                       bias=1.0).then_inc(gate_ln, 1)
                    for t in range(TILES):
                        if t < LAT_TILES:
                            b = wait_bank(act, ("b", d, t))
                            act.activation(q_dec[:, t, :], bank[b][:, :], ACT.Exp).then_inc(exp_ready, 1)
                            act.activation(k_inv[:, t, :], bank[b][:, :], ACT.Exp,
                                           scale=-1.0).then_inc(bank_drained[b], 1)
                        b = wait_bank(act, ("rest", d, t))
                        act.activation(k_end[:, t, :], bank[b][:, :], ACT.Exp).then_inc(bank_drained[b], 1)
                    b = wait_bank(act, ("end", d))
                    act.activation(decay_end.rearrange("p a b c -> p (a b c)"), bank[b][:, 0:32],
                                   ACT.Exp).then_inc(bank_drained[b], 1)
                    for t in range(LAT_TILES):
                        for which, dst in enumerate((q_decT, k_invT)):
                            b = wait_bank(act, ("qkdT", d, t, which))
                            act.activation(dst[:, :, t * P:(t + 1) * P],
                                           bank[b][:, :].rearrange("p (k n) -> p k n", k=4),
                                           ACT.Copy).then_inc(bank_drained[b], 1)
                act.wait_ge(out_ready, 1)
                sum_squares(lambda i: gla_o[:, i // GLA_HEADS, (i % GLA_HEADS) * DV:(i % GLA_HEADS + 1) * DV],
                            lambda i: silu_r[:, i // GLA_HEADS, (i % GLA_HEADS) * DV:(i % GLA_HEADS + 1) * DV],
                            len(gla_jobs))
                for t in range(LAT_TILES):
                    act.activation(silu_r[:, t, :], gla_lat[:, t, 2 * KD + VD:2 * KD + 2 * VD], ACT.Exp,
                                   scale=-1.0).then_inc(silu_exp, 1)

            def turn_keys(layer):
                for g in range(4):
                    b = wait_bank(act, ("keysT", layer, g))
                    act.activation(keysT[:, 4 * g:4 * g + 4, :].rearrange("p a b -> p (a b)"), bank[b][:, :],
                                   ACT.Copy).then_inc(bank_drained[b], 1)

            def experts(layer, tiles):
                base = layer * GATHER_LAYER_STEPS
                last = PEER_HEADS - 1

                def copy_query(j):
                    act.wait_ge(query_done, j + 1)
                    act.activation(query_rows.rearrange("p a b -> p (a b)"), bank[4][:, 0:2 * P],
                                   ACT.Copy).then_inc(query_rows_ready, 1)

                def copy_queryT(j):
                    act.wait_ge(query_turned, j + 1)
                    act.activation(queryT.rearrange("p a b -> p (a b)"), bank[5][:, 0:2 * P],
                                   ACT.Copy).then_inc(queryT_ready, 1)

                def copy_scores(j, par, first):
                    act.wait_ge(scores_done, j + 1)
                    if not first:
                        act.wait_ge(idx_u_ready, j + (-1))
                    act.activation(head_scores[:, par, :], bank[6 + par][:, 0:2 * P],
                                   ACT.Copy).then_inc(head_scores_ready, 1)

                def gate(g, par):
                    act.wait_ge(best_ready, g + 1)
                    act.activation(gate_num[:, par, :], best[:, par, :], ACT.Exp, bias=neg_best[:, par:par + 1],
                                   accum_out=gate_sum[:, par:par + 1]).then_inc(gate_num_ready, 1)

                def gelu(g, par):
                    act.wait_ge(u_free, (g + 1) * TOPK + RING)
                    act.activation(act_gelu[:, par, :], act_raw[:, par, :], ACT.Gelu).then_inc(gelu_ready, 1)

                def diags(g, par, first, end):
                    for k in range(first, end):
                        act.wait_ge(v_free, g * TOPK + (k + 1 - DIAGS + RING))
                        act.activation(diag[:, k % DIAGS, :], ident, ACT.Copy,
                                       scale=pick_weight[:, par, k:k + 1]).then_inc(diag_ready, 1)

                def body(head, t, prev, nxt, query):
                    g, par = head * tiles + (base + t), t % 2
                    if nxt:
                        copy_scores(g + 1, 1 - par, isinstance(head, int) and base + head * tiles + t == 0)
                    if prev:
                        gelu(g + (-1), 1 - par)
                        act.wait_ge(weight_ready, g)
                        diags(g + (-1), 1 - par, 0, 7)
                    if query:
                        copy_query(g + 2)
                    if prev:
                        diags(g + (-1), 1 - par, 7, 12)
                    if query:
                        copy_queryT(g + 2)
                    if prev:
                        diags(g + (-1), 1 - par, 12, TOPK)
                    if nxt:
                        gate(g + 1, 1 - par)

                for t in range(2):
                    copy_query(base + t)
                    copy_queryT(base + t)
                    if t == 0:
                        copy_scores(base, 0, base == 0)
                gate(base, 0)
                for t in range(tiles):
                    body(0, t, t > 0, True, True)
                with act.Fori(1, last) as head:
                    for t in range(tiles):
                        body(head, t, True, True, True)
                for t in range(tiles):
                    body(last, t, True, t + 1 < tiles, t + 2 < tiles)
                g = base + tiles * PEER_HEADS
                gelu(g - 1, 1)
                act.wait_ge(weight_ready, g)
                diags(g - 1, 1, 0, TOPK)

            def program():
                conditions()
                act.wait_ge(pool_loads, first_loads)
                sum_squares(lambda t: xs[:, t, :], lambda t: h[:, t, :], TILES)
                turn_rows("hT0", hT0, TILES)
                attn_in()
                if end_stage("act", act):
                    return
                attention()
                if end_stage("act", act):
                    return
                turn_rows("oT0", hT, TILES)
                if end_stage("act", act):
                    return
                sum_squares(lambda t: xs[:, t, :], lambda t: ffn_in[:, t, :], TILES)
                turn_rows("fT0", ffn_inT, TILES)
                turn_keys(0)
                if end_stage("act", act):
                    return
                experts(0, TILES)
                if end_stage("act", act):
                    return
                sum_squares(lambda t: xs[:, t, :], lambda t: h_gla[:, t, :], TILES)
                turn_rows("hT1", gla_hT, TILES)
                gla_in()
                if end_stage("act", act):
                    return
                gla()
                if end_stage("act", act):
                    return
                turn_rows("oT1", gla_hT, LAT_TILES)
                if end_stage("act", act):
                    return
                sum_squares(lambda t: xs[:, t, :], lambda t: ffn_in[:, t, :], LAT_TILES)
                turn_rows("fT1", ffn_inT, LAT_TILES)
                turn_keys(1)
                if end_stage("act", act):
                    return
                experts(1, LAT_TILES)
                end_stage("act", act)
                sum_squares(lambda t: xs[:, t, :], lambda t: ffn_in[:, t, :], LAT_TILES)

            program()

        @block.gpsimd
        def _(pool):
            def load(dst, src):
                pool.dma_start(dst, src).then_inc(pool_loads, 16)

            def row(src, n, parts=P):
                return src.rearrange("(a n) -> a n", a=1).to_broadcast((parts, n))

            def modulation(layer, section, conds, gate):
                for cond in range(conds):
                    src = mod_dram[cond, layer, section:section + 2, :].rearrange("a b -> (a b)")
                    load(mod_rows[:, cond, :, :].rearrange("p a b -> p (a b)"), row(src, 2 * D))
                    load(gate_rows[:, cond, :], row(mod_dram[cond, layer, gate, :], D))

            def experts(layer, tiles):
                base = layer * GATHER_LAYER_STEPS
                last = PEER_HEADS - 1

                def gather_u(g, par, k):
                    pool.wait_ge(u_free, g * TOPK + (k + 1))
                    hold(pool)
                    pool.indirect_dma_start(u_rows[:, k % RING, :], None, expert_u,
                                            bass.IndirectOffsetOnAxis(idx_u[:, par, k:k + 1], 0)
                                            ).then_inc(u_in[k % RING], 16)

                def gather_v(g, par, k):
                    pool.wait_ge(v_free, g * TOPK + (k + 1))
                    hold(pool)
                    pool.indirect_dma_start(v_rows[:, k % RING, :], None, expert_v,
                                            bass.IndirectOffsetOnAxis(idx_v[:, par, k:k + 1], 0)
                                            ).then_inc(v_in[k % RING], 16)

                def body(g, par):
                    pool.wait_ge(idx_u_ready, g + 1)
                    pool.wait_ge(idx_v_ready, g)
                    for k in range(TOPK):
                        gather_u(g, par, k)
                        gather_v(g + (-1), 1 - par, k)

                def heads_steps(head, first):
                    for t in range(first, tiles):
                        body(head * tiles + (base + t), t % 2)

                pool.wait_ge(idx_u_ready, base + 1)
                for k in range(TOPK):
                    gather_u(base, 0, k)
                heads_steps(0, 1)
                with pool.Fori(1, last + 1) as head:
                    heads_steps(head, 0)
                n = base + tiles * PEER_HEADS
                pool.wait_ge(idx_v_ready, n)
                for k in range(TOPK):
                    gather_v(n - 1, 1, k)

            def program():
                load(mods[0:2, :], row(ada_b.rearrange("l n -> (l n)"), LAYERS * MOD_DIM, 2))
                load(norm_gains[0:2, 0:2, :].rearrange("p a b -> p (a b)"),
                     row(norm_mix.rearrange("l n -> (l n)"), LAYERS * D, 2))
                load(norm_gains[0:2, 2:4, :].rearrange("p a b -> p (a b)"),
                     row(norm_ffn.rearrange("l n -> (l n)"), LAYERS * D, 2))
                load(xs[:, 0:LAT_TILES, :], x[0].rearrange("(t p) d -> p t d", p=P))
                load(xs[:, LAT_TILES:TILES, :], ctx[0].rearrange("(t p) d -> p t d", p=P))
                for layer in range(LAYERS):
                    pool.wait_ge(mods_ready, layer + 1)
                    pool.dma_start(mod_dram[:, layer, :, :].rearrange("c s d -> c (s d)"),
                                   mods[0:2, layer * MOD_DIM:(layer + 1) * MOD_DIM]).then_inc(stored, 16)
                    pool.wait_ge(stored, 16 * (layer + 1))
                    if layer == 0:
                        modulation(0, 0, 2, 2)
                if end_stage("pool", pool):
                    return
                load(qk_gain[:, 0, :], row(attn_q_gain[0], HEAD_DIM))
                load(qk_gain[:, 1, :], row(attn_k_gain[0], HEAD_DIM))
                load(sinks, row(attn_sink[0], HEADS_A))
                for _ in range(2):
                    if end_stage("pool", pool):
                        return
                modulation(0, 3, 2, 5)
                load(keys, peer_keys[0].rearrange("h s n d -> n (h s) d"))
                if end_stage("pool", pool):
                    return
                experts(0, TILES)
                if end_stage("pool", pool):
                    return
                modulation(1, 0, 2, 2)
                if end_stage("pool", pool):
                    return
                load(gate_w[0:RANK, :, :], gla_gate_w[0].rearrange("d r n -> r d n"))
                load(gate_bias.rearrange("p a b -> p (a b)"), row(gla_gate_b[0].rearrange("d n -> (d n)"), 2 * KD))
                load(head_gain, row(gla_head_gain[0], DV))
                for _ in range(2):
                    if end_stage("pool", pool):
                        return
                modulation(1, 3, 1, 5)
                load(keys, peer_keys[1].rearrange("h s n d -> n (h s) d"))
                if end_stage("pool", pool):
                    return
                experts(1, LAT_TILES)
                end_stage("pool", pool)
                load(mod_rows[:, 0, 0, :], row(final_norm, D))
                pool.wait_ge(h_ready, final_rows)
                pool.dma_start(out[0].rearrange("(t p) d -> p t d", p=P), ffn_in[:, 0:LAT_TILES, :]).then_inc(stored, 16)
                pool.wait_ge(stored, 16 * (LAYERS + 1))

            program()

        @block.vector
        def _(dve):
            steps = Steps(dve, dve_step)
            link = steps.link
            count = Count()

            def conditions():
                dve.wait_ge(cond_exp_ready, 1)
                link(dve.tensor_scalar_add(cond_tmp, cond_tmp, 1.0))
                link(dve.reciprocal(cond_tmp, cond_tmp))
                dve.tensor_tensor(cond_act, bank[7][:, 0:2 * KC], cond_tmp, ALU.mult).then_inc(cond_ready, 1)
                dve.wait_ge(cond_ready, 1)
                dve.sem_inc(bank_drained[7], 1)

            def modulation(layer):
                dve.wait_ge(pool_loads, cond_loads)
                for n in range(MOD_DIM // WBLK):
                    b = wait_bank(dve, ("ada", layer, n))
                    cols = mods[0:2, layer * MOD_DIM + n * WBLK:layer * MOD_DIM + (n + 1) * WBLK]
                    dve.tensor_tensor(cols, bank[b][0:2, :], cols, ALU.add).then_inc(bank_drained[b], 1)
                    wait_drained(dve, ("ada", layer, n))
                for section, gains in ((1, 0), (4, 2)):
                    c0 = layer * MOD_DIM + section * D
                    link(dve.scalar_tensor_tensor(mods[0:2, c0:c0 + D], mods[0:2, c0:c0 + D], 1.0,
                                                  norm_gains[0:2, gains + layer, :], ALU.add, ALU.mult))
                dve.sem_inc(mods_ready, 1)

            def inverse_root(n, width):
                dve.wait_ge(sumsq_ready, count.next("sumsq"))
                dve.tensor_scalar(stat[:, 8:8 + n], stat[:, 0:n], 1.0 / width, EPS, ALU.mult,
                                  ALU.add).then_inc(mean_ready, 1)
                dve.wait_ge(root_ready, count.next("root"))
                link(dve.reciprocal(stat[:, 24:24 + n], stat[:, 16:16 + n]))

            def modulate(dst, tiles, loads):
                inverse_root(tiles, D)
                dve.wait_ge(pool_loads, loads)
                for t in range(tiles):
                    cond = t // LAT_TILES
                    link(dve.scalar_tensor_tensor(dst[:, t, :], xs[:, t, :], stat[:, 24 + t:25 + t],
                                                  mod_rows[:, cond, 1, :], ALU.mult, ALU.mult))
                    dve.tensor_tensor(dst[:, t, :], dst[:, t, :], mod_rows[:, cond, 0, :],
                                      ALU.add).then_inc(h_ready, 1)

            def rotate(rows, t):
                heads = rows.rearrange("p (h a s r) -> p (h a) s r", h=10, a=2, s=2)
                swap = swapped.rearrange("p (h a s r) -> p (h a) s r", h=10, a=2, s=2)
                for s in range(2):
                    ins = dve.tensor_copy(swap[:, :, s, :], heads[:, :, 1 - s, :])
                link(ins)
                w = HEAD_DIM
                cos = cst[:, C_COS + t * w:C_COS + (t + 1) * w].unsqueeze(1).to_broadcast([P, 10, w])
                sin = cst[:, C_SIN + t * w:C_SIN + (t + 1) * w].unsqueeze(1).to_broadcast([P, 10, w])
                by_head = rows.rearrange("p (h n) -> p h n", h=10)
                sw = swapped.rearrange("p (h n) -> p h n", h=10)
                dve.tensor_tensor(by_head, by_head, cos, ALU.mult)
                link(dve.tensor_tensor(sw, sw, sin, ALU.mult))
                link(dve.tensor_tensor(by_head, by_head, sw, ALU.add))

            def attention():
                dve.wait_ge(pool_loads, attn_loads)
                for t in range(TILES):
                    rows = proj[:, t, B_OFF:B_OFF + 640]
                    link(dve.tensor_tensor(turned, rows, rows, ALU.mult))
                    link(dve.tensor_reduce(qk_stat[:, 0, 10 * t:10 * t + 10], turned.rearrange("p (h n) -> p h n", h=10),
                                           AX_X, ALU.add))
                dve.tensor_scalar(qk_stat[:, 1, :], qk_stat[:, 0, :], 1.0 / HEAD_DIM, EPS, ALU.mult,
                                  ALU.add).then_inc(mean_ready, 1)
                dve.wait_ge(root_ready, count.next("root"))
                link(dve.reciprocal(qk_stat[:, 3, :], qk_stat[:, 2, :]))
                for t in range(TILES):
                    rows = proj[:, t, B_OFF:B_OFF + 640].rearrange("p (h n) -> p h n", h=10)
                    link(dve.tensor_tensor(rows, rows, qk_stat[:, 3, 10 * t:10 * t + 10].unsqueeze(2).to_broadcast(
                        [P, 10, HEAD_DIM]), ALU.mult))
                    dve.tensor_tensor(rows[:, 0:8, :], rows[:, 0:8, :],
                                      qk_gain[:, 0:1, :].to_broadcast([P, 8, HEAD_DIM]), ALU.mult)
                    link(dve.tensor_tensor(rows[:, 8:10, :], rows[:, 8:10, :],
                                           qk_gain[:, 1:2, :].to_broadcast([P, 2, HEAD_DIM]), ALU.mult))
                    if t < LAT_TILES:
                        rotate(proj[:, t, 0:640], t)
                        rotate(proj[:, t, B_OFF:B_OFF + 640], t)
                    if t >= 2:
                        wait_bank(dve, ("qkT", t - 2, 2))
                    for kind in range(2):
                        k0 = kind * B_OFF + 512
                        for kv in range(2):
                            src = proj[:, t, k0 + kv * HEAD_DIM:k0 + (kv + 1) * HEAD_DIM]
                            ins = dve.tensor_copy(kdup[:, t % 2, 2 * kind + kv, :].rearrange("p (a b) -> p a b", a=2),
                                                  src.unsqueeze(1).to_broadcast([P, 2, HEAD_DIM]))
                    ins.then_inc(qk_ready, 1)
                for i in range(len(attn_steps) + 2):
                    if i < len(attn_steps):
                        t, hd = attn_steps[i]
                        nk = TILES if t < LAT_TILES else LAT_TILES
                        st = att_stat[:, i % 4, :]
                        b = wait_bank(dve, ("s", i))
                        if hd < HEADS_A and t < LAT_TILES:
                            cols = bank[b][:, (1 - t) * P:(2 - t) * P]
                            link(dve.tensor_tensor(cols, cols, cst[:, C_BAND + t * P:C_BAND + (t + 1) * P], ALU.add))
                        link(dve.tensor_reduce(st[:, 0:1], bank[b][:, 0:nk * P], AX_X, ALU.max))
                        if hd < HEADS_A:
                            link(dve.tensor_scalar(st[:, 0:1], st[:, 0:1], ATTN_SCALE, sinks[:, hd:hd + 1], ALU.mult,
                                                   ALU.max))
                            dve.tensor_scalar(st[:, 1:2], st[:, 0:1], -1.0, None, ALU.mult).then_inc(att_max, 1)
                        else:
                            dve.tensor_scalar(st[:, 1:2], st[:, 0:1], -ATTN_SCALE, None, ALU.mult).then_inc(att_max, 1)
                    if i >= 2:
                        m = i - 2
                        t, hd = attn_steps[m]
                        st = att_stat[:, m % 4, :]
                        wait_drained(dve, ("s", m))
                        if hd < HEADS_A:
                            dve.wait_ge(sink_exp, count.next("sink"))
                            link(dve.tensor_tensor(st[:, 2:3], st[:, 2:3], st[:, 3:4], ALU.add))
                        link(dve.reciprocal(st[:, 2:3], st[:, 2:3]))
                        b = wait_bank(dve, ("o", m))
                        dve.tensor_scalar(h[:, t, hd * HEAD_DIM:(hd + 1) * HEAD_DIM], bank[b][:, 0:HEAD_DIM],
                                          st[:, 2:3], None, ALU.mult).then_inc(bank_drained[b], 1)

            def residual(name, tiles):
                for n in range(D // WBLK):
                    for t in range(tiles):
                        b = wait_bank(dve, (name, n, t))
                        cols = slice(n * WBLK, (n + 1) * WBLK)
                        link(dve.tensor_tensor(update[:, t % 2, :], bank[b][:, :],
                                               gate_rows[:, t // LAT_TILES, cols], ALU.mult))
                        dve.sem_inc(bank_drained[b], 1)
                        dve.tensor_tensor(xs[:, t, cols], xs[:, t, cols], update[:, t % 2, :], ALU.add)

            def gla():
                dve.wait_ge(pool_loads, gla_loads)
                ins = dve.memset(att_masked, 0.0)
                link(ins)
                for d in range(2):
                    for t in range(TILES + 1):
                        if t < TILES:
                            z = gate_tmp[:, t % 2, :]
                            b = wait_bank(dve, ("z", d, t))
                            dve.tensor_tensor(z, bank[b][:, :], gate_bias[:, d, :], ALU.add).then_inc(bank_drained[b], 1)
                            wait_drained(dve, ("z", d, t))
                            dve.tensor_scalar(log_decay[:, t, :], z, 0.0, 1.0 / GATE_NORM, ALU.min, ALU.mult)
                            link(dve.scalar_tensor_tensor(z, z, -1.0, z, ALU.mult, ALU.max))
                            dve.sem_inc(gate_z, 1)
                        if t >= 1:
                            m = t - 1
                            dve.wait_ge(gate_ln, count.next("ln"))
                            dve.scalar_tensor_tensor(log_decay[:, m, :], gate_tmp[:, m % 2, :], -1.0 / GATE_NORM,
                                                     log_decay[:, m, :], ALU.mult, ALU.add).then_inc(decay_ready, 1)
                            dve.wait_ge(decay_ready, TILES * d + t)
                    for t in range(TILES):
                        if t < LAT_TILES:
                            q, k = gla_lat[:, t, 0:KD], gla_lat[:, t, KD:2 * KD]
                            dve.wait_ge(exp_ready, count.next("exp"))
                            dve.scalar_tensor_tensor(q_dec[:, t, :], q, DK**-0.5, q_dec[:, t, :], ALU.mult, ALU.mult)
                            wait_drained(dve, ("b", d, t))
                            dve.tensor_tensor(k_inv[:, t, :], k_inv[:, t, :], k, ALU.mult)
                        else:
                            k = gla_ctx[:, t - LAT_TILES, 0:KD]
                        wait_drained(dve, ("rest", d, t))
                        dve.tensor_tensor(k_end[:, t, :], k_end[:, t, :], k, ALU.mult).then_inc(keyed_ready, 1)
                    wait_drained(dve, ("end", d))
                    done = {}
                    for n, (hh, kind, chunk, slot) in enumerate(gla_updates(d)):
                        b = wait_bank(dve, ("kv", d, n))
                        new = states[:, hh, slot, :]
                        if hh not in done:
                            ins = dve.tensor_copy(new, bank[b][:, 0:DV])
                        else:
                            tile = chunk // 2 + (LAT_TILES if kind == "ctx" else 0)
                            ins = dve.scalar_tensor_tensor(new, states[:, hh, done[hh], :],
                                                           decay_end[:, hh, tile, chunk % 2:chunk % 2 + 1],
                                                           bank[b][:, 0:DV], ALU.mult, ALU.add)
                        done[hh] = slot
                        ins.then_inc(state_ready, 1)
                        dve.wait_ge(state_ready, count.next("state"))
                        dve.sem_inc(bank_drained[b], 1)
                    mask = cst[:, (C_UPPER, C_LOWER)[d]:(C_UPPER, C_LOWER)[d] + P].bitcast(U32)
                    for i in range(len(gla_jobs) + 1):
                        if i < len(gla_jobs):
                            b = wait_bank(dve, ("att", d, i))
                            if i >= 2:
                                wait_bank(dve, ("go", d, i - 2))
                            dve.copy_predicated(att_masked[:, 2 * d + i % 2, :], mask,
                                                bank[b][:, 0:P]).then_inc(masked_ready, 1)
                            dve.wait_ge(masked_ready, count.next("masked"))
                            dve.sem_inc(bank_drained[b], 1)
                        if i >= 1:
                            m = i - 1
                            t, hh = gla_jobs[m]
                            o = gla_o[:, t, hh * DV:(hh + 1) * DV]
                            b = wait_bank(dve, ("go", d, m))
                            if d == 0:
                                ins = dve.tensor_copy(o, bank[b][:, 0:DV])
                            else:
                                ins = dve.tensor_tensor(o, bank[b][:, 0:DV], o, ALU.add)
                            ins.then_inc(bank_drained[b], 1)
                dve.drain().then_inc(out_ready, 1)
                inverse_root(len(gla_jobs), DV)
                for t in range(LAT_TILES):
                    dve.wait_ge(silu_exp, t + 1)
                    e = silu_r[:, t, :]
                    link(dve.tensor_scalar_add(e, e, 1.0))
                    link(dve.reciprocal(e, e))
                    link(dve.tensor_tensor(e, e, gla_lat[:, t, 2 * KD + VD:2 * KD + 2 * VD], ALU.mult))
                    for hh in range(GLA_HEADS):
                        o = gla_o[:, t, hh * DV:(hh + 1) * DV]
                        j = 24 + t * GLA_HEADS + hh
                        link(dve.scalar_tensor_tensor(o, o, stat[:, j:j + 1], head_gain, ALU.mult, ALU.mult))
                    dve.tensor_tensor(gla_o[:, t, :], gla_o[:, t, :], e, ALU.mult)

            def largest(values, at_u, src, rest):
                hold(dve)
                link(dve.max(values[:, 0:8], src))
                hold(dve)
                dve.max_index(at_u[:, 0:8], values[:, 0:8], src)
                link(dve.match_replace(rest, values[:, 0:8], src, LOWEST))
                hold(dve)
                link(dve.max(values[:, 8:16], rest))
                hold(dve)
                link(dve.max_index(at_u[:, 8:16], values[:, 8:16], rest))

            def route_half(g, par, half):
                if half == 0:
                    dve.wait_ge(head_scores_ready, g + 1)
                largest(top[:, half, :], top_at_u[:, half, :],
                        head_scores[:, par, half * N_KEYS:(half + 1) * N_KEYS], rest_scores[:, half, :])

            def route_sums():
                dve.tensor_tensor(sums.rearrange("p (a b) -> p a b", a=TOPK),
                                  top[:, 0, :].unsqueeze(2).to_broadcast([P, TOPK, TOPK]),
                                  top[:, 1:2, :].to_broadcast([P, TOPK, TOPK]), ALU.add)
                link(dve.tensor_copy(top_at, top_at_u))

            def route_best(g, par, layer):
                largest(best[:, par, :], best_at_u, sums, rest_sums)
                dve.tensor_scalar(neg_best[:, par:par + 1], best[:, par, 0:1], -1.0, None, ALU.mult).then_inc(best_ready, 1)
                link(dve.tensor_scalar(top_at[:, 0, :], top_at[:, 0, :], float(N_KEYS), float(layer * EXPERTS),
                                       ALU.mult, ALU.add))

            def route_experts(g, par):
                pair_u = best_pair_u.rearrange("p (k s) -> p k s", s=2)
                dve.tensor_scalar(pair_u[:, :, 0], best_at_u, 4, None, ALU.logical_shift_right)
                link(dve.tensor_scalar(pair_u[:, :, 1], best_at_u, 15, None, ALU.bitwise_and))
                link(dve.tensor_copy(best_pair, best_pair_u))
                hot = one_hot.rearrange("p (k s j) -> p k s j", k=TOPK, s=2)
                link(dve.tensor_tensor(one_hot.rearrange("p (k j) -> p k j", j=TOPK),
                                       best_pair.unsqueeze(2).to_broadcast([P, 2 * TOPK, TOPK]),
                                       cst[:, C_IOTA:C_IOTA + TOPK].unsqueeze(1).to_broadcast([P, 2 * TOPK, TOPK]),
                                       ALU.is_equal))
                link(dve.tensor_tensor(hot, hot, top_at.unsqueeze(1).to_broadcast([P, TOPK, 2, TOPK]), ALU.mult))
                link(dve.tensor_reduce(best_pair[:, 0:TOPK], one_hot.rearrange("p (k j) -> p k j", k=TOPK), AX_X,
                                       ALU.add))
                dve.tensor_copy(idx_u[:, par, :], best_pair[:, 0:TOPK]).then_inc(idx_u_ready, 1)

            def route_all(g, par, layer):
                route_half(g, par, 0)
                route_half(g, par, 1)
                route_sums()
                route_best(g, par, layer)
                route_experts(g, par)

            def weigh(g, par):
                dve.wait_ge(gate_num_ready, g + 1)
                link(dve.reciprocal(gate_sum[:, par:par + 1], gate_sum[:, par:par + 1]))
                dve.wait_ge(gelu_ready, g + 1)
                dve.scalar_tensor_tensor(pick_weight[:, par, :], act_gelu[:, par, :], gate_sum[:, par:par + 1],
                                         gate_num[:, par, :], ALU.mult, ALU.mult).then_inc(weight_ready, 1)

            def add_y(tile, g, par):
                dve.wait_ge(v_free, g * TOPK + (TOPK + RING))
                for half in range(2):
                    cols = slice(half * WBLK, (half + 1) * WBLK)
                    b = bank[2 * par + half]
                    link(dve.tensor_tensor(b[:, :], b[:, :], gate_rows[:, tile // LAT_TILES, cols], ALU.mult))
                    rows = xs[:, tile, cols]
                    ins = dve.tensor_tensor(rows, rows, b[:, :], ALU.add)
                    if half == 0:
                        link(ins)
                ins.then_inc(y_free, 1)

            def body(head, t, base, layer, tiles, prev, done, nxt):
                g, par = head * tiles + (base + t), t % 2
                for k in range(TOPK):
                    dve.wait_ge(u_in[k % RING], g * 32 + 16 * (k // RING + 1))
                    dve.tensor_tensor_reduce(u_rows[:, k % RING, :], u_rows[:, k % RING, :], ffn_in[:, t, :], 1.0, 0.0,
                                             ALU.mult, ALU.add, act_raw[:, par, k:k + 1]).then_inc(u_free, 1)
                    if k == 1 and prev:
                        weigh(g + (-1), 1 - par)
                    if k == 3 and nxt:
                        route_half(g + 1, 1 - par, 0)
                    if k == 5 and nxt:
                        route_half(g + 1, 1 - par, 1)
                    if k == 6 and done:
                        add_y((t - 2) % tiles, g + (-2), par)
                    if k == 7 and nxt:
                        route_sums()
                    if k == 9 and nxt:
                        route_best(g + 1, 1 - par, layer)
                    if k == 10:
                        if prev or layer:
                            dve.wait_ge(v_free, g * TOPK + (RING - TOPK))
                        dve.tensor_copy(idx_v[:, par, :], idx_u[:, par, :]).then_inc(idx_v_ready, 1)
                    if k == 12 and nxt:
                        route_experts(g + 1, 1 - par)

            LINKS = 23

            def experts(layer, tiles):
                n, base = tiles * PEER_HEADS, layer * GATHER_LAYER_STEPS
                last = PEER_HEADS - 1
                if layer == 0:
                    dve.sem_inc(u_free, RING)
                    dve.sem_inc(y_free, 2)
                route_all(base, 0, layer)
                for t in range(tiles):
                    body(0, t, base, layer, tiles, t > 0, t > 1, True)
                steps_before = steps.n
                steps.n = 0
                with dve.Fori(0, last - 1) as turn_no:
                    steps.base = turn_no * (tiles * LINKS) + steps_before
                    for t in range(tiles):
                        body(turn_no + 1, t, base, layer, tiles, True, True, True)
                assert steps.n == tiles * LINKS, steps.n
                steps.base, steps.n = 0, steps_before + (last - 1) * tiles * LINKS
                for t in range(tiles):
                    body(last, t, base, layer, tiles, True, True, t + 1 < tiles)
                weigh(base + n - 1, 1)
                add_y(tiles - 2, base + n - 2, 0)
                add_y(tiles - 1, base + n - 1, 1)

            def final():
                inverse_root(LAT_TILES, D)
                dve.wait_ge(pool_loads, final_loads)
                for t in range(LAT_TILES):
                    dve.scalar_tensor_tensor(ffn_in[:, t, :], xs[:, t, :], stat[:, 24 + t:25 + t],
                                             mod_rows[:, 0, 0, :], ALU.mult, ALU.mult).then_inc(h_ready, 1)

            def program():
                conditions()
                modulation(0)
                modulate(h, TILES, first_loads)
                modulation(1)
                if end_stage("dve", dve):
                    return
                attention()
                if end_stage("dve", dve):
                    return
                residual("out0", TILES)
                if end_stage("dve", dve):
                    return
                modulate(ffn_in, TILES, key_loads[0])
                if end_stage("dve", dve):
                    return
                experts(0, TILES)
                if end_stage("dve", dve):
                    return
                modulate(h_gla, TILES, gla_loads - 48)
                if end_stage("dve", dve):
                    return
                gla()
                if end_stage("dve", dve):
                    return
                residual("out1", LAT_TILES)
                if end_stage("dve", dve):
                    return
                modulate(ffn_in, LAT_TILES, key_loads[1])
                if end_stage("dve", dve):
                    return
                experts(1, LAT_TILES)
                end_stage("dve", dve)
                final()

            program()


_INS = ["x", "c", "ctx", "c_ctx", "ada_w", "ada_b", "norm_mix", "norm_ffn", "attn_w_in", "attn_sink",
        "attn_q_gain", "attn_k_gain", "attn_w_out", "gla_w_in", "gla_gate_w", "gla_gate_b", "gla_head_gain",
        "gla_w_out", "peer_wq", "peer_keys", "peer_u", "peer_v", "final_norm"]


def kernel(**inputs):
    import concourse.bacc as bacc
    from concourse.bass_utils import run_bass_kernel_spmd

    nc = bacc.Bacc("TRN2", target_bir_lowering=False, num_devices=1)
    arrays, args = {}, []
    for name in _INS:
        arrays[f"in_{name}"] = np.ascontiguousarray(inputs[name])
    arrays["in_consts"] = shape_constants()
    for name, a in arrays.items():
        args.append(nc.dram_tensor(name, a.shape, mybir.dt.from_np(a.dtype), kind="ExternalInput").ap())
    args.append(nc.dram_tensor("out", (1, SEQ, D), F32, kind="ExternalOutput").ap())
    build(nc, *args)
    r = run_bass_kernel_spmd(nc, [arrays], core_ids=[0])
    return r.results[0]["out"]
```

```python
from contextlib import ExitStack

import concourse.bass as bass
import numpy as np
from concourse import mybir

F32 = mybir.dt.float32
U32 = mybir.dt.uint32
ALU = mybir.AluOpType
ACT = mybir.ActivationFunctionType
AX_X = mybir.AxisListType.X

P = 128
D = 1024
KC = D // P
SEQ = 256
LAT_TILES = SEQ // P
TILES = 2 * LAT_TILES
WBLK = 512
EPS = 1e-6
LAYERS = 2
SECTIONS = 6
MOD_DIM = SECTIONS * D

HEAD_DIM = 64
GRID_W = 64
ROPE_PAIRS = HEAD_DIM // 4
HEADS_A = 8
ATTN_HEADS = 16
KV_GROUP = 4
ATTN_IN = 1536
ATTN_SCALE = HEAD_DIM**-0.5
B_OFF = 768
WINDOW = 128

GLA_HEADS = 4
DK = 128
DV = 256
KD = GLA_HEADS * DK
VD = GLA_HEADS * DV
RANK = 16
GATE_NORM = 16.0
CHUNK = 64
CHUNKS = SEQ // CHUNK
GLA_IN = 2 * KD + 2 * VD + 2 * RANK

PEER_HEADS = 8
N_KEYS = 128
EXPERTS = N_KEYS * N_KEYS
TOPK = 16
RING = 8
DIAGS = 4
PROB_BUFS = 4
GATE_BUFS = 6
LOWEST = -3.0e38

C_IDENT = 0
C_UPPER = 128
C_LOWER = 256
C_UPPER_STRICT = 384
C_LOWER_STRICT = 512
C_BAND = 640
C_COS = 896
C_SIN = 1024
C_IOTA = 1152
C_CHUNK = 1168
C_COLS = 1170


def shape_constants():
    c = np.zeros((P, C_COLS), np.float32)
    i = np.arange(P)
    same = (i[:, None] // CHUNK) == (i[None, :] // CHUNK)
    c[:, C_IDENT:C_IDENT + P] = np.eye(P)
    c[:, C_UPPER:C_UPPER + P] = same & (i[:, None] <= i[None, :])
    c[:, C_LOWER:C_LOWER + P] = same & (i[:, None] >= i[None, :])
    c[:, C_UPPER_STRICT:C_UPPER_STRICT + P] = same & (i[:, None] < i[None, :])
    c[:, C_LOWER_STRICT:C_LOWER_STRICT + P] = same & (i[:, None] > i[None, :])
    for t in range(LAT_TILES):
        query, key = t * P + i[:, None], (1 - t) * P + i[None, :]
        c[:, C_BAND + t * P:C_BAND + (t + 1) * P] = np.where(np.abs(query - key) <= WINDOW, 0.0, -1e30)
        tok = t * P + i
        pos = np.stack([tok // GRID_W, tok % GRID_W], -1).astype(np.float32)
        inv = (10000.0 ** (-np.arange(ROPE_PAIRS, dtype=np.float32) / ROPE_PAIRS)).astype(np.float32)
        ang = pos[:, :, None] * inv
        cos, sin = np.cos(ang), np.sin(ang)
        w = HEAD_DIM
        c[:, C_COS + t * w:C_COS + (t + 1) * w] = np.stack([cos, cos], 2).reshape(P, w)
        c[:, C_SIN + t * w:C_SIN + (t + 1) * w] = np.stack([-sin, sin], 2).reshape(P, w)
    c[:, C_IOTA:C_IOTA + TOPK] = np.arange(TOPK)
    c[:, C_CHUNK] = i < CHUNK
    c[:, C_CHUNK + 1] = i >= CHUNK
    return c


def build(nc, x, c, ctx, c_ctx, ada_w, ada_b, norm_mix, norm_ffn, attn_w_in, attn_sink, attn_q_gain,
          attn_k_gain, attn_w_out, gla_w_in, gla_gate_w, gla_gate_b, gla_head_gain, gla_w_out,
          peer_wq, peer_keys, peer_u, peer_v, final_norm, consts, out, stop=99):
    mod_dram = nc.dram_tensor("mod_dram", (2, LAYERS, SECTIONS, D), F32, kind="Internal").ap()
    expert_u = peer_u.rearrange("l e d -> (l e) d")
    expert_v = peer_v.rearrange("l e d -> (l e) d")

    blocks = []

    def stream(name, w, n):
        for b in range(-(-n // WBLK)):
            cols = min(WBLK, n - b * WBLK)
            blocks.append((name, b, w.rearrange("(k p) n -> p k n", p=P)[:, :, b * WBLK:b * WBLK + cols], cols))

    for layer in range(LAYERS):
        stream(f"ada{layer}", ada_w[layer], MOD_DIM)
    stream("attn_in", attn_w_in[0], ATTN_IN)
    stream("out0", attn_w_out[0], D)
    stream("gla_in", gla_w_in[0], GLA_IN)
    stream("out1", gla_w_out[0], D)
    block_at = {(name, b): n for n, (name, b, _, _) in enumerate(blocks)}
    WSLOTS = 3
    slot_of, load_no, slot_before = [], [], []
    n_ada = LAYERS * MOD_DIM // WBLK
    for n in range(len(blocks)):
        slot = n % WSLOTS if n < n_ada else (n - n_ada) % (WSLOTS - 1)
        same = [m for m in range(n) if slot_of[m] == slot]
        slot_of.append(slot)
        load_no.append(len(same))
        slot_before.append(same[-1] if same else None)

    with ExitStack() as es:
        def sb(name, shape, dt=F32):
            return es.enter_context(nc.sbuf_tensor(name, shape, dt))

        def sem(name):
            return es.enter_context(nc.semaphore(name))

        xs = sb("xs", [P, TILES, D])
        wring = sb("wring", [P, WSLOTS, KC, WBLK])
        mod_rows = sb("mod_rows", [P, 2, 2, D])
        gate_rows = sb("gate_rows", [P, 2, D])
        cst = sb("cst", [P, C_COLS])
        work = sb("work", [P, 28672])
        stat = sb("stat", [P, 32])
        diag = sb("diag", [P, DIAGS, P])
        picks_u = sb("picks_u", [P, 80], U32)
        idx_u = sb("idx_u", [P, 2, TOPK], U32)
        idx_v = sb("idx_v", [P, 2, TOPK], U32)
        query_w = wring[:, WSLOTS - 1, :, :].rearrange("p k (s n) -> p s k n", s=2)
        bank = [es.enter_context(nc.psum_tensor(f"bank{i}", [P, WBLK], F32)) for i in range(8)]

        def at(start, *dims):
            n = int(np.prod(dims))
            v = work[:, start:start + n]
            if len(dims) == 2:
                return v.rearrange("p (a b) -> p a b", a=dims[0])
            if len(dims) == 3:
                return v.rearrange("p (a b c) -> p a b c", a=dims[0], b=dims[1])
            return v

        ident = cst[:, C_IDENT:C_IDENT + P]

        mods = at(0, LAYERS * MOD_DIM)
        norm_gains = at(12288, 4, D)
        proj = at(0, TILES, ATTN_IN)
        qkT = at(6144, 12, TILES * P)
        hT = at(12288, KC, TILES * P)
        h = at(16384, TILES, D)
        kdup = at(12288, 2, 4, P)
        swapped = at(13312, 640)
        squares = at(13952, 640)
        qk_gain = at(14592, 2, HEAD_DIM)
        sinks = at(14720, HEADS_A)
        probs = at(20480, PROB_BUFS, TILES * P)
        probsT = at(22528, PROB_BUFS, TILES * P)
        update = at(11264, 2, WBLK)
        att_stat = at(25984, 4, 4)
        qk_stat = at(26000, 4, TILES * 10)
        cond_in = at(24576, P)
        cond_act = at(24704, 2 * KC)
        cond_tmp = at(24720, 2 * KC)
        hT0 = at(20480, KC, TILES * P)

        ffn_in = at(0, TILES, D)
        ffn_inT = at(4096, KC, TILES * P)
        keysT = at(8192, 2 * PEER_HEADS, P)
        query_rows = at(10240, 2, P)
        queryT = at(10496, 2, P)
        head_scores = at(10752, 2, 2 * N_KEYS)
        keys = [at(20480, 2 * PEER_HEADS, P), at(12288, 2 * PEER_HEADS, P)]
        u_rows = at(12288, RING, D)
        v_rows = at(20480, RING, D)
        route = mod_rows[:, 1, :, :].rearrange("p a b -> p (a b)")

        def route_at(start, *dims):
            n = int(np.prod(dims))
            v = route[:, start:start + n]
            return v.rearrange("p (a b) -> p a b", a=dims[0]) if len(dims) == 2 else v

        best = route_at(512, 2, TOPK)
        sums = route_at(768, TOPK * TOPK)
        rest_sums = route_at(1024, TOPK * TOPK)
        one_hot = route_at(1280, 2 * TOPK * TOPK)
        rest_scores = route_at(1280, 2, N_KEYS)
        act_raw = route_at(1792, 2, TOPK)
        act_gelu = route_at(1824, 2, TOPK)
        gate_num = route_at(1856, 2, TOPK)
        pick_weight = route_at(1888, 2, TOPK)
        gate_sum = route_at(1920, 2)
        neg_best = route_at(1922, 2)
        top = route_at(1924, 2, TOPK)
        top_at = route_at(1956, 2, TOPK)
        best_pair = route_at(1988, 2 * TOPK)
        top_at_u = picks_u[:, 0:2 * TOPK].rearrange("p (a b) -> p a b", a=2)
        best_at_u = picks_u[:, 2 * TOPK:3 * TOPK]
        best_pair_u = picks_u[:, 3 * TOPK:5 * TOPK]

        gla_lat = at(0, LAT_TILES, 2 * KD + 2 * VD)
        gla_ctx = at(6144, LAT_TILES, KD + VD)
        gate_low = at(9216, TILES, 2 * RANK)
        log_decay_f = at(9344, TILES, KD)
        k_end = at(11392, TILES, KD)
        q_dec = at(13440, LAT_TILES, KD)
        k_inv = at(14464, LAT_TILES, KD)
        q_decT = at(15488, GLA_HEADS, SEQ)
        k_invT = at(16512, GLA_HEADS, SEQ)
        states = at(17536, GLA_HEADS, CHUNKS, DV)
        decay_end = at(21632, GLA_HEADS, TILES, 2)
        gla_o = at(21664, LAT_TILES, VD)
        att_masked = at(23712, 4, P)
        head_gain = at(24224, DV)
        gla_hT = at(24576, KC, TILES * P)
        h_gla = at(20480, TILES, D)
        gate_w = at(21664, 2, KD)
        gate_bias = at(22688, 2, KD)
        gate_tmp = at(24576, GATE_BUFS, KD)
        gate_lowT = at(27648, 2, TILES * P)
        squares_junk = at(9344, LAT_TILES, VD)
        silu_r = mod_rows[:, :, 0, :]
        log_decay_b = mod_rows[:, :, 1, :].rearrange("p a (b n) -> p a b n", b=2)

        def log_decay(d, t):
            return log_decay_b[:, t // 2, t % 2, :] if d else log_decay_f[:, t, :]

        w_loaded = [sem(f"w_loaded{i}") for i in range(WSLOTS)]
        bank_filled = [sem(f"bank_filled{i}") for i in range(8)]
        bank_drained = [sem(f"bank_drained{i}") for i in range(8)]
        stage_over = sem("stage_over")
        dve_step = sem("dve_step")
        held = sem("held")
        act_step = sem("act_step")
        pool_loads = sem("pool_loads")
        stored = sem("stored")
        cond_in_ready = sem("cond_in_ready")
        cond_exp_ready = sem("cond_exp_ready")
        cond_ready = sem("cond_ready")
        mods_ready = sem("mods_ready")
        sumsq_ready = sem("sumsq_ready")
        mean_ready = sem("mean_ready")
        root_ready = sem("root_ready")
        h_ready = sem("h_ready")
        qk_ready = sem("qk_ready")
        att_max = sem("att_max")
        gate_z = sem("gate_z")
        gate_ln = sem("gate_ln")
        decay_ready = sem("decay_ready")
        exp_ready = sem("exp_ready")
        sink_exp = sem("sink_exp")
        decay_end_ready = sem("decay_end_ready")
        keyed_ready = sem("keyed_ready")
        state_ready = sem("state_ready")
        masked_ready = sem("masked_ready")
        silu_exp = sem("silu_exp")
        normed_ready = sem("normed_ready")
        sigmoid_ready = sem("sigmoid_ready")
        silu_ready = sem("silu_ready")
        pool_step = sem("pool_step")
        residual_ready = sem("residual_ready")
        gate_loads = sem("gate_loads")

        u_in = [sem(f"u_in{i}") for i in range(RING)]
        v_in = [sem(f"v_in{i}") for i in range(RING)]
        u_free = sem("u_free")
        v_free = sem("v_free")
        y_free = sem("y_free")
        idx_u_ready = sem("idx_u_ready")
        idx_v_ready = sem("idx_v_ready")
        head_scores_ready = sem("head_scores_ready")
        query_loaded = sem("query_loaded")
        query_done = sem("query_done")
        query_rows_ready = sem("query_rows_ready")
        query_turned = sem("query_turned")
        queryT_ready = sem("queryT_ready")
        scores_done = sem("scores_done")
        best_ready = sem("best_ready")
        gate_num_ready = sem("gate_num_ready")
        gelu_ready = sem("gelu_ready")
        weight_ready = sem("weight_ready")
        diag_ready = sem("diag_ready")

        block = es.enter_context(nc.Block())

        class Count:

            def __init__(self):
                self.n = {}

            def next(self, name, more=1):
                self.n[name] = self.n.get(name, 0) + more
                return self.n[name]

        class Steps:

            def __init__(self, eng, done):
                self.eng, self.done, self.base, self.n = eng, done, 0, 0

            def link(self, ins):
                self.n += 1
                ins.then_inc(self.done, 1)
                self.eng.wait_ge(self.done, self.base + self.n)

        def hold(eng):
            eng.sem_inc(held, 1)

        stage_count = {}

        def end_stage(name, eng):
            n = stage_count[name] = stage_count.get(name, 0) + 1
            eng.drain().then_inc(stage_over, 1)
            eng.wait_ge(stage_over, 4 * n)
            return n >= stop

        uses = [0] * 8
        turn = {}
        weights_done = {}

        def open_bank(pe, key, b):
            n = uses[b]
            uses[b] += 1
            turn[key] = (b, n)
            if n:
                pe.wait_ge(bank_drained[b], n)
            return bank[b]

        def wait_bank(eng, key):
            b, n = turn[key]
            eng.wait_ge(bank_filled[b], n + 1)
            return b

        def wait_drained(eng, key):
            b, n = turn[key]
            eng.wait_ge(bank_drained[b], n + 1)

        def wait_weights(pe, name, b):
            n = block_at[name, b]
            pe.wait_ge(w_loaded[slot_of[n]], 16 * (load_no[n] + 1))
            return wring[:, slot_of[n], :, :]

        def last_four(name, tiles):
            return [(name, t, half) for t in range(tiles - 2, tiles) for half in range(2)]

        cond_loads = 16 * 5
        first_loads = cond_loads + 16 * 4
        attn_loads = first_loads + 16 * 3
        key_loads = [attn_loads + 16 * 3, 0]
        mod_loads = [key_loads[0] + 16, key_loads[0] + 16 * 2]
        gla_loads = mod_loads[1] + 16 * 3
        key_loads[1] = gla_loads + 16 * 2
        final_loads = key_loads[1] + 16
        final_rows = 3 * TILES + LAT_TILES + LAT_TILES

        attn_steps = [(t, hd) for t in range(TILES) for hd in range(ATTN_HEADS)]
        gla_jobs = [(t, hh) for t in range(LAT_TILES) for hh in range(GLA_HEADS)]
        GATHER_LAYER_STEPS = TILES * PEER_HEADS

        def gla_tiles(n):
            return range(TILES) if n in (1, 2, 3, 6) else range(LAT_TILES)

        def gla_updates(d):
            order = range(CHUNKS) if d == 0 else range(CHUNKS - 1, -1, -1)
            order = list(order)
            out = []
            for n in range(0, CHUNKS, 2):
                out += [(hh, "ctx", order[m], order[0]) for hh in range(GLA_HEADS) for m in (n, n + 1)]
            for n in range(0, CHUNKS - 1, 2):
                out += [(hh, "lat", order[m], order[m + 1]) for hh in range(GLA_HEADS)
                        for m in range(n, min(n + 2, CHUNKS - 1))]
            return out

        @block.tensor
        def _(pe):
            count = Count()

            def conditions():
                pe.wait_ge(cond_in_ready, 48)
                b = open_bank(pe, "cond", 7)
                pe.transpose(b[:, 0:2 * KC], cond_in[0:2 * KC, :], ident[0:2 * KC, 0:2 * KC]).then_inc(bank_filled[7], 1)
                pe.wait_ge(cond_ready, 1)
                cond = cond_act.rearrange("p (c k) -> p k c", c=2)
                for layer in range(LAYERS):
                    for n in range(MOD_DIM // WBLK):
                        w = wait_weights(pe, f"ada{layer}", n)
                        j = n % 4
                        b = open_bank(pe, ("ada", layer, n), j)
                        for k in range(KC):
                            mm = pe.matmul(b[0:2, :], cond[:, k, :], w[:, k, :], start=(k == 0), stop=(k == KC - 1))
                        mm.then_inc(bank_filled[j], 1)
                        weights_done[f"ada{layer}", n] = turn["ada", layer, n]

            def turn_tile(name, src, t):
                if name == "oT0":
                    wait_drained(pe, ("o", (t + 1) * ATTN_HEADS - 1))
                elif name == "oT1":
                    pe.wait_ge(normed_ready, t + 1)
                else:
                    pe.wait_ge(h_ready, count.next("h"))
                for half in range(2):
                    j = (2 * t + half) % 4
                    b = open_bank(pe, (name, t, half), j)
                    for k in range(4):
                        c0 = (4 * half + k) * P
                        mm = pe.transpose(b[:, k * P:(k + 1) * P], src[:, t, c0:c0 + P], ident)
                    mm.then_inc(bank_filled[j], 1)

            def turn_rows(name, src, tiles):
                for t in range(tiles):
                    turn_tile(name, src, t)
                for key in last_four(name, tiles):
                    wait_drained(pe, key)

            def project(name, src, n_cols, tiles_of):
                step = 0
                for n in range(-(-n_cols // WBLK)):
                    cols = min(WBLK, n_cols - n * WBLK)
                    w = wait_weights(pe, name, n)
                    for t in tiles_of(n):
                        j = 4 + step % 2
                        step += 1
                        b = open_bank(pe, (name, n, t), j)
                        for k in range(KC):
                            mm = pe.matmul(b[:, 0:cols], src[:, k, t * P:(t + 1) * P], w[:, k, 0:cols],
                                           start=(k == 0), stop=(k == KC - 1))
                        mm.then_inc(bank_filled[j], 1)
                    weights_done[name, n] = turn[name, n, t]

            def mix_out(layer, tiles, srcT):
                name = f"out{layer}"
                w = [wait_weights(pe, name, n) for n in range(2)]
                for t in range(tiles):
                    for n in range(2):
                        b = open_bank(pe, (name, n, t), 4 + n)
                        for k in range(KC):
                            mm = pe.matmul(b[:, :], srcT[:, k, t * P:(t + 1) * P], w[n][:, k, :],
                                           start=(k == 0), stop=(k == KC - 1))
                        mm.then_inc(bank_filled[4 + n], 1)
                        weights_done[name, n] = turn[name, n, t]
                    if t == 0:
                        turn_keys(layer)
                    else:
                        turn_tile(f"fT{layer}", ffn_in, t - 1)

            def attention():
                for t in range(TILES):
                    pe.wait_ge(qk_ready, t + 1)
                    for g in range(3):
                        j = (3 * t + g) % 4
                        b = open_bank(pe, ("qkT", t, g), j)
                        for k in range(4):
                            if g < 2:
                                c0 = g * B_OFF + k * P
                                src = proj[:, t, c0:c0 + P]
                            else:
                                src = kdup[:, t % 2, k, :]
                            mm = pe.transpose(b[:, k * P:(k + 1) * P], src, ident)
                        mm.then_inc(bank_filled[j], 1)
                for g in range(8, 3 * TILES):
                    wait_drained(pe, ("qkT", g // 3, g % 3))
                for i in range(len(attn_steps) + 3):
                    if i < len(attn_steps) and i % 2 == 0:
                        for n in range(i, i + 2):
                            t, hd = attn_steps[n]
                            kind, hh = divmod(hd, HEADS_A)
                            rows = slice(HEAD_DIM * (hh % 2), HEAD_DIM * (hh % 2) + HEAD_DIM)
                            k0 = 0 if t < LAT_TILES else SEQ
                            j = n % 4
                            b = open_bank(pe, ("s", n), j)
                            pe.matmul(b[:, 0:TILES * P - k0], qkT[rows, kind * 4 + hh // 2, t * P:(t + 1) * P],
                                      qkT[rows, 8 + kind * 2 + hh // KV_GROUP, k0:TILES * P],
                                      start=True, stop=True).then_inc(bank_filled[j], 1)
                    if 2 <= i < len(attn_steps) + 2:
                        m = i - 2
                        nk = TILES if attn_steps[m][0] < LAT_TILES else LAT_TILES
                        j = 6 + m % 2
                        b = open_bank(pe, ("pT", m), j)
                        wait_drained(pe, ("s", m))
                        for k in range(nk):
                            mm = pe.transpose(b[:, k * P:(k + 1) * P], probs[:, m % PROB_BUFS, k * P:(k + 1) * P], ident)
                        mm.then_inc(bank_filled[j], 1)
                    if i >= 3:
                        m = i - 3
                        t, hd = attn_steps[m]
                        kind, hh = divmod(hd, HEADS_A)
                        nk = TILES if t < LAT_TILES else LAT_TILES
                        vcol = kind * B_OFF + 640 + (hh // KV_GROUP) * HEAD_DIM
                        j = 4 + m % 2
                        b = open_bank(pe, ("o", m), j)
                        wait_drained(pe, ("pT", m))
                        for k in range(nk):
                            mm = pe.matmul(b[:, 0:HEAD_DIM], probsT[:, m % PROB_BUFS, k * P:(k + 1) * P],
                                           proj[:, TILES - nk + k, vcol:vcol + HEAD_DIM],
                                           start=(k == 0), stop=(k == nk - 1))
                        mm.then_inc(bank_filled[j], 1)

            def gla():
                pe.wait_ge(pool_loads, gla_loads)
                for d in range(2):
                    b = open_bank(pe, ("gateT", d), d)
                    for t in range(TILES):
                        mm = pe.transpose(b[0:RANK, t * P:(t + 1) * P], gate_low[:, t, d * RANK:(d + 1) * RANK], ident)
                    mm.then_inc(bank_filled[d], 1)
                for d in range(2):
                    wait_drained(pe, ("gateT", d))
                for d in range(2):
                    for t in range(TILES):
                        j = t % 2
                        b = open_bank(pe, ("z", d, t), j)
                        pe.matmul(b[:, :], gate_lowT[0:RANK, d, t * P:(t + 1) * P], gate_w[0:RANK, d, :],
                                  start=True, stop=True).then_inc(bank_filled[j], 1)
                for d in range(2):
                    c_incl, c_rest = (C_UPPER, C_LOWER)[d], (C_LOWER_STRICT, C_UPPER_STRICT)[d]
                    for t in range(TILES):
                        pe.wait_ge(decay_ready, count.next("decay"))
                        if t < LAT_TILES:
                            b = open_bank(pe, ("b", d, t), 2)
                            pe.matmul(b[:, :], cst[:, c_incl:c_incl + P], log_decay(d, t),
                                      start=True, stop=True).then_inc(bank_filled[2], 1)
                        b = open_bank(pe, ("rest", d, t), 3)
                        pe.matmul(b[:, :], cst[:, c_rest:c_rest + P], log_decay(d, t),
                                  start=True, stop=True).then_inc(bank_filled[3], 1)
                    b = open_bank(pe, ("end", d), 4)
                    for hh in range(GLA_HEADS):
                        for t in range(TILES):
                            c0 = (hh * TILES + t) * 2
                            mm = pe.matmul(b[:, c0:c0 + 2], log_decay(d, t)[:, hh * DK:(hh + 1) * DK],
                                           cst[:, C_CHUNK:C_CHUNK + 2], start=True, stop=True)
                    mm.then_inc(bank_filled[4], 1)
                    pe.wait_ge(keyed_ready, count.next("keyed", TILES))
                    for t in range(LAT_TILES):
                        for which, src in enumerate((q_dec, k_inv)):
                            j = 5 + which
                            b = open_bank(pe, ("qkdT", d, t, which), j)
                            for hh in range(GLA_HEADS):
                                mm = pe.transpose(b[:, hh * P:(hh + 1) * P], src[:, t, hh * DK:(hh + 1) * DK], ident)
                            mm.then_inc(bank_filled[j], 1)
                    for n, (hh, kind, chunk, _) in enumerate(gla_updates(d)):
                        t, r = divmod(chunk, 2)
                        rows = slice(CHUNK * r, CHUNK * r + CHUNK)
                        j = n % 4
                        b = open_bank(pe, ("kv", d, n), j)
                        if kind == "ctx":
                            v = gla_ctx[rows, t, KD + hh * DV:KD + (hh + 1) * DV]
                            t += LAT_TILES
                        else:
                            v = gla_lat[rows, t, 2 * KD + hh * DV:2 * KD + (hh + 1) * DV]
                        pe.matmul(b[:, 0:DV], k_end[rows, t, hh * DK:(hh + 1) * DK], v,
                                  start=True, stop=True).then_inc(bank_filled[j], 1)
                    for which in range(2):
                        wait_drained(pe, ("qkdT", d, LAT_TILES - 1, which))
                    pe.wait_ge(state_ready, count.next("state", len(gla_updates(d))))
                    for i in range(len(gla_jobs) + 1):
                        if i < len(gla_jobs):
                            t, hh = gla_jobs[i]
                            j = 2 + i % 2
                            b = open_bank(pe, ("att", d, i), j)
                            cols = slice(t * P, (t + 1) * P)
                            pe.matmul(b[:, 0:P], k_invT[:, hh, cols], q_decT[:, hh, cols],
                                      start=True, stop=True).then_inc(bank_filled[j], 1)
                        if i >= 1:
                            m = i - 1
                            t, hh = gla_jobs[m]
                            j = 4 + m % 2
                            b = open_bank(pe, ("go", d, m), j)
                            pe.wait_ge(masked_ready, count.next("masked"))
                            pe.matmul(b[:, 0:DV], att_masked[:, 2 * d + m % 2, :],
                                      gla_lat[:, t, 2 * KD + hh * DV:2 * KD + (hh + 1) * DV],
                                      start=True, stop=False, skip_group_check=True)
                            for r in range(2):
                                c0 = t * P + r * CHUNK
                                mm = pe.matmul(b[r * CHUNK:(r + 1) * CHUNK, 0:DV], q_decT[:, hh, c0:c0 + CHUNK],
                                               states[:, hh, 2 * t + r, :], start=False, stop=True,
                                               skip_group_check=True)
                            mm.then_inc(bank_filled[j], 1)

            def turn_keys(layer):
                pe.wait_ge(pool_loads, key_loads[layer])
                for g in range(4):
                    j = 6 + g % 2
                    b = open_bank(pe, ("keysT", layer, g), j)
                    for k in range(4):
                        mm = pe.transpose(b[:, k * P:(k + 1) * P], keys[layer][:, 4 * g + k, :], ident)
                    mm.then_inc(bank_filled[j], 1)

            def wait_query(head, layer):
                pe.wait_ge(query_loaded, head * 16 + (layer * PEER_HEADS + 1) * 16)

            def query_product(step, tile, slot):
                if not (isinstance(step, int) and step == 0):
                    pe.wait_ge(query_rows_ready, step)
                for k in range(KC):
                    w = query_w[:, slot, k, :]
                    mm = pe.matmul(bank[4][:, 0:2 * P], ffn_inT[:, k, tile * P:(tile + 1) * P],
                                   w if isinstance(slot, int) else w.rearrange("p a n -> p (a n)"),
                                   start=(k == 0), stop=(k == KC - 1))
                mm.then_inc(query_done, 1)

            def combine_start(g):
                pe.wait_ge(y_free, g)

            def combine(step, par, k):
                pe.wait_ge(v_in[k % RING], step * 32 + 16 * (k // RING + 1))
                pe.wait_ge(diag_ready, step * TOPK + (k + 1))
                for half in range(2):
                    mm = pe.matmul(bank[2 * par + half][:, :], diag[:, k % DIAGS, :],
                                   v_rows[:, k % RING, half * WBLK:(half + 1) * WBLK],
                                   start=(k == 0), stop=(k == TOPK - 1), skip_group_check=True)
                mm.then_inc(v_free, 1)

            def query_turn(step):
                pe.wait_ge(query_rows_ready, step + 1)
                for half in range(2):
                    mm = pe.transpose(bank[5][:, half * P:(half + 1) * P], query_rows[:, half, :], ident)
                mm.then_inc(query_turned, 1)

            def query_scores(step, head, par):
                pe.wait_ge(queryT_ready, step + 1)
                if not (isinstance(step, int) and step < 2):
                    pe.wait_ge(head_scores_ready, step + (-1))
                for half in range(2):
                    mm = pe.matmul(bank[6 + par][:, half * P:(half + 1) * P], queryT[:, half, :],
                                   keysT[:, bass.ds(head * 2 + half, 1), :].rearrange("p a b -> p (a b)"),
                                   start=True, stop=True)
                mm.then_inc(scores_done, 1)

            def experts(layer, tiles):
                base = layer * GATHER_LAYER_STEPS
                last = PEER_HEADS - 1

                def body(head, hpar, t, prev, nxt):
                    g = head * tiles + (base + t)
                    j, jt = g + 2, (t + 2) % tiles
                    carry = (t + 2) // tiles
                    jhead = head + carry
                    slot = jhead % 2 if isinstance(head, int) else bass.ds(jhead & 1, 1)
                    if prev:
                        combine_start(g)
                        for k in range(0, 4):
                            combine(g + (-1), 1 - t % 2, k)
                    if nxt:
                        if jt == 0:
                            wait_query(jhead, layer)
                        query_product(j, jt, slot)
                    if prev:
                        for k in range(4, 9):
                            combine(g + (-1), 1 - t % 2, k)
                    if nxt:
                        query_turn(j)
                    if prev:
                        for k in range(9, 14):
                            combine(g + (-1), 1 - t % 2, k)
                    if nxt:
                        query_scores(j, jhead, t % 2)
                    if prev:
                        for k in range(14, TOPK):
                            combine(g + (-1), 1 - t % 2, k)

                if layer == 0:
                    pe.sem_inc(v_free, RING)
                for n in range(2):
                    wait_drained(pe, (f"out{layer}", n, tiles - 1))
                    wait_drained(pe, ("keysT", layer, 2 + n))
                wait_query(0, layer)
                for t in range(2):
                    if t == 1:
                        turn_tile(f"fT{layer}", ffn_in, tiles - 1)
                    for half in range(2):
                        wait_drained(pe, (f"fT{layer}", t, half))
                    query_product(base + t, t, 0)
                    query_turn(base + t)
                    query_scores(base + t, 0, t)
                for key in last_four(f"fT{layer}", tiles):
                    wait_drained(pe, key)
                for t in range(tiles):
                    body(0, 0, t, t > 0, True)
                with pe.Fori(1, last) as head:
                    for t in range(tiles):
                        body(head, None, t, True, True)
                for t in range(tiles):
                    body(last, 1, t, True, t + 2 < tiles)
                g = base + tiles * PEER_HEADS
                combine_start(g)
                for k in range(TOPK):
                    combine(g - 1, 1, k)

            def program():
                conditions()
                turn_rows("hT0", h, TILES)
                project("attn_in", hT0, ATTN_IN, lambda n: range(TILES))
                attention()
                turn_rows("oT0", h, TILES)
                mix_out(0, TILES, hT)
                experts(0, TILES)
                if end_stage("pe", pe):
                    return
                turn_rows("hT1", h_gla, TILES)
                project("gla_in", gla_hT, GLA_IN, gla_tiles)
                if end_stage("pe", pe):
                    return
                gla()
                turn_rows("oT1", gla_o, LAT_TILES)
                mix_out(1, LAT_TILES, gla_hT)
                experts(1, LAT_TILES)
                end_stage("pe", pe)

            program()

        @block.sync
        def _(sp):
            sp.dma_start(cst[:, :], consts).then_inc(cond_in_ready, 16)
            sp.dma_start(cond_in[0:KC, :], c.rearrange("b (k p) -> (b k) p", p=P)).then_inc(cond_in_ready, 16)
            sp.dma_start(cond_in[KC:2 * KC, :], c_ctx.rearrange("(k p) -> k p", p=P)).then_inc(cond_in_ready, 16)

            def load_query(layer, tiles, head, slot):
                src = peer_wq[layer].rearrange("(k p) n -> p k n", p=P)[:, :, bass.ds(head * 2 * P, 2 * P)]
                sp.wait_ge(query_loaded, head * 16 + layer * PEER_HEADS * 16)
                sp.dma_start(query_w[:, slot, :, :], src).then_inc(query_loaded, 16)

            def queries(layer, tiles):
                base = layer * GATHER_LAYER_STEPS
                if layer == 0:
                    j, m = weights_done[blocks[n_ada - 1][0], blocks[n_ada - 1][1]]
                    sp.wait_ge(bank_filled[j], m + 1)
                for head in range(2):
                    src = peer_wq[layer].rearrange("(k p) n -> p k n", p=P)[:, :, head * 2 * P:(head + 1) * 2 * P]
                    if layer + head:
                        sp.wait_ge(query_loaded, 16 * (layer * PEER_HEADS + head))
                    if layer:
                        sp.wait_ge(query_done, base)
                    sp.dma_start(query_w[:, head, :, :], src).then_inc(query_loaded, 16)
                with sp.Fori(1, PEER_HEADS // 2) as pair:
                    for slot in range(2):
                        sp.wait_ge(query_done, pair * (2 * tiles) + (base + (slot - 1) * tiles))
                        load_query(layer, tiles, pair * 2 + slot, slot)

            for n, (name, b, src, cols) in enumerate(blocks):
                if (name, b) not in weights_done:
                    break
                before = slot_before[n]
                if before is not None:
                    j, m = weights_done[blocks[before][0], blocks[before][1]]
                    sp.wait_ge(bank_filled[j], m + 1)
                sp.dma_start(wring[:, slot_of[n], :, 0:cols], src).then_inc(w_loaded[slot_of[n]], 16)
                if (name, b) == ("out0", 1) and stop >= 1:
                    queries(0, TILES)
                if (name, b) == ("out1", 1) and stop >= 3:
                    queries(1, LAT_TILES)

        @block.scalar
        def _(act):
            steps = Steps(act, act_step)
            count = Count()

            def conditions():
                wait_bank(act, "cond")
                act.activation(cond_tmp, bank[7][:, 0:2 * KC], ACT.Exp, scale=-1.0).then_inc(cond_exp_ready, 1)

            def sum_squares(srcs, junk, n, first=0):
                for i in range(first, first + n):
                    ins = act.activation(junk(i), srcs(i), ACT.Square, accum_out=stat[:, i:i + 1])
                ins.then_inc(sumsq_ready, 1)
                act.wait_ge(mean_ready, count.next("mean"))
                act.activation(stat[:, 16 + first:16 + first + n], stat[:, 8 + first:8 + first + n],
                               ACT.Sqrt).then_inc(root_ready, 1)

            def tile_squares(dst, t):
                sum_squares(lambda i: xs[:, i, :], lambda i: dst[:, i, :], 1, t)

            def turn_tile(name, dst, t):
                for half in range(2):
                    b = wait_bank(act, (name, t, half))
                    act.activation(dst[:, 4 * half:4 * half + 4, t * P:(t + 1) * P],
                                   bank[b][:, :].rearrange("p (k n) -> p k n", k=4),
                                   ACT.Copy).then_inc(bank_drained[b], 1)

            def turn_rows(name, dst, tiles):
                for t in range(tiles):
                    turn_tile(name, dst, t)

            def mix_out(layer, tiles):
                turn_keys(layer)
                for t in range(tiles):
                    if t >= 1:
                        turn_tile(f"fT{layer}", ffn_inT, t - 1)
                    act.wait_ge(residual_ready, layer * TILES + t + 1)
                    tile_squares(ffn_in, t)

            def attn_in():
                for n in range(ATTN_IN // WBLK):
                    for t in range(TILES):
                        b = wait_bank(act, ("attn_in", n, t))
                        act.activation(proj[:, t, n * WBLK:(n + 1) * WBLK], bank[b][:, :],
                                       ACT.Copy).then_inc(bank_drained[b], 1)
                        if n == 2 and t >= 1:
                            head_roots(t - 1)
                head_roots(TILES - 1)

            def head_roots(t):
                heads = slice(10 * t, 10 * t + 10)
                act.wait_ge(mean_ready, count.next("mean"))
                act.activation(qk_stat[:, 2, heads], qk_stat[:, 1, heads], ACT.Sqrt).then_inc(root_ready, 1)

            def attention():
                for t in range(TILES):
                    for g in range(3):
                        b = wait_bank(act, ("qkT", t, g))
                        act.activation(qkT[:, 4 * g:4 * g + 4, t * P:(t + 1) * P],
                                       bank[b][:, :].rearrange("p (k n) -> p k n", k=4),
                                       ACT.Copy).then_inc(bank_drained[b], 1)
                for i in range(len(attn_steps) + 2):
                    if i < len(attn_steps):
                        t, hd = attn_steps[i]
                        nk = TILES if t < LAT_TILES else LAT_TILES
                        act.wait_ge(att_max, i + 1)
                        if i >= PROB_BUFS:
                            wait_bank(act, ("pT", i - PROB_BUFS))
                        b = turn["s", i][0]
                        ins = act.activation(probs[:, i % PROB_BUFS, 0:nk * P], bank[b][:, 0:nk * P], ACT.Exp,
                                             bias=att_stat[:, i % 4, 1:2], scale=ATTN_SCALE,
                                             accum_out=att_stat[:, i % 4, 2:3])
                        ins.then_inc(bank_drained[b], 1)
                        if hd < HEADS_A:
                            act.activation(att_stat[:, i % 4, 3:4], sinks[:, hd:hd + 1], ACT.Exp,
                                           bias=att_stat[:, i % 4, 1:2]).then_inc(sink_exp, 1)
                    if i >= 2:
                        m = i - 2
                        nk = TILES if attn_steps[m][0] < LAT_TILES else LAT_TILES
                        if m >= PROB_BUFS:
                            wait_bank(act, ("o", m - PROB_BUFS))
                        b = wait_bank(act, ("pT", m))
                        act.activation(probsT[:, m % PROB_BUFS, 0:nk * P], bank[b][:, 0:nk * P],
                                       ACT.Copy).then_inc(bank_drained[b], 1)

            def gla_in():
                for n in range(-(-GLA_IN // WBLK)):
                    for t in gla_tiles(n):
                        b = wait_bank(act, ("gla_in", n, t))
                        if n == 6:
                            dst, cols = gate_low[:, t, :], 2 * RANK
                        elif t < LAT_TILES:
                            dst, cols = gla_lat[:, t, n * WBLK:(n + 1) * WBLK], WBLK
                        else:
                            dst, cols = gla_ctx[:, t - LAT_TILES, (n - 1) * WBLK:n * WBLK], WBLK
                        act.activation(dst, bank[b][:, 0:cols], ACT.Copy).then_inc(bank_drained[b], 1)

            def gla():
                for d in range(2):
                    b = wait_bank(act, ("gateT", d))
                    act.activation(gate_lowT[0:RANK, d, :], bank[b][0:RANK, :], ACT.Copy).then_inc(bank_drained[b], 1)
                for d in range(2):
                    z = [gate_tmp[:, (TILES * d + t) % GATE_BUFS, :] for t in range(TILES)]
                    for t in range(TILES):
                        act.wait_ge(gate_z, count.next("z"))
                        steps.link(act.activation(z[t], z[t], ACT.Exp, scale=-1.0))
                    for t in range(TILES):
                        act.activation(z[t], z[t], ACT.Ln, bias=1.0).then_inc(gate_ln, 1)
                for d in range(2):
                    for t in range(TILES):
                        if t < LAT_TILES:
                            b = wait_bank(act, ("b", d, t))
                            act.activation(q_dec[:, t, :], bank[b][:, :], ACT.Exp).then_inc(exp_ready, 1)
                            act.activation(k_inv[:, t, :], bank[b][:, :], ACT.Exp,
                                           scale=-1.0).then_inc(bank_drained[b], 1)
                        b = wait_bank(act, ("rest", d, t))
                        act.activation(k_end[:, t, :], bank[b][:, :], ACT.Exp).then_inc(bank_drained[b], 1)
                    if d == 0:
                        for t in range(LAT_TILES):
                            act.activation(silu_r[:, t, :], gla_lat[:, t, 2 * KD + VD:2 * KD + 2 * VD], ACT.Exp,
                                           scale=-1.0).then_inc(silu_exp, 1)
                    b = wait_bank(act, ("end", d))
                    act.activation(decay_end.rearrange("p a b c -> p (a b c)"), bank[b][:, 0:32],
                                   ACT.Exp).then_inc(bank_drained[b], 1)
                    for t in range(LAT_TILES):
                        for which, dst in enumerate((q_decT, k_invT)):
                            b = wait_bank(act, ("qkdT", d, t, which))
                            act.activation(dst[:, :, t * P:(t + 1) * P],
                                           bank[b][:, :].rearrange("p (k n) -> p k n", k=4),
                                           ACT.Copy).then_inc(bank_drained[b], 1)
                for t in range(LAT_TILES):
                    wait_drained(act, ("go", 1, (t + 1) * GLA_HEADS - 1))
                    sum_squares(lambda i: gla_o[:, t, (i % GLA_HEADS) * DV:(i % GLA_HEADS + 1) * DV],
                                lambda i: squares_junk[:, t, (i % GLA_HEADS) * DV:(i % GLA_HEADS + 1) * DV],
                                GLA_HEADS, t * GLA_HEADS)

            def turn_keys(layer):
                for g in range(4):
                    b = wait_bank(act, ("keysT", layer, g))
                    act.activation(keysT[:, 4 * g:4 * g + 4, :].rearrange("p a b -> p (a b)"), bank[b][:, :],
                                   ACT.Copy).then_inc(bank_drained[b], 1)

            def experts(layer, tiles):
                base = layer * GATHER_LAYER_STEPS
                last = PEER_HEADS - 1

                def copy_query(j):
                    act.wait_ge(query_done, j + 1)
                    act.activation(query_rows.rearrange("p a b -> p (a b)"), bank[4][:, 0:2 * P],
                                   ACT.Copy).then_inc(query_rows_ready, 1)

                def copy_queryT(j):
                    act.wait_ge(query_turned, j + 1)
                    act.activation(queryT.rearrange("p a b -> p (a b)"), bank[5][:, 0:2 * P],
                                   ACT.Copy).then_inc(queryT_ready, 1)

                def copy_scores(j, par, first):
                    act.wait_ge(scores_done, j + 1)
                    if not first:
                        act.wait_ge(idx_u_ready, j + (-1))
                    act.activation(head_scores[:, par, :], bank[6 + par][:, 0:2 * P],
                                   ACT.Copy).then_inc(head_scores_ready, 1)

                def gate(g, par):
                    act.wait_ge(best_ready, g + 1)
                    act.activation(gate_num[:, par, :], best[:, par, :], ACT.Exp, bias=neg_best[:, par:par + 1],
                                   accum_out=gate_sum[:, par:par + 1]).then_inc(gate_num_ready, 1)

                def gelu(g, par):
                    act.wait_ge(u_free, (g + 1) * TOPK + RING)
                    act.activation(act_gelu[:, par, :], act_raw[:, par, :], ACT.Gelu).then_inc(gelu_ready, 1)

                def diags(g, par, first, end):
                    for k in range(first, end):
                        act.wait_ge(v_free, g * TOPK + (k + 1 - DIAGS + RING))
                        act.activation(diag[:, k % DIAGS, :], ident, ACT.Copy,
                                       scale=pick_weight[:, par, k:k + 1]).then_inc(diag_ready, 1)

                def body(head, t, prev, nxt, query):
                    g, par = head * tiles + (base + t), t % 2
                    if nxt:
                        copy_scores(g + 1, 1 - par, isinstance(head, int) and base + head * tiles + t == 0)
                    if prev:
                        gelu(g + (-1), 1 - par)
                        act.wait_ge(weight_ready, g)
                        diags(g + (-1), 1 - par, 0, 7)
                    if query:
                        copy_query(g + 2)
                    if prev:
                        diags(g + (-1), 1 - par, 7, 12)
                    if query:
                        copy_queryT(g + 2)
                    if prev:
                        diags(g + (-1), 1 - par, 12, TOPK)
                    if nxt:
                        gate(g + 1, 1 - par)

                for t in range(2):
                    if t == 1:
                        turn_tile(f"fT{layer}", ffn_inT, tiles - 1)
                    copy_query(base + t)
                    copy_queryT(base + t)
                    if t == 0:
                        copy_scores(base, 0, base == 0)
                gate(base, 0)
                for t in range(tiles):
                    body(0, t, t > 0, True, True)
                with act.Fori(1, last) as head:
                    for t in range(tiles):
                        body(head, t, True, True, True)
                for t in range(tiles):
                    body(last, t, True, t + 1 < tiles, t + 2 < tiles)
                g = base + tiles * PEER_HEADS
                gelu(g - 1, 1)
                act.wait_ge(weight_ready, g)
                diags(g - 1, 1, 0, TOPK)

            def program():
                conditions()
                act.wait_ge(pool_loads, first_loads)
                for t in range(TILES):
                    tile_squares(h, t)
                turn_rows("hT0", hT0, TILES)
                attn_in()
                attention()
                turn_rows("oT0", hT, TILES)
                mix_out(0, TILES)
                experts(0, TILES)
                if end_stage("act", act):
                    return
                for t in range(TILES):
                    tile_squares(h_gla, t)
                turn_rows("hT1", gla_hT, TILES)
                gla_in()
                if end_stage("act", act):
                    return
                gla()
                turn_rows("oT1", gla_hT, LAT_TILES)
                mix_out(1, LAT_TILES)
                experts(1, LAT_TILES)
                end_stage("act", act)
                sum_squares(lambda t: xs[:, t, :], lambda t: ffn_in[:, t, :], LAT_TILES)

            program()

        @block.gpsimd
        def _(pool):
            steps = Steps(pool, pool_step)
            link = steps.link

            def load(dst, src):
                pool.dma_start(dst, src).then_inc(pool_loads, 16)

            def row(src, n, parts=P):
                return src.rearrange("(a n) -> a n", a=1).to_broadcast((parts, n))

            def modulation(layer, section, conds, gate):
                for cond in range(conds):
                    src = mod_dram[cond, layer, section:section + 2, :].rearrange("a b -> (a b)")
                    load(mod_rows[:, cond, :, :].rearrange("p a b -> p (a b)"), row(src, 2 * D))
                    load(gate_rows[:, cond, :], row(mod_dram[cond, layer, gate, :], D))

            def shift_and_scale(layer, section, cond):
                src = mod_dram[cond, layer, section:section + 2, :].rearrange("a b -> (a b)")
                load(mod_rows[:, cond, :, :].rearrange("p a b -> p (a b)"), row(src, 2 * D))

            def gate(layer, section, cond):
                pool.dma_start(gate_rows[:, cond, :], row(mod_dram[cond, layer, section, :], D)).then_inc(gate_loads, 16)

            def expert_loads(layer, conds):
                for cond in range(conds):
                    shift_and_scale(layer, 3, cond)
                load(keys[layer], peer_keys[layer].rearrange("h s n d -> n (h s) d"))
                pool.wait_ge(residual_ready, (TILES, TILES + LAT_TILES)[layer])
                for cond in range(conds):
                    gate(layer, 5, cond)

            def silu():
                pool.wait_ge(pool_loads, gla_loads)
                for t in range(LAT_TILES):
                    e = silu_r[:, t, :]
                    pool.wait_ge(sigmoid_ready, t + 1)
                    link(pool.tensor_tensor(e, e, gla_lat[:, t, 2 * KD + VD:2 * KD + 2 * VD], ALU.mult))
                    heads = e.rearrange("p (h n) -> p h n", h=GLA_HEADS)
                    pool.tensor_tensor(heads, heads, head_gain.unsqueeze(1).to_broadcast([P, GLA_HEADS, DV]),
                                       ALU.mult).then_inc(silu_ready, 1)

            def experts(layer, tiles):
                base = layer * GATHER_LAYER_STEPS
                last = PEER_HEADS - 1

                def gather_u(g, par, k):
                    pool.wait_ge(u_free, g * TOPK + (k + 1))
                    hold(pool)
                    pool.indirect_dma_start(u_rows[:, k % RING, :], None, expert_u,
                                            bass.IndirectOffsetOnAxis(idx_u[:, par, k:k + 1], 0)
                                            ).then_inc(u_in[k % RING], 16)

                def gather_v(g, par, k):
                    pool.wait_ge(v_free, g * TOPK + (k + 1))
                    hold(pool)
                    pool.indirect_dma_start(v_rows[:, k % RING, :], None, expert_v,
                                            bass.IndirectOffsetOnAxis(idx_v[:, par, k:k + 1], 0)
                                            ).then_inc(v_in[k % RING], 16)

                def body(g, par):
                    pool.wait_ge(idx_u_ready, g + 1)
                    pool.wait_ge(idx_v_ready, g)
                    for k in range(TOPK):
                        gather_u(g, par, k)
                        gather_v(g + (-1), 1 - par, k)

                def heads_steps(head, first):
                    for t in range(first, tiles):
                        body(head * tiles + (base + t), t % 2)

                pool.wait_ge(idx_u_ready, base + 1)
                if layer == 0:
                    shift_and_scale(1, 0, 0)
                else:
                    load(mod_rows[:, 0, 0, :], row(final_norm, D))
                for k in range(TOPK):
                    gather_u(base, 0, k)
                heads_steps(0, 1)
                with pool.Fori(1, last + 1) as head:
                    heads_steps(head, 0)
                n = base + tiles * PEER_HEADS
                pool.wait_ge(idx_v_ready, n)
                for k in range(TOPK):
                    gather_v(n - 1, 1, k)

            def program():
                load(mods[0:2, :], row(ada_b.rearrange("l n -> (l n)"), LAYERS * MOD_DIM, 2))
                load(norm_gains[0:2, 0:2, :].rearrange("p a b -> p (a b)"),
                     row(norm_mix.rearrange("l n -> (l n)"), LAYERS * D, 2))
                load(norm_gains[0:2, 2:4, :].rearrange("p a b -> p (a b)"),
                     row(norm_ffn.rearrange("l n -> (l n)"), LAYERS * D, 2))
                load(xs[:, 0:LAT_TILES, :], x[0].rearrange("(t p) d -> p t d", p=P))
                load(xs[:, LAT_TILES:TILES, :], ctx[0].rearrange("(t p) d -> p t d", p=P))
                for layer in range(LAYERS):
                    pool.wait_ge(mods_ready, layer + 1)
                    pool.dma_start(mod_dram[:, layer, :, :].rearrange("c s d -> c (s d)"),
                                   mods[0:2, layer * MOD_DIM:(layer + 1) * MOD_DIM]).then_inc(stored, 16)
                    pool.wait_ge(stored, 16 * (layer + 1))
                    if layer == 0:
                        modulation(0, 0, 2, 2)
                load(qk_gain[:, 0, :], row(attn_q_gain[0], HEAD_DIM))
                load(qk_gain[:, 1, :], row(attn_k_gain[0], HEAD_DIM))
                load(sinks, row(attn_sink[0], HEADS_A))
                wait_bank(pool, ("pT", len(attn_steps) - 1))
                expert_loads(0, 2)
                experts(0, TILES)
                if end_stage("pool", pool):
                    return
                shift_and_scale(1, 0, 1)
                for cond in range(2):
                    gate(1, 2, cond)
                wait_bank(pool, ("hT1", TILES - 1, 1))
                load(gate_w[0:RANK, :, :], gla_gate_w[0].rearrange("d r n -> r d n"))
                load(gate_bias.rearrange("p a b -> p (a b)"), row(gla_gate_b[0].rearrange("d n -> (d n)"), 2 * KD))
                load(head_gain, row(gla_head_gain[0], DV))
                if end_stage("pool", pool):
                    return
                silu()
                pool.wait_ge(normed_ready, LAT_TILES)
                expert_loads(1, 1)
                experts(1, LAT_TILES)
                end_stage("pool", pool)
                pool.wait_ge(h_ready, final_rows)
                pool.dma_start(out[0].rearrange("(t p) d -> p t d", p=P), ffn_in[:, 0:LAT_TILES, :]).then_inc(stored, 16)
                pool.wait_ge(stored, 16 * (LAYERS + 1))

            program()

        @block.vector
        def _(dve):
            steps = Steps(dve, dve_step)
            link = steps.link
            count = Count()

            def conditions():
                dve.wait_ge(cond_exp_ready, 1)
                link(dve.tensor_scalar_add(cond_tmp, cond_tmp, 1.0))
                link(dve.reciprocal(cond_tmp, cond_tmp))
                dve.tensor_tensor(cond_act, bank[7][:, 0:2 * KC], cond_tmp, ALU.mult).then_inc(cond_ready, 1)
                dve.wait_ge(cond_ready, 1)
                dve.sem_inc(bank_drained[7], 1)

            def modulation(layer):
                dve.wait_ge(pool_loads, cond_loads)
                for n in range(MOD_DIM // WBLK):
                    b = wait_bank(dve, ("ada", layer, n))
                    cols = mods[0:2, layer * MOD_DIM + n * WBLK:layer * MOD_DIM + (n + 1) * WBLK]
                    dve.tensor_tensor(cols, bank[b][0:2, :], cols, ALU.add).then_inc(bank_drained[b], 1)
                    wait_drained(dve, ("ada", layer, n))
                for section, gains in ((1, 0), (4, 2)):
                    c0 = layer * MOD_DIM + section * D
                    link(dve.scalar_tensor_tensor(mods[0:2, c0:c0 + D], mods[0:2, c0:c0 + D], 1.0,
                                                  norm_gains[0:2, gains + layer, :], ALU.add, ALU.mult))
                dve.sem_inc(mods_ready, 1)

            def inverse_root(n, width, first=0):
                dve.wait_ge(sumsq_ready, count.next("sumsq"))
                dve.tensor_scalar(stat[:, 8 + first:8 + first + n], stat[:, first:first + n], 1.0 / width, EPS,
                                  ALU.mult, ALU.add).then_inc(mean_ready, 1)
                dve.wait_ge(root_ready, count.next("root"))
                link(dve.reciprocal(stat[:, 24 + first:24 + first + n], stat[:, 16 + first:16 + first + n]))

            def modulate(dst, tiles, loads):
                for t in range(tiles):
                    modulate_tile(dst, t, loads)

            def modulate_tile(dst, t, loads):
                inverse_root(1, D, t)
                cond = t // LAT_TILES
                dve.wait_ge(pool_loads, loads[cond])
                link(dve.scalar_tensor_tensor(dst[:, t, :], xs[:, t, :], stat[:, 24 + t:25 + t],
                                              mod_rows[:, cond, 1, :], ALU.mult, ALU.mult))
                dve.tensor_tensor(dst[:, t, :], dst[:, t, :], mod_rows[:, cond, 0, :],
                                  ALU.add).then_inc(h_ready, 1)

            def rotate(rows, t):
                heads = rows.rearrange("p (h a s r) -> p (h a) s r", h=10, a=2, s=2)
                swap = swapped.rearrange("p (h a s r) -> p (h a) s r", h=10, a=2, s=2)
                for s in range(2):
                    ins = dve.tensor_copy(swap[:, :, s, :], heads[:, :, 1 - s, :])
                link(ins)
                w = HEAD_DIM
                cos = cst[:, C_COS + t * w:C_COS + (t + 1) * w].unsqueeze(1).to_broadcast([P, 10, w])
                sin = cst[:, C_SIN + t * w:C_SIN + (t + 1) * w].unsqueeze(1).to_broadcast([P, 10, w])
                by_head = rows.rearrange("p (h n) -> p h n", h=10)
                sw = swapped.rearrange("p (h n) -> p h n", h=10)
                dve.tensor_tensor(by_head, by_head, cos, ALU.mult)
                link(dve.tensor_tensor(sw, sw, sin, ALU.mult))
                link(dve.tensor_tensor(by_head, by_head, sw, ALU.add))

            def queries_and_keys():
                dve.wait_ge(pool_loads, attn_loads)
                dve.wait_ge(stored, 16 * LAYERS)
                for t in range(LAT_TILES):
                    wait_drained(dve, ("attn_in", 1, t))
                    rotate(proj[:, t, 0:640], t)
                for t in range(TILES):
                    wait_drained(dve, ("attn_in", 2, t))
                    flat = proj[:, t, B_OFF:B_OFF + 640]
                    rows = flat.rearrange("p (h n) -> p h n", h=10)
                    heads = slice(10 * t, 10 * t + 10)
                    link(dve.tensor_tensor(squares, flat, flat, ALU.mult))
                    link(dve.tensor_reduce(qk_stat[:, 0, heads], squares.rearrange("p (h n) -> p h n", h=10),
                                           AX_X, ALU.add))
                    dve.tensor_scalar(qk_stat[:, 1, heads], qk_stat[:, 0, heads], 1.0 / HEAD_DIM, EPS, ALU.mult,
                                      ALU.add).then_inc(mean_ready, 1)
                    dve.wait_ge(root_ready, count.next("root"))
                    link(dve.reciprocal(qk_stat[:, 3, heads], qk_stat[:, 2, heads]))
                    link(dve.tensor_tensor(rows, rows, qk_stat[:, 3, heads].unsqueeze(2).to_broadcast(
                        [P, 10, HEAD_DIM]), ALU.mult))
                    dve.tensor_tensor(rows[:, 0:8, :], rows[:, 0:8, :],
                                      qk_gain[:, 0:1, :].to_broadcast([P, 8, HEAD_DIM]), ALU.mult)
                    link(dve.tensor_tensor(rows[:, 8:10, :], rows[:, 8:10, :],
                                           qk_gain[:, 1:2, :].to_broadcast([P, 2, HEAD_DIM]), ALU.mult))
                    if t < LAT_TILES:
                        rotate(flat, t)
                    if t >= 2:
                        wait_bank(dve, ("qkT", t - 2, 2))
                    for kind in range(2):
                        k0 = kind * B_OFF + 512
                        for kv in range(2):
                            src = proj[:, t, k0 + kv * HEAD_DIM:k0 + (kv + 1) * HEAD_DIM]
                            ins = dve.tensor_copy(kdup[:, t % 2, 2 * kind + kv, :].rearrange("p (a b) -> p a b", a=2),
                                                  src.unsqueeze(1).to_broadcast([P, 2, HEAD_DIM]))
                    ins.then_inc(qk_ready, 1)

            def attention():
                for i in range(len(attn_steps) + 3):
                    if i < len(attn_steps):
                        t, hd = attn_steps[i]
                        nk = TILES if t < LAT_TILES else LAT_TILES
                        st = att_stat[:, i % 4, :]
                        b = wait_bank(dve, ("s", i))
                        if hd < HEADS_A and t < LAT_TILES:
                            cols = bank[b][:, (1 - t) * P:(2 - t) * P]
                            link(dve.tensor_tensor(cols, cols, cst[:, C_BAND + t * P:C_BAND + (t + 1) * P], ALU.add))
                        link(dve.tensor_reduce(st[:, 0:1], bank[b][:, 0:nk * P], AX_X, ALU.max))
                        if hd < HEADS_A:
                            link(dve.tensor_scalar(st[:, 0:1], st[:, 0:1], ATTN_SCALE, sinks[:, hd:hd + 1], ALU.mult,
                                                   ALU.max))
                            dve.tensor_scalar(st[:, 1:2], st[:, 0:1], -1.0, None, ALU.mult).then_inc(att_max, 1)
                        else:
                            dve.tensor_scalar(st[:, 1:2], st[:, 0:1], -ATTN_SCALE, None, ALU.mult).then_inc(att_max, 1)
                    if i >= 3:
                        m = i - 3
                        t, hd = attn_steps[m]
                        st = att_stat[:, m % 4, :]
                        wait_drained(dve, ("s", m))
                        if hd < HEADS_A:
                            dve.wait_ge(sink_exp, count.next("sink"))
                            link(dve.tensor_tensor(st[:, 2:3], st[:, 2:3], st[:, 3:4], ALU.add))
                        link(dve.reciprocal(st[:, 2:3], st[:, 2:3]))
                        b = wait_bank(dve, ("o", m))
                        dve.tensor_scalar(h[:, t, hd * HEAD_DIM:(hd + 1) * HEAD_DIM], bank[b][:, 0:HEAD_DIM],
                                          st[:, 2:3], None, ALU.mult).then_inc(bank_drained[b], 1)

            def mix_out(layer, tiles):
                if layer:
                    dve.wait_ge(gate_loads, 16 * 4)
                for t in range(tiles):
                    for n in range(D // WBLK):
                        b = wait_bank(dve, (f"out{layer}", n, t))
                        cols = slice(n * WBLK, (n + 1) * WBLK)
                        link(dve.tensor_tensor(update[:, n, :], bank[b][:, :],
                                               gate_rows[:, t // LAT_TILES, cols], ALU.mult))
                        dve.sem_inc(bank_drained[b], 1)
                        ins = dve.tensor_tensor(xs[:, t, cols], xs[:, t, cols], update[:, n, :], ALU.add)
                    ins.then_inc(residual_ready, 1)
                    modulate_tile(ffn_in, t, [key_loads[layer]] * 2)

            def gla():
                dve.wait_ge(pool_loads, gla_loads)
                ins = dve.memset(att_masked, 0.0)
                link(ins)
                gates = [(d, t) for d in range(2) for t in range(TILES)]
                for n in range(len(gates) + GATE_BUFS):
                    if n >= GATE_BUFS:
                        m = n - GATE_BUFS
                        decay = log_decay(*gates[m])
                        dve.wait_ge(gate_ln, count.next("ln"))
                        dve.scalar_tensor_tensor(decay, gate_tmp[:, m % GATE_BUFS, :], -1.0 / GATE_NORM, decay,
                                                 ALU.mult, ALU.add).then_inc(decay_ready, 1)
                        dve.wait_ge(decay_ready, m + 1)
                    if n < len(gates):
                        d, t = gates[n]
                        z = gate_tmp[:, n % GATE_BUFS, :]
                        b = wait_bank(dve, ("z", d, t))
                        dve.tensor_tensor(z, bank[b][:, :], gate_bias[:, d, :], ALU.add).then_inc(bank_drained[b], 1)
                        wait_drained(dve, ("z", d, t))
                        dve.tensor_scalar(log_decay(d, t), z, 0.0, 1.0 / GATE_NORM, ALU.min, ALU.mult)
                        link(dve.scalar_tensor_tensor(z, z, -1.0, z, ALU.mult, ALU.max))
                        dve.sem_inc(gate_z, 1)
                for d in range(2):
                    for t in range(TILES):
                        if t < LAT_TILES:
                            q, k = gla_lat[:, t, 0:KD], gla_lat[:, t, KD:2 * KD]
                            dve.wait_ge(exp_ready, count.next("exp"))
                            dve.scalar_tensor_tensor(q_dec[:, t, :], q, DK**-0.5, q_dec[:, t, :], ALU.mult, ALU.mult)
                            wait_drained(dve, ("b", d, t))
                            dve.tensor_tensor(k_inv[:, t, :], k_inv[:, t, :], k, ALU.mult)
                        else:
                            k = gla_ctx[:, t - LAT_TILES, 0:KD]
                        wait_drained(dve, ("rest", d, t))
                        dve.tensor_tensor(k_end[:, t, :], k_end[:, t, :], k, ALU.mult).then_inc(keyed_ready, 1)
                    wait_drained(dve, ("end", d))
                    done = {}
                    for n, (hh, kind, chunk, slot) in enumerate(gla_updates(d)):
                        b = wait_bank(dve, ("kv", d, n))
                        new = states[:, hh, slot, :]
                        if hh not in done:
                            ins = dve.tensor_copy(new, bank[b][:, 0:DV])
                        else:
                            tile = chunk // 2 + (LAT_TILES if kind == "ctx" else 0)
                            ins = dve.scalar_tensor_tensor(new, states[:, hh, done[hh], :],
                                                           decay_end[:, hh, tile, chunk % 2:chunk % 2 + 1],
                                                           bank[b][:, 0:DV], ALU.mult, ALU.add)
                        done[hh] = slot
                        ins.then_inc(state_ready, 1)
                        dve.wait_ge(state_ready, count.next("state"))
                        dve.sem_inc(bank_drained[b], 1)
                    mask = cst[:, (C_UPPER, C_LOWER)[d]:(C_UPPER, C_LOWER)[d] + P].bitcast(U32)
                    for i in range(len(gla_jobs) + 1):
                        if i < len(gla_jobs):
                            b = wait_bank(dve, ("att", d, i))
                            if i >= 2:
                                wait_bank(dve, ("go", d, i - 2))
                            dve.copy_predicated(att_masked[:, 2 * d + i % 2, :], mask,
                                                bank[b][:, 0:P]).then_inc(masked_ready, 1)
                            dve.wait_ge(masked_ready, count.next("masked"))
                            dve.sem_inc(bank_drained[b], 1)
                        if i >= 1:
                            m = i - 1
                            t, hh = gla_jobs[m]
                            o = gla_o[:, t, hh * DV:(hh + 1) * DV]
                            b = wait_bank(dve, ("go", d, m))
                            if d == 0:
                                ins = dve.tensor_copy(o, bank[b][:, 0:DV])
                            else:
                                ins = dve.tensor_tensor(o, bank[b][:, 0:DV], o, ALU.add)
                            ins.then_inc(bank_drained[b], 1)
                    if d == 0:
                        for t in range(LAT_TILES):
                            dve.wait_ge(silu_exp, t + 1)
                            link(dve.tensor_scalar_add(silu_r[:, t, :], silu_r[:, t, :], 1.0))
                            dve.reciprocal(silu_r[:, t, :], silu_r[:, t, :]).then_inc(sigmoid_ready, 1)
                dve.wait_ge(silu_ready, LAT_TILES)
                for t in range(LAT_TILES):
                    inverse_root(GLA_HEADS, DV, t * GLA_HEADS)
                    for hh in range(GLA_HEADS):
                        o = gla_o[:, t, hh * DV:(hh + 1) * DV]
                        j = 24 + t * GLA_HEADS + hh
                        ins = dve.scalar_tensor_tensor(o, o, stat[:, j:j + 1], silu_r[:, t, hh * DV:(hh + 1) * DV],
                                                       ALU.mult, ALU.mult)
                    ins.then_inc(normed_ready, 1)

            def largest(values, at_u, src, rest):
                hold(dve)
                link(dve.max(values[:, 0:8], src))
                hold(dve)
                dve.max_index(at_u[:, 0:8], values[:, 0:8], src)
                link(dve.match_replace(rest, values[:, 0:8], src, LOWEST))
                hold(dve)
                link(dve.max(values[:, 8:16], rest))
                hold(dve)
                link(dve.max_index(at_u[:, 8:16], values[:, 8:16], rest))

            def route_half(g, par, half):
                if half == 0:
                    dve.wait_ge(head_scores_ready, g + 1)
                largest(top[:, half, :], top_at_u[:, half, :],
                        head_scores[:, par, half * N_KEYS:(half + 1) * N_KEYS], rest_scores[:, half, :])

            def route_sums():
                dve.tensor_tensor(sums.rearrange("p (a b) -> p a b", a=TOPK),
                                  top[:, 0, :].unsqueeze(2).to_broadcast([P, TOPK, TOPK]),
                                  top[:, 1:2, :].to_broadcast([P, TOPK, TOPK]), ALU.add)
                link(dve.tensor_copy(top_at, top_at_u))

            def route_best(g, par, layer):
                largest(best[:, par, :], best_at_u, sums, rest_sums)
                dve.tensor_scalar(neg_best[:, par:par + 1], best[:, par, 0:1], -1.0, None, ALU.mult).then_inc(best_ready, 1)
                link(dve.tensor_scalar(top_at[:, 0, :], top_at[:, 0, :], float(N_KEYS), float(layer * EXPERTS),
                                       ALU.mult, ALU.add))

            def route_experts(g, par):
                pair_u = best_pair_u.rearrange("p (k s) -> p k s", s=2)
                dve.tensor_scalar(pair_u[:, :, 0], best_at_u, 4, None, ALU.logical_shift_right)
                link(dve.tensor_scalar(pair_u[:, :, 1], best_at_u, 15, None, ALU.bitwise_and))
                link(dve.tensor_copy(best_pair, best_pair_u))
                hot = one_hot.rearrange("p (k s j) -> p k s j", k=TOPK, s=2)
                link(dve.tensor_tensor(one_hot.rearrange("p (k j) -> p k j", j=TOPK),
                                       best_pair.unsqueeze(2).to_broadcast([P, 2 * TOPK, TOPK]),
                                       cst[:, C_IOTA:C_IOTA + TOPK].unsqueeze(1).to_broadcast([P, 2 * TOPK, TOPK]),
                                       ALU.is_equal))
                link(dve.tensor_tensor(hot, hot, top_at.unsqueeze(1).to_broadcast([P, TOPK, 2, TOPK]), ALU.mult))
                link(dve.tensor_reduce(best_pair[:, 0:TOPK], one_hot.rearrange("p (k j) -> p k j", k=TOPK), AX_X,
                                       ALU.add))
                dve.tensor_copy(idx_u[:, par, :], best_pair[:, 0:TOPK]).then_inc(idx_u_ready, 1)

            def route_all(g, par, layer):
                route_half(g, par, 0)
                route_half(g, par, 1)
                route_sums()
                route_best(g, par, layer)
                route_experts(g, par)

            def weigh(g, par):
                dve.wait_ge(gate_num_ready, g + 1)
                link(dve.reciprocal(gate_sum[:, par:par + 1], gate_sum[:, par:par + 1]))
                dve.wait_ge(gelu_ready, g + 1)
                dve.scalar_tensor_tensor(pick_weight[:, par, :], act_gelu[:, par, :], gate_sum[:, par:par + 1],
                                         gate_num[:, par, :], ALU.mult, ALU.mult).then_inc(weight_ready, 1)

            def add_y(tile, g, par):
                dve.wait_ge(v_free, g * TOPK + (TOPK + RING))
                for half in range(2):
                    cols = slice(half * WBLK, (half + 1) * WBLK)
                    b = bank[2 * par + half]
                    link(dve.tensor_tensor(b[:, :], b[:, :], gate_rows[:, tile // LAT_TILES, cols], ALU.mult))
                    rows = xs[:, tile, cols]
                    ins = dve.tensor_tensor(rows, rows, b[:, :], ALU.add)
                    if half == 0:
                        link(ins)
                ins.then_inc(y_free, 1)

            def body(head, t, base, layer, tiles, prev, done, nxt):
                g, par = head * tiles + (base + t), t % 2
                for k in range(TOPK):
                    dve.wait_ge(u_in[k % RING], g * 32 + 16 * (k // RING + 1))
                    dve.tensor_tensor_reduce(u_rows[:, k % RING, :], u_rows[:, k % RING, :], ffn_in[:, t, :], 1.0, 0.0,
                                             ALU.mult, ALU.add, act_raw[:, par, k:k + 1]).then_inc(u_free, 1)
                    if k == 1 and prev:
                        weigh(g + (-1), 1 - par)
                    if k == 3 and nxt:
                        route_half(g + 1, 1 - par, 0)
                    if k == 5 and nxt:
                        route_half(g + 1, 1 - par, 1)
                    if k == 6 and done:
                        add_y((t - 2) % tiles, g + (-2), par)
                    if k == 7 and nxt:
                        route_sums()
                    if k == 9 and nxt:
                        route_best(g + 1, 1 - par, layer)
                    if k == 10:
                        if prev or layer:
                            dve.wait_ge(v_free, g * TOPK + (RING - TOPK))
                        dve.tensor_copy(idx_v[:, par, :], idx_u[:, par, :]).then_inc(idx_v_ready, 1)
                    if k == 12 and nxt:
                        route_experts(g + 1, 1 - par)

            LINKS = 23

            def experts(layer, tiles):
                n, base = tiles * PEER_HEADS, layer * GATHER_LAYER_STEPS
                last = PEER_HEADS - 1
                if layer == 0:
                    dve.sem_inc(u_free, RING)
                    dve.sem_inc(y_free, 2)
                route_all(base, 0, layer)
                dve.wait_ge(gate_loads, (16 * 2, 16 * 5)[layer])
                for t in range(tiles):
                    body(0, t, base, layer, tiles, t > 0, t > 1, True)
                steps_before = steps.n
                steps.n = 0
                with dve.Fori(0, last - 1) as turn_no:
                    steps.base = turn_no * (tiles * LINKS) + steps_before
                    for t in range(tiles):
                        body(turn_no + 1, t, base, layer, tiles, True, True, True)
                assert steps.n == tiles * LINKS, steps.n
                steps.base, steps.n = 0, steps_before + (last - 1) * tiles * LINKS
                for t in range(tiles):
                    body(last, t, base, layer, tiles, True, True, t + 1 < tiles)
                weigh(base + n - 1, 1)
                add_y(tiles - 2, base + n - 2, 0)
                add_y(tiles - 1, base + n - 1, 1)

            def final():
                inverse_root(LAT_TILES, D)
                dve.wait_ge(pool_loads, final_loads)
                for t in range(LAT_TILES):
                    dve.scalar_tensor_tensor(ffn_in[:, t, :], xs[:, t, :], stat[:, 24 + t:25 + t],
                                             mod_rows[:, 0, 0, :], ALU.mult, ALU.mult).then_inc(h_ready, 1)

            def program():
                conditions()
                modulation(0)
                modulate(h, TILES, [first_loads] * 2)
                modulation(1)
                queries_and_keys()
                attention()
                mix_out(0, TILES)
                experts(0, TILES)
                if end_stage("dve", dve):
                    return
                modulate(h_gla, TILES, mod_loads)
                if end_stage("dve", dve):
                    return
                gla()
                mix_out(1, LAT_TILES)
                experts(1, LAT_TILES)
                end_stage("dve", dve)
                final()

            program()


_INS = ["x", "c", "ctx", "c_ctx", "ada_w", "ada_b", "norm_mix", "norm_ffn", "attn_w_in", "attn_sink",
        "attn_q_gain", "attn_k_gain", "attn_w_out", "gla_w_in", "gla_gate_w", "gla_gate_b", "gla_head_gain",
        "gla_w_out", "peer_wq", "peer_keys", "peer_u", "peer_v", "final_norm"]


def kernel(**inputs):
    import concourse.bacc as bacc
    from concourse.bass_utils import run_bass_kernel_spmd

    nc = bacc.Bacc("TRN2", target_bir_lowering=False, num_devices=1)
    arrays, args = {}, []
    for name in _INS:
        arrays[f"in_{name}"] = np.ascontiguousarray(inputs[name])
    arrays["in_consts"] = shape_constants()
    for name, a in arrays.items():
        args.append(nc.dram_tensor(name, a.shape, mybir.dt.from_np(a.dtype), kind="ExternalInput").ap())
    args.append(nc.dram_tensor("out", (1, SEQ, D), F32, kind="ExternalOutput").ap())
    build(nc, *args)
    r = run_bass_kernel_spmd(nc, [arrays], core_ids=[0])
    return r.results[0]["out"]
```
